# Optimizing a Trainium2 kernel written in Bass

```python
import jax, jax.numpy as jnp
from jax import lax
import numpy as np
import math
import jax
import jax.numpy as jnp

D_MODEL = 1024
BATCH = 1
SEQ = 256
DEPTH = 2

HEAD_DIM = 64
N_HEADS_TOTAL = D_MODEL // HEAD_DIM
N_HEADS_A = N_HEADS_TOTAL // 4
N_HEADS_B = N_HEADS_TOTAL // 4
N_HEADS_C = N_HEADS_TOTAL // 2
N_KV_C = N_HEADS_C // 4
N_IDX_HEADS = 4
IDX_DIM = HEAD_DIM
TOPK_MAX = 256
WINDOW = 128
BLOCK = 128
ROPE_THETA = 10000.0
NORM_EPS = 1e-6
MIX_WIDTH = N_HEADS_TOTAL * HEAD_DIM
D_FF = -(-8 * D_MODEL // (3 * 256)) * 256
_COLS = (N_HEADS_A * HEAD_DIM, HEAD_DIM, HEAD_DIM,
         N_IDX_HEADS * IDX_DIM, IDX_DIM, N_IDX_HEADS,
         N_HEADS_B * HEAD_DIM, N_HEADS_B * HEAD_DIM, N_HEADS_B * HEAD_DIM,
         N_HEADS_C * HEAD_DIM, N_KV_C * HEAD_DIM, N_KV_C * HEAD_DIM)
IN_COLS = sum(_COLS)


def _rms(x, g):
    xf = x.astype(jnp.float32)
    y = xf * lax.rsqrt(jnp.mean(xf * xf, axis=-1, keepdims=True) + NORM_EPS)
    return (y * g.astype(jnp.float32)).astype(x.dtype)

def _rope_tables(L):
    inv = 1.0 / (ROPE_THETA ** (jnp.arange(0, HEAD_DIM, 2, dtype=jnp.float32) / HEAD_DIM))
    ang = jnp.arange(L, dtype=jnp.float32)[:, None] * inv[None, :]
    return jnp.cos(ang), jnp.sin(ang)

def _rope(x, cos, sin):
    c = cos[None, :, None, :].astype(x.dtype)
    s = sin[None, :, None, :].astype(x.dtype)
    x1, x2 = jnp.split(x, 2, axis=-1)
    return jnp.concatenate([x1 * c - x2 * s, x2 * c + x1 * s], axis=-1)

def _blocks(a):
    B, L = a.shape[:2]
    return jnp.moveaxis(a.reshape((B, L // BLOCK, BLOCK) + a.shape[2:]), 1, 0)

def _unblocks(a):
    nb, B = a.shape[:2]
    return jnp.moveaxis(a, 0, 1).reshape((B, nb * BLOCK) + a.shape[3:])

def _split_points():
    pts, acc = [], 0
    for w in _COLS[:-1]:
        acc += w
        pts.append(acc)
    return pts

def _dsa(q, k, v, qi, ki, wi):
    B, L, H, D = q.shape
    n_sel = min(TOPK_MAX, L // 4)
    scale = D ** -0.5
    idx_scale = (N_IDX_HEADS * IDX_DIM) ** -0.5
    kpos = jnp.arange(L)

    def one_block(inp):
        qn, qin, win, n = inp
        tq = n * BLOCK + jnp.arange(BLOCK)
        rel = jax.nn.relu(jnp.einsum('bqhd,bsd->bqhs', qin, ki).astype(jnp.float32))
        score = jnp.einsum('bqh,bqhs->bqs', win.astype(jnp.float32), rel) * idx_scale
        causal = kpos[None, :] <= tq[:, None]
        score = jnp.where(causal[None], score, -jnp.inf)
        _, sel = lax.top_k(score, n_sel)
        valid = sel <= tq[None, :, None]
        ks = jax.vmap(lambda a, i: a[i])(k, sel)
        vs = jax.vmap(lambda a, i: a[i])(v, sel)
        s = jnp.einsum('bqhd,bqkd->bhqk', qn, ks).astype(jnp.float32) * scale
        s = jnp.where(valid[:, None], s, -jnp.inf)
        p = jax.nn.softmax(s, axis=-1)
        return jnp.einsum('bhqk,bqkd->bqhd', p.astype(vs.dtype), vs)

    out = lax.map(one_block, (_blocks(q), _blocks(qi), _blocks(wi), jnp.arange(L // BLOCK)))
    return _unblocks(out)

def _stick_breaking(q, k, v):
    B, L, H, D = q.shape
    scale = D ** -0.5
    kpos = jnp.arange(L)

    def one_block(inp):
        qn, n = inp
        tq = n * BLOCK + jnp.arange(BLOCK)
        strict = (kpos[None, :] < tq[:, None])[None, None]
        z = jnp.einsum('bqhd,bshd->bhqs', qn, k).astype(jnp.float32) * scale
        log_keep = jnp.where(strict, jax.nn.log_sigmoid(-z), 0.0)
        log_between = lax.cumsum(log_keep, axis=3, reverse=True) - log_keep
        a = jnp.where(strict, jnp.exp(jax.nn.log_sigmoid(z) + log_between), 0.0)
        return jnp.einsum('bhqs,bshd->bqhd', a.astype(v.dtype), v)

    out = lax.map(one_block, (_blocks(q), jnp.arange(L // BLOCK)))
    return _unblocks(out)

def _swa_sinks(q, k, v, sinks):
    B, L, H, D = q.shape
    G = H // N_KV_C
    nb = L // BLOCK
    scale = D ** -0.5
    pad = ((0, 0), (1, 0), (0, 0), (0, 0), (0, 0))
    kb = k.reshape(B, nb, BLOCK, N_KV_C, D)
    vb = v.reshape(B, nb, BLOCK, N_KV_C, D)
    kk = jnp.concatenate([jnp.pad(kb, pad)[:, :-1], kb], axis=2)
    vv = jnp.concatenate([jnp.pad(vb, pad)[:, :-1], vb], axis=2)
    qg = q.reshape(B, nb, BLOCK, N_KV_C, G, D)
    kloc = jnp.arange(2 * BLOCK)
    diff = (jnp.arange(BLOCK)[:, None] + BLOCK) - kloc[None, :]
    band = (diff >= 0) & (diff < WINDOW)
    sink = sinks.astype(jnp.float32).reshape(N_KV_C, G)[None, :, :, None, None]

    def one_block(inp):
        qn, kn, vn, n = inp
        s = jnp.einsum('bqkgd,bskd->bkgqs', qn, kn).astype(jnp.float32) * scale
        mask = band & ((n > 0) | (kloc >= BLOCK))[None, :]
        s = jnp.where(mask, s, -jnp.inf)
        m = jnp.maximum(jnp.max(s, axis=-1, keepdims=True), sink)
        e = jnp.exp(s - m)
        p = e / (jnp.sum(e, axis=-1, keepdims=True) + jnp.exp(sink - m))
        return jnp.einsum('bkgqs,bskd->bqkgd', p.astype(vn.dtype), vn)

    out = lax.map(one_block, (jnp.moveaxis(qg, 1, 0), jnp.moveaxis(kk, 1, 0),
                              jnp.moveaxis(vv, 1, 0), jnp.arange(nb)))
    return _unblocks(out).reshape(B, L, H, D)

def _mixing(h, w_in, qn_a, kn_a, qn_c, kn_c, sinks, g_out, w_o, cos, sin):
    B, L, _ = h.shape
    p = h @ w_in
    qa, ka, va, qi, ki, wi, qb, kb, vb, qc, kc, vc = jnp.split(p, _split_points(), axis=-1)
    qa = _rope(_rms(qa.reshape(B, L, N_HEADS_A, HEAD_DIM), qn_a), cos, sin)
    ka = _rope(_rms(ka.reshape(B, L, 1, HEAD_DIM), kn_a), cos, sin)[:, :, 0]
    qi = _rope(qi.reshape(B, L, N_IDX_HEADS, IDX_DIM), cos, sin)
    ki = _rope(ki.reshape(B, L, 1, IDX_DIM), cos, sin)[:, :, 0]
    oa = _dsa(qa, ka, va, qi, ki, wi)
    ob = _stick_breaking(qb.reshape(B, L, N_HEADS_B, HEAD_DIM),
                         kb.reshape(B, L, N_HEADS_B, HEAD_DIM),
                         vb.reshape(B, L, N_HEADS_B, HEAD_DIM))
    qc = _rope(_rms(qc.reshape(B, L, N_HEADS_C, HEAD_DIM), qn_c), cos, sin)
    kc = _rope(_rms(kc.reshape(B, L, N_KV_C, HEAD_DIM), kn_c), cos, sin)
    oc = _swa_sinks(qc, kc, vc.reshape(B, L, N_KV_C, HEAD_DIM), sinks)
    o = jnp.concatenate([oa, ob, oc], axis=2)
    o = _rms(o, g_out).reshape(B, L, MIX_WIDTH)
    return o @ w_o

def _swiglu(h, w_gate, w_up, w_down):
    return (jax.nn.silu(h @ w_gate) * (h @ w_up)) @ w_down

def first_inputs(seed: int = 0) -> dict:
    key = jax.random.key(seed)
    ks = jax.random.split(key, 20)
    f = jnp.float32
    D = D_MODEL

    def nrm(k, shape, scale):
        return jax.random.normal(k, shape, f) * scale

    def gain(k, shape):
        return 1.0 + 0.02 * jax.random.normal(k, shape, f)

    return {
        "x": nrm(ks[0], (BATCH, SEQ, D), 1.0),
        "c": nrm(ks[1], (BATCH, D), 1.0),
        "ln1": gain(ks[2], (DEPTH, D)),
        "ln2": gain(ks[3], (DEPTH, D)),
        "w_mod": nrm(ks[4], (DEPTH, D, 6 * D), 0.5 * D ** -0.5),
        "b_mod": nrm(ks[5], (DEPTH, 6 * D), 0.02),
        "w_in": nrm(ks[6], (DEPTH, D, IN_COLS), D ** -0.5),
        "qn_a": gain(ks[7], (DEPTH, HEAD_DIM)),
        "kn_a": gain(ks[8], (DEPTH, HEAD_DIM)),
        "qn_c": gain(ks[9], (DEPTH, HEAD_DIM)),
        "kn_c": gain(ks[10], (DEPTH, HEAD_DIM)),
        "sinks": nrm(ks[11], (DEPTH, N_HEADS_C), 0.5),
        "g_out": gain(ks[12], (DEPTH, N_HEADS_TOTAL, HEAD_DIM)),
        "w_o": nrm(ks[13], (DEPTH, MIX_WIDTH, D), MIX_WIDTH ** -0.5),
        "w_gate": nrm(ks[14], (DEPTH, D, D_FF), D ** -0.5),
        "w_up": nrm(ks[15], (DEPTH, D, D_FF), D ** -0.5),
        "w_down": nrm(ks[16], (DEPTH, D_FF, D), D_FF ** -0.5),
    }

def first_block(x, c, ln1, ln2, w_mod, b_mod, w_in, qn_a, kn_a, qn_c, kn_c, sinks, g_out, w_o,
              w_gate, w_up, w_down):
    L = x.shape[1]
    cos, sin = _rope_tables(L)
    c_act = jax.nn.silu(c)
    for l in range(DEPTH):
        mod = c_act @ w_mod[l] + b_mod[l]
        sh1, sc1, g1, sh2, sc2, g2 = [m[:, None, :] for m in jnp.split(mod, 6, axis=-1)]
        h = _rms(x, ln1[l]) * (1 + sc1) + sh1
        x = x + g1 * _mixing(h, w_in[l], qn_a[l], kn_a[l], qn_c[l], kn_c[l], sinks[l],
                             g_out[l], w_o[l], cos, sin)
        h = _rms(x, ln2[l]) * (1 + sc2) + sh2
        x = x + g2 * _swiglu(h, w_gate[l], w_up[l], w_down[l])
    return x


CTX_LEN = 256
GRID_W = 64
EPS = 1e-6

A_HEADS = 4
A_QK = 128
A_V = 256
A_WIDTH = A_HEADS * A_V
A_CHUNK = 64
F_BIAS_LO = 3.0
F_BIAS_HI = 6.0

B_HEADS = 8
B_QK = 64
B_V = 128
B_WIDTH = B_HEADS * B_V
B_QBLOCK = 128
ROPE_AXIS_DIM = B_QK // 2

C_GROUPS = 4
C_GROUP_DIM = 256
C_WIDTH = C_GROUPS * C_GROUP_DIM

N_BRANCH = 3

COL_SIZES = (
    A_HEADS * A_QK, A_HEADS * A_QK, A_WIDTH, 4 * A_HEADS, A_WIDTH, A_WIDTH,
    B_HEADS * 2 * B_QK, B_HEADS * 2 * B_QK, B_WIDTH, B_WIDTH,
    C_WIDTH, C_WIDTH,
    N_BRANCH * D_MODEL,
)
D_IN = 2 * A_HEADS * A_QK + 3 * A_WIDTH + 4 * A_HEADS + 4 * B_HEADS * B_QK + 2 * B_WIDTH + 2 * C_WIDTH + N_BRANCH * D_MODEL


def rmsnorm(x, w):
    xf = x.astype(jnp.float32)
    y = xf * lax.rsqrt(jnp.mean(xf * xf, axis=-1, keepdims=True) + EPS)
    return (y * w.astype(jnp.float32)).astype(x.dtype)

def split_cols(p):
    parts, start = [], 0
    for size in COL_SIZES:
        parts.append(p[..., start:start + size])
        start += size
    return parts

def axial_rope_tables(n_tokens):
    rows = n_tokens // GRID_W
    row = jnp.repeat(jnp.arange(rows, dtype=jnp.float32), GRID_W)
    col = jnp.tile(jnp.arange(GRID_W, dtype=jnp.float32), rows)
    inv_freq = ROPE_THETA ** (-jnp.arange(0, ROPE_AXIS_DIM, 2, dtype=jnp.float32) / ROPE_AXIS_DIM)
    ang_r = row[:, None] * inv_freq
    ang_c = col[:, None] * inv_freq
    ex = lambda t: t[:, None, None, :]
    return (ex(jnp.cos(ang_r)), ex(jnp.sin(ang_r)), ex(jnp.cos(ang_c)), ex(jnp.sin(ang_c)))

def _rotate(x, cos, sin):
    x1, x2 = jnp.split(x, 2, axis=-1)
    return jnp.concatenate([x1 * cos - x2 * sin, x2 * cos + x1 * sin], axis=-1)

def apply_axial_rope(x, rope):
    cos_r, sin_r, cos_c, sin_c = rope
    xr, xc = jnp.split(x.astype(jnp.float32), 2, axis=-1)
    return jnp.concatenate([_rotate(xr, cos_r, sin_r), _rotate(xc, cos_c, sin_c)], axis=-1).astype(x.dtype)

def mlstm_prep(q, k, v, g, b_if):
    bsz, n, _ = q.shape
    heads = lambda t, d: t.astype(jnp.float32).reshape(bsz, n, A_HEADS, d).transpose(0, 2, 1, 3)
    qh = heads(q, A_QK)
    kh = heads(k, A_QK) * (A_QK ** -0.5)
    vh = heads(v, A_V)
    pre = (g.astype(jnp.float32).reshape(bsz, n, 4, A_HEADS)
           + b_if.astype(jnp.float32).reshape(4, A_HEADS)).transpose(2, 0, 3, 1)
    fwd = (pre[0], jax.nn.log_sigmoid(pre[1]))
    bwd = (pre[2], jax.nn.log_sigmoid(pre[3]))
    return qh, kh, vh, (fwd, bwd)

def mlstm_zero_state(bsz):
    return (jnp.zeros((bsz, A_HEADS, A_QK, A_V), jnp.float32),
            jnp.zeros((bsz, A_HEADS, A_QK), jnp.float32),
            jnp.zeros((bsz, A_HEADS), jnp.float32))

def mlstm_scan(q, k, v, ig, lf, state):
    bsz, nh, n, _ = q.shape
    nc = n // A_CHUNK

    def chunks(t):
        return jnp.moveaxis(t.reshape(bsz, nh, nc, A_CHUNK, *t.shape[3:]), 2, 0)

    tril = jnp.tril(jnp.ones((A_CHUNK, A_CHUNK), dtype=bool))

    def body(carry, inp):
        c_st, n_st, m_st = carry
        qc, kc, vc, ic, fc = inp
        b = jnp.cumsum(fc, axis=-1)
        dmat = jnp.where(tril, b[..., :, None] - b[..., None, :] + ic[..., None, :], -jnp.inf)
        inter = b + m_st[..., None]
        m_row = jnp.maximum(jnp.max(dmat, axis=-1), inter)
        a = jnp.exp(dmat - m_row[..., None]) * jnp.einsum('bhtd,bhsd->bhts', qc, kc)
        w_inter = jnp.exp(inter - m_row)
        num = jnp.einsum('bhts,bhsv->bhtv', a, vc) + w_inter[..., None] * jnp.einsum('bhtd,bhdv->bhtv', qc, c_st)
        den = jnp.sum(a, axis=-1) + w_inter * jnp.einsum('bhtd,bhd->bht', qc, n_st)
        h = num / jnp.maximum(jnp.abs(den), jnp.exp(-m_row))[..., None]
        b_last = b[..., -1]
        g = b_last[..., None] - b + ic
        m_new = jnp.maximum(b_last + m_st, jnp.max(g, axis=-1))
        wk = jnp.exp(g - m_new[..., None])
        decay = jnp.exp(b_last + m_st - m_new)
        c_new = decay[..., None, None] * c_st + jnp.einsum('bhsd,bhsv->bhdv', kc * wk[..., None], vc)
        n_new = decay[..., None] * n_st + jnp.einsum('bhs,bhsd->bhd', wk, kc)
        return (c_new, n_new, m_new), h

    state, h = lax.scan(body, state, (chunks(q), chunks(k), chunks(v), chunks(ig), chunks(lf)))
    return jnp.moveaxis(h, 0, 2).reshape(bsz, nh, n, v.shape[-1]), state

def mlstm_direction(q, k, v, ig, lf, state, reverse):
    if reverse:
        h, state = mlstm_scan(jnp.flip(q, 2), jnp.flip(k, 2), jnp.flip(v, 2), jnp.flip(ig, 2), jnp.flip(lf, 2), state)
        return jnp.flip(h, 2), state
    return mlstm_scan(q, k, v, ig, lf, state)

def mlstm_mixer(q, k, v, gates, q_c, k_c, v_c, gates_c):
    h_lat, h_ctx = [], []
    for d, reverse in enumerate((False, True)):
        ig_c, lf_c = gates_c[d]
        ig, lf = gates[d]
        hc_d, st = mlstm_direction(q_c, k_c, v_c, ig_c, lf_c, mlstm_zero_state(q_c.shape[0]), reverse)
        h_d, _ = mlstm_direction(q, k, v, ig, lf, st, reverse)
        h_lat.append(h_d)
        h_ctx.append(hc_d)
    return h_lat[0] + h_lat[1], h_ctx[0] + h_ctx[1]

def mlstm_out(h, o, z, a_norm_w):
    bsz, _, n, _ = h.shape
    hn = rmsnorm(h.transpose(0, 2, 1, 3), a_norm_w.reshape(A_HEADS, A_V)).reshape(bsz, n, A_WIDTH)
    return hn.astype(o.dtype) * jax.nn.sigmoid(o) * jax.nn.silu(z)

def diffattn_prep(q, k, v, q_norm_w, k_norm_w, rope):
    bsz, n, _ = q.shape
    qh = rmsnorm(q.reshape(bsz, n, B_HEADS, 2, B_QK), q_norm_w)
    kh = rmsnorm(k.reshape(bsz, n, B_HEADS, 2, B_QK), k_norm_w)
    if rope is not None:
        qh = apply_axial_rope(qh, rope)
        kh = apply_axial_rope(kh, rope)
    vh = v.reshape(bsz, n, B_HEADS, B_V).transpose(0, 2, 1, 3)
    return qh.transpose(0, 2, 3, 1, 4), kh.transpose(0, 2, 3, 1, 4), vh

def attend(q, k, v, lam):
    s = jnp.einsum('bhmqd,bhmkd->bhmqk', q, k, preferred_element_type=jnp.float32) * (B_QK ** -0.5)
    p = jax.nn.softmax(s, axis=-1)
    w = p[:, :, 0] - lam * p[:, :, 1]
    return jnp.einsum('bhqk,bhkv->bhqv', w.astype(v.dtype), v)

def attend_blocked(q, k, v, lam):
    bsz, nh, nm, n, d = q.shape
    nb = n // B_QBLOCK
    qb = jnp.moveaxis(q.reshape(bsz, nh, nm, nb, B_QBLOCK, d), 3, 0)
    o = lax.map(lambda blk: attend(blk, k, v, lam), qb)
    return jnp.moveaxis(o, 0, 2).reshape(bsz, nh, n, v.shape[-1])

def diffattn_out(o, subln_w, lam_init):
    bsz, _, n, _ = o.shape
    return (rmsnorm(o, subln_w) * (1.0 - lam_init)).transpose(0, 2, 1, 3).reshape(bsz, n, B_WIDTH)

def fourier_mix(u):
    bsz, n, _ = u.shape
    uf = u.astype(jnp.float32).reshape(bsz, n, C_GROUPS, C_GROUP_DIM)
    y = jnp.fft.fft2(uf, axes=(1, 3), norm="ortho").real
    return y.reshape(bsz, n, C_WIDTH).astype(u.dtype)

def merge(y_a, y_b, y_c, mg, w_a_out, w_b_out, w_c_out, w_out):
    g_a, g_b, g_c = jnp.split(jax.nn.sigmoid(mg), N_BRANCH, axis=-1)
    y = g_a * (y_a @ w_a_out) + g_b * (y_b @ w_b_out) + g_c * (y_c @ w_c_out)
    return y @ w_out

def hybrid_layer(x, ctx, sc, sc_ctx, rope, layer_idx, last, norm_w, w_ada, b_ada, w_in, b_if, a_norm_w,
                 q_norm_w, k_norm_w, lambda_q1, lambda_k1, lambda_q2, lambda_k2, subln_w,
                 w_a_out, w_b_out, w_c_out, w_out):
    shift, scale, gate = jnp.split((sc @ w_ada + b_ada)[:, None, :], 3, axis=-1)
    shift_c, scale_c, gate_c = jnp.split(sc_ctx @ w_ada + b_ada, 3)
    h = rmsnorm(x, norm_w) * (1.0 + scale) + shift
    hc = rmsnorm(ctx, norm_w) * (1.0 + scale_c) + shift_c
    aq, ak, av, ag, ao, az, bq, bk, bv, bz, cu, cz, mg = split_cols(h @ w_in)
    aq_c, ak_c, av_c, ag_c, ao_c, az_c, bq_c, bk_c, bv_c, bz_c, cu_c, cz_c, mg_c = split_cols(hc @ w_in)

    qa, ka, va, ga = mlstm_prep(aq, ak, av, ag, b_if)
    qa_c, ka_c, va_c, ga_c = mlstm_prep(aq_c, ak_c, av_c, ag_c, b_if)
    h_a, h_a_c = mlstm_mixer(qa, ka, va, ga, qa_c, ka_c, va_c, ga_c)
    y_a = mlstm_out(h_a, ao, az, a_norm_w)

    lam_init = 0.8 - 0.6 * math.exp(-0.3 * layer_idx)
    f32 = jnp.float32
    lam = (jnp.exp(jnp.sum(lambda_q1.astype(f32) * lambda_k1.astype(f32)))
           - jnp.exp(jnp.sum(lambda_q2.astype(f32) * lambda_k2.astype(f32))) + lam_init)
    qb, kb, vb = diffattn_prep(bq, bk, bv, q_norm_w, k_norm_w, rope)
    qb_c, kb_c, vb_c = diffattn_prep(bq_c, bk_c, bv_c, q_norm_w, k_norm_w, None)
    o_b = attend_blocked(qb, jnp.concatenate([kb_c, kb], axis=3), jnp.concatenate([vb_c, vb], axis=2), lam)
    y_b = diffattn_out(o_b, subln_w, lam_init) * jax.nn.silu(bz)

    y_c = fourier_mix(cu) * jax.nn.silu(cz)

    x = x + gate * merge(y_a, y_b, y_c, mg, w_a_out, w_b_out, w_c_out, w_out)
    if not last:
        y_a_c = mlstm_out(h_a_c, ao_c, az_c, a_norm_w)
        y_b_c = diffattn_out(attend(qb_c, kb_c, vb_c, lam), subln_w, lam_init) * jax.nn.silu(bz_c)
        y_c_c = fourier_mix(cu_c) * jax.nn.silu(cz_c)
        ctx = ctx + gate_c * merge(y_a_c, y_b_c, y_c_c, mg_c, w_a_out, w_b_out, w_c_out, w_out)
    return x, ctx

def second_inputs(seed: int = 0) -> dict:
    key = jax.random.key(seed)
    ks = jax.random.split(key, 24)
    f32 = jnp.float32
    nrm = lambda k, shape, s: jax.random.normal(k, shape, f32) * s
    f_base = jnp.linspace(F_BIAS_LO, F_BIAS_HI, A_HEADS, dtype=f32)
    zeros_h = jnp.zeros((A_HEADS,), f32)
    b_if = jnp.concatenate([zeros_h, f_base, zeros_h, f_base])[None, :] + nrm(ks[8], (DEPTH, 4 * A_HEADS), 0.1)
    return {
        "x": nrm(ks[0], (BATCH, SEQ, D_MODEL), 1.0),
        "c": nrm(ks[1], (BATCH, D_MODEL), 1.0),
        "ctx": nrm(ks[2], (BATCH, CTX_LEN, D_MODEL), 1.0),
        "c_ctx": nrm(ks[3], (D_MODEL,), 1.0),
        "norm_w": 1.0 + nrm(ks[4], (DEPTH, D_MODEL), 0.02),
        "w_ada": nrm(ks[5], (DEPTH, D_MODEL, 3 * D_MODEL), 0.5 * D_MODEL ** -0.5),
        "b_ada": nrm(ks[6], (DEPTH, 3 * D_MODEL), 0.02),
        "w_in": nrm(ks[7], (DEPTH, D_MODEL, D_IN), D_MODEL ** -0.5),
        "b_if": b_if,
        "a_norm_w": 1.0 + nrm(ks[9], (DEPTH, A_WIDTH), 0.02),
        "q_norm_w": 1.0 + nrm(ks[10], (DEPTH, B_QK), 0.02),
        "k_norm_w": 1.0 + nrm(ks[11], (DEPTH, B_QK), 0.02),
        "lambda_q1": nrm(ks[12], (DEPTH, B_QK), 0.1),
        "lambda_k1": nrm(ks[13], (DEPTH, B_QK), 0.1),
        "lambda_q2": nrm(ks[14], (DEPTH, B_QK), 0.1),
        "lambda_k2": nrm(ks[15], (DEPTH, B_QK), 0.1),
        "subln_w": 1.0 + nrm(ks[16], (DEPTH, B_V), 0.02),
        "w_a_out": nrm(ks[17], (DEPTH, A_WIDTH, D_MODEL), A_WIDTH ** -0.5),
        "w_b_out": nrm(ks[18], (DEPTH, B_WIDTH, D_MODEL), B_WIDTH ** -0.5),
        "w_c_out": nrm(ks[19], (DEPTH, C_WIDTH, D_MODEL), C_WIDTH ** -0.5),
        "w_out": nrm(ks[20], (DEPTH, D_MODEL, D_MODEL), D_MODEL ** -0.5),
    }

def second_block(x, c, ctx, c_ctx, norm_w, w_ada, b_ada, w_in, b_if, a_norm_w, q_norm_w, k_norm_w,
              lambda_q1, lambda_k1, lambda_q2, lambda_k2, subln_w, w_a_out, w_b_out, w_c_out, w_out):
    rope = axial_rope_tables(x.shape[1])
    sc = jax.nn.silu(c)
    sc_ctx = jax.nn.silu(c_ctx)
    for l in range(DEPTH):
        x, ctx = hybrid_layer(x, ctx, sc, sc_ctx, rope, l, l == DEPTH - 1,
                              norm_w[l], w_ada[l], b_ada[l], w_in[l], b_if[l], a_norm_w[l],
                              q_norm_w[l], k_norm_w[l], lambda_q1[l], lambda_k1[l], lambda_q2[l], lambda_k2[l],
                              subln_w[l], w_a_out[l], w_b_out[l], w_c_out[l], w_out[l])
    return x


def setup_inputs(seed=0):
    out = dict(first_inputs(seed))
    for name, value in second_inputs(seed + 1).items():
        if name != "x":
            out[name + "_2"] = value
    return out


def reference(
    x, c, ln1, ln2, w_mod, b_mod, w_in, qn_a, kn_a, qn_c, kn_c, sinks, g_out, w_o, w_gate, w_up,
    w_down, c_2, ctx_2, c_ctx_2, norm_w_2, w_ada_2, b_ada_2, w_in_2, b_if_2, a_norm_w_2,
    q_norm_w_2, k_norm_w_2, lambda_q1_2, lambda_k1_2, lambda_q2_2, lambda_k2_2, subln_w_2,
    w_a_out_2, w_b_out_2, w_c_out_2, w_out_2,
):
    x = first_block(
        x, c, ln1, ln2, w_mod, b_mod, w_in, qn_a, kn_a, qn_c, kn_c, sinks, g_out, w_o, w_gate,
        w_up, w_down,
    )
    return second_block(
        x, c_2, ctx_2, c_ctx_2, norm_w_2, w_ada_2, b_ada_2, w_in_2, b_if_2, a_norm_w_2,
        q_norm_w_2, k_norm_w_2, lambda_q1_2, lambda_k1_2, lambda_q2_2, lambda_k2_2, subln_w_2,
        w_a_out_2, w_b_out_2, w_c_out_2, w_out_2,
    )


_drawn_inputs = setup_inputs


def setup_inputs(seed=0):
    import zlib

    import numpy as np

    out = dict(_drawn_inputs(seed))
    spreads = {}
    factors = {'ln1': 3.11,
     'ln2': 6.24,
     'qn_a': 8.0,
     'kn_a': 8.0,
     'qn_c': 8.0,
     'kn_c': 8.0,
     'sinks': 8.0,
     'g_out': 5.735,
     'norm_w_2': 8.0,
     'b_ada_2': 3.649,
     'a_norm_w_2': 8.0,
     'q_norm_w_2': 8.0,
     'k_norm_w_2': 8.0,
     'lambda_q1_2': 8.0,
     'lambda_k1_2': 8.0,
     'lambda_q2_2': 6.339,
     'lambda_k2_2': 8.0,
     'subln_w_2': 8.0}
    for name, (base, spread) in spreads.items():
        noise = np.random.default_rng([zlib.crc32(name.encode()), seed]).standard_normal(out[name].shape)
        drawn = base * np.exp(spread * noise) if base else spread * noise
        out[name] = jnp.asarray(drawn.astype(out[name].dtype))
    for name, factor in factors.items():
        out[name] = (out[name] * factor).astype(out[name].dtype)
    return out
```

```python
import numpy as np

import concourse.bass as bass
from concourse import mybir
from contextlib import ExitStack

P = 128
T = 256
D = 1024
KC = D // P
DEPTH = 2
D_FF = 2816
FC = D_FF // P
BIG = 1.0e30
GONE = -3.0e38
TOPK = T // 4
PLACE = (0, 2, 1, 3)
EPS = 1e-6

UNIT = KC * P
V_UNITS, QK_UNITS, WO_UNITS, FF_UNITS, DOWN_UNITS = 4, 16, KC, 2 * FC, 3 * KC
FIRST_UNITS = V_UNITS + QK_UNITS + WO_UNITS + FF_UNITS + DOWN_UNITS
SECOND = [("aqk", 8), ("av", 8), ("ag", 1), ("ao", 8), ("az", 8), ("amerge", 16),
          ("bq", 8), ("bk", 8), ("bv", 8), ("bz", 8), ("bmerge", 16),
          ("cu", 8), ("cz", 8), ("cmerge", 16), ("out", 8)]
SECOND_UNITS = sum(n for _, n in SECOND)
MOD1, MOD2 = 48, 24
BATCHES = [16, 16, 16, MOD1, 2 * MOD2]

def _places(sizes):
    at, out = 0, {}
    for name, n in sizes:
        out[name] = at
        at += n
    return out, at

CONST, COMMON_W = _places([("ident", P), ("ones", P), ("heads", P)])
FIRST_CONST, FIRST_W = _places([("rot", P), ("cos", T), ("sin", T), ("causal", 2 * T), ("strict", 2 * T),
                                ("band", 2 * T)])
SECOND_CONST, SECOND_W = _places([("axrot", P), ("axcos", T), ("axsin", T), ("lower", P), ("upper", P),
                                  ("dft", 2 * 512), ("dftc", 2 * T), ("dfts", 2 * T), ("pick", 4 * P)])
CONST.update({k: COMMON_W + v for k, v in [*FIRST_CONST.items(), *SECOND_CONST.items()]})
CONST_W = COMMON_W + max(FIRST_W, SECOND_W)
PAR1, PAR1_W = _places([("ln1", KC), ("ln2", KC), ("bmod", MOD1), ("gain", 9), ("gout", KC),
                        ("sinks", 8)])
PAR2, PAR2_W = _places([("norm", KC), ("bada", MOD2), ("bif", 1), ("anorm", KC), ("qn", 1),
                        ("kn", 1), ("subln", 1), ("lam", 4 * 64)])


def constants():
    f = np.float32
    first, second = np.zeros((P, COMMON_W + FIRST_W), f), np.zeros((P, COMMON_W + SECOND_W), f)
    r = np.arange(P)

    def put(name, a):
        c = second if name in SECOND_CONST else first
        c[:a.shape[0], CONST[name]:CONST[name] + a.shape[1]] = a

    put("ident", np.eye(P, dtype=f))
    put("ones", np.ones((P, P), f))
    put("heads", (r[:, None] // 64 == r[None, :] // 64).astype(f))

    def rotation(half):
        m = np.zeros((P, P), f)
        for o in range(P):
            if o % (2 * half) < half:
                m[o + half, o] = -1.0
            else:
                m[o - half, o] = 1.0
        return m

    put("rot", rotation(32))
    put("axrot", rotation(16))
    inv = (1.0 / (f(10000.0) ** (np.arange(0, 64, 2, dtype=f) / f(64)))).astype(f)
    ang = inv[r % 32][:, None] * np.arange(T, dtype=f)[None, :]
    put("cos", np.cos(ang))
    put("sin", np.sin(ang))
    inv = (f(10000.0) ** (-np.arange(0, 32, 2, dtype=f) / f(32))).astype(f)
    t = np.arange(T)
    pos = np.where((r % 64 < 32)[:, None], (t // 64)[None, :], (t % 64)[None, :]).astype(f)
    ang = inv[r % 16][:, None] * pos
    put("axcos", np.cos(ang))
    put("axsin", np.sin(ang))
    q = (np.arange(2)[None, :, None] * P + r[:, None, None])
    s = np.arange(T)[None, None, :]
    put("causal", np.where(s <= q, 0, -BIG).astype(f).reshape(P, 2 * T))
    put("strict", np.where(s < q, 0, -BIG).astype(f).reshape(P, 2 * T))
    put("band", np.where((s <= q) & (q - s < 128), 0, -BIG).astype(f).reshape(P, 2 * T))
    put("lower", np.where(r[:, None] <= r[None, :], 0, -BIG).astype(f))
    put("upper", np.where(r[:, None] >= r[None, :], 0, -BIG).astype(f))
    w = 2 * np.pi * ((np.arange(T)[:, None] * np.arange(T)[None, :]) % T) / T
    cos, sin = (np.cos(w) / 16).astype(f), (np.sin(w) / 16).astype(f)
    both = np.concatenate([cos, sin], 1)
    put("dft", both.reshape(2, P, 512).transpose(1, 0, 2).reshape(P, -1))
    put("dftc", cos.reshape(2, P, T).transpose(1, 0, 2).reshape(P, -1))
    put("dfts", (-sin).reshape(2, P, T).transpose(1, 0, 2).reshape(P, -1))
    pick = np.zeros((4, 4, P), f)
    for h in range(4):
        pick[h, h] = 1.0
    put("pick", pick.reshape(4, -1))
    return first, second[:, COMMON_W:]


def build(nc, stream, mods, consts, consts2, par1, par2, ccols, xT, ctxT, outT, debug=None):
    f32, f32r = mybir.dt.float32, mybir.dt.float32r
    ALU, ACT, AX = mybir.AluOpType, mybir.ActivationFunctionType, mybir.AxisListType
    PER = FIRST_UNITS
    ctx = ExitStack()

    def sb(name, shape, dt=f32):
        return ctx.enter_context(nc.sbuf_tensor(name, shape, dt))

    def sem(name):
        return ctx.enter_context(nc.semaphore(name))

    C = sb("C", [P, CONST_W])
    XX = sb("XX", [P, KC, 2 * T])
    AR = sb("AR", [P, 16384], f32r)
    WH = sb("WH", [P, 2, KC, P], f32r)
    WL = sb("WL", [P, 2, KC, P], f32r)
    RAW = sb("RAW", [P, 4, KC, P])
    P1 = sb("P1", [P, DEPTH, PAR1_W])
    P2 = sb("P2", [P, DEPTH, PAR2_W])
    CC = sb("CC", [P, 3, KC])
    CA = sb("CA", [P, 3, KC])
    CT = sb("CT", [P, 2, 3, KC])
    M1 = sb("M1", [P, DEPTH, MOD1])
    A1 = sb("A1", [P, DEPTH, 2, KC])
    M2 = sb("M2", [P, DEPTH, MOD2, 2])
    A2 = sb("A2", [P, DEPTH, KC, 2])
    COL = sb("COL", [P, 64])
    EPSC = sb("EPSC", [P, 2])
    WORK = sb("WORK", [P, 22528])

    def const(name, n=P):
        return C[:, CONST[name]:CONST[name] + n]

    ident, ones, heads = const("ident"), const("ones"), const("heads")
    X = XX[:, :, T:2 * T]
    H1 = AR[:, 0:2 * KC * T].rearrange("p (s k t) -> p s k t", s=2, k=KC)
    HID = AR[:, 2 * KC * T:2 * KC * T + 2 * FC * T].rearrange("p (s k t) -> p s k t", s=2, k=FC)
    OS = AR[:, 2 * KC * T:4 * KC * T].rearrange("p (s k t) -> p s k t", s=2, k=KC)

    def work(at, *shape):
        n = int(np.prod(shape))
        v = WORK[:, at:at + n]
        names = "abcd"[:len(shape)]
        if len(shape) > 1:
            v = v.rearrange(f"p ({' '.join(names)}) -> p {' '.join(names)}",
                            **{names[i]: shape[i] for i in range(len(shape))})
        return v

    F = work(0, QK_UNITS, T)
    V = work(4096, 2, 512)
    O = work(5120, KC, T)
    SM = work(7168, 2, 4, T)
    PR = work(9216, 2, 4, T)
    PT = work(11264, 2, 3, 4, P)
    WK = work(14336, 2, T)
    SEL = work(14848, 2, T)
    GATE = work(15360, 4, T)
    GRING = work(16384, 4, KC, P)
    RS = work(20480, 2, T)
    SQ = work(7168, KC, T)
    TMP = work(9216, 9, T)
    NX = work(9216, 4, T)
    VM = work(5120, 9, T)
    VO = work(11264, KC, T)
    SN = work(7680, 2, 2, T)
    RSO = work(9216, KC, T)
    STK = work(15360, 4, T)
    RO = work(11520, 12, T)

    H2 = AR[:, 0:8192].rearrange("p (s k t) -> p s k t", s=2, k=KC)
    Y2 = AR[:, 8192:16384].rearrange("p (s k t) -> p s k t", s=2, k=KC)
    YB = work(0, KC, 2 * T)
    KB = work(4096, KC, 2 * T)
    EB = work(4096, 2, 4, 2 * T)
    V2 = work(8192, 4, D)
    ACC = work(12288, KC, 2 * T)
    SQ2 = work(12288, KC, 2 * T)
    GT = work(12288, 2 * T)
    GI, GF, CF = work(12800, 2, 2 * T), work(13824, 2, 2 * T), work(14848, 2, 2 * T)
    CM, TG = work(16384, 2, 2 * T), work(17408, 2, 2 * T)
    NMS, NMD, EMS = (work(18432 + 1024 * i, 2, 2 * T) for i in range(3))
    DN, TM2 = work(21504, 2 * T), work(22016, 2 * T)
    NX2, RS2 = work(16384, 4, 2 * T), work(18432, 2, 2 * T)
    SG, SZ = work(20480, 2, 2 * T), work(21504, 2, 2 * T)
    SQB, RB = work(16384, 2, 2 * T), work(17408, 2, 2 * T)
    TC, TS = work(18432, 2, T), work(18944, 2, T)
    PB, WT = work(19456, 2, 2, 2 * T), work(21504, 2, 4, P)
    VB, VP = work(18432, 2, 2 * T), work(19456, 2, 2 * T)
    UC = sb("UC", [P, 8, 4])
    LM = sb("LM", [P, 2 * DEPTH + 2 * DEPTH])
    LT = work(16384, 2, DEPTH, 64)
    LR = sb("LR", [P, 2, DEPTH])
    BC = sb("BC", [P, 2, 8])

    PS = ctx.enter_context(nc.psum_tensor("PS", [P, 8, 512], f32))

    consts_in, consts2_in = sem("consts_in"), sem("consts2_in")
    raw_full = [sem(f"raw_full{i}") for i in range(4)]
    hi_done, lo_done = sem("hi_done"), sem("lo_done")
    unit_done = sem("unit_done")
    bank_read = [sem(f"bank_read{i}") for i in range(4)]
    mod_full = [sem(f"mod_full{i}") for i in range(4)]
    mod_used, mod_read = sem("mod_used"), sem("mod_read")
    dve_chain, act_chain = sem("dve_chain"), sem("act_chain")
    cexp, cact = sem("cexp"), sem("cact")
    sq_done, sum_done, rstd_done = sem("sq_done"), sem("sum_done"), sem("rstd_done")
    nx_done, nhi_done, norm_done = sem("nx_done"), sem("nhi_done"), sem("norm_done")
    rsq_done, ms_done, mr_done, rms_done = sem("rsq_done"), sem("ms_done"), sem("mr_done"), sem("rms_done")
    rx_done = sem("rx_done")
    sticks, wk_done = sem("sticks"), sem("wk_done")
    ffg = sem("ffg")
    rot_done, cosd, rot_read = sem("rot_done"), sem("cosd"), sem("rot_read")
    rope_done = sem("rope_done")
    scores, scores_read = sem("scores"), sem("scores_read")
    masked, exped, probs = sem("masked"), sem("exped"), sem("probs")
    turned, pt_ready, pv_done, o_ready = sem("turned"), sem("pt_ready"), sem("pv_done"), sem("o_ready")
    wis_done = sem("wis_done")
    bl, bq = sem("bl"), sem("bq")
    osq, oms, orr, ohf, ohi, olo = (sem(n) for n in ("osq", "oms", "orr", "ohf", "ohi", "olo"))
    ffsig, ffhi, ff_done = sem("ffsig"), sem("ffhi"), sem("ff_done")
    out_done = sem("out_done")
    lam_r, lam_e, lam_done = sem("lam_r"), sem("lam_e"), sem("lam_done")
    gprep, gdve, gexp, gturn, uc_done = (sem(n) for n in ("gprep", "gdve", "gexp", "gturn", "uc_done"))
    st_done, nm_full, nms, em_full, ems = (sem(n) for n in ("st_done", "nm_full", "nms", "em_full", "ems"))
    nmd, decayed, weighted, num_done, post_done = (sem(n) for n in ("nmd", "decayed", "weighted", "num_done", "post_done"))
    gsq, gms, grs, grx, gnorm, prx = (sem(n) for n in ("gsq", "gms", "grs", "grx", "gnorm", "prx"))
    sig_done, gated, yhi, y_done = (sem(n) for n in ("sig_done", "gated", "yhi", "y_done"))
    o_gated = sem("o_gated")
    mg_done, m_mul, acc_done, ahi, a_done = (sem(n) for n in ("mg_done", "m_mul", "acc_done", "ahi", "a_done"))
    psq, pms, prs, pscaled, prot, pcos, psin, p_done = (
        sem(n) for n in ("psq", "pms", "prs", "pscaled", "prot", "pcos", "psin", "p_done"))
    s2, mx2, ex2, w2, t2, wt2, pv2, ob2 = (sem(n) for n in ("s2", "mx2", "ex2", "w2", "t2", "wt2", "pv2", "ob2"))
    f1, f1_read, f2, f2_read = (sem(n) for n in ("f1", "f1_read", "f2", "f2_read"))

    block = ctx.enter_context(nc.Block())
    total = DEPTH * PER + DEPTH * SECOND_UNITS if debug is None else debug["units"]

    class Chain:

        def __init__(self, eng, s):
            self.eng, self.s, self.n = eng, s, 0

        def __call__(self, ins):
            ins.then_inc(self.s, 1)
            self.n += 1

        def wait(self):
            self.eng.wait_ge(self.s, self.n)

    def earlier(u):
        layer = (FIRST_UNITS - DOWN_UNITS + KC) // 4
        done = min(u // FIRST_UNITS, DEPTH)
        return done * layer + (u - done * FIRST_UNITS) // 4

    def looped(eng, base, count, step, body):
        with eng.Fori(0, count // step) as i:
            for j in range(step):
                body(i, j)

    def stages(l):
        at, out = DEPTH * FIRST_UNITS + l * SECOND_UNITS, {}
        for name, n in SECOND:
            out[name] = at
            at += n
        return out

    def cover(d, c, l):
        low = 2 * l
        if d == 0:
            return [(max(c, low), 4)]
        found = {0: [(0, 1), (2, 4)], 1: [(0, 4)], 2: [(2, 3)], 3: [(2, 4)]}[c]
        return [(max(a, low), b) for a, b in found if b > low]

    def beyond(d, c, l):
        out = []
        for a, b in cover(d, c, l):
            if a <= c < b:
                out += [(a, c), (c + 1, b)]
            else:
                out.append((a, b))
        return [(a, b) for a, b in out if a < b]

    def tiles(l):
        return [(h, n) for h in range(8) for n in range(2 * l, 4)]

    def tile_base(l):
        return 32 * l

    def parts(l):
        return range(l, 2)

    def second_pe(pe, feature_unit, token_unit):
        def layer(l):
            st, t0 = stages(l), l * T
            idx = 4 + l
            moving, all_moving, ymoving = H2[:, :, :, t0:], H2, Y2[:, :, :, t0:]
            n = 2 * T - t0
            for k in range(KC):
                pe.wait_ge(sq_done, idx * KC + k + 1)
                last = pe.matmul(PS[:, 6, :], ones, SQ2[:, k, :], start=(k == 0), stop=(k == KC - 1))
            last.then_inc(sum_done, 1)
            pe.wait_ge(norm_done, (idx + 1) * KC)
            b = st["aqk"]

            def qk(i, j):
                if j % 2:
                    feature_unit(b, i, j, all_moving, 2 * T)
                else:
                    feature_unit(b, i, j, moving, n)

            looped(pe, b, 8, 4, qk)
            looped(pe, st["av"], 8, 4, lambda i, j: token_unit(st["av"], i, j, H2, 4))
            feature_unit(st["ag"], 0, 0, all_moving, 2 * T)
            pe.wait_ge(gdve, l + 1)
            for d in range(2):
                for c in range(4):
                    at = (4 * d + c) * 4
                    last = pe.transpose(PS[:, 4, at:at + 4], GI[0:4, d, c * P:(c + 1) * P], ident[0:4, 0:4])
            last.then_inc(gturn, 1)
            pe.wait_ge(gexp, l + 1)
            pe.wait_ge(uc_done, l + 1)
            for j in range(4):
                pe.wait_ge(bank_read[(st["ao"] + j) % 4], earlier(st["ao"] + j))
            pick = const("pick", 4 * P)

            def numerator(e):
                h, d = e // 2, e % 2
                pe.wait_ge(weighted, 8 * l + e + 1)
                if 8 * l + e:
                    pe.wait_ge(post_done, 8 * l + e)
                order = [1, 0, 2, 3] if d else [0, 1, 2, 3]
                for v in range(3):
                    runs = [(c, a, b) for c in order for a, b in cover(d, c, l)]
                    for r, (c, a, b) in enumerate(runs):
                        lhs = ones if v == 2 else V2[:, c, (2 * h + v) * P:(2 * h + v + 1) * P]
                        last = pe.matmul(PS[:, 5 + v, a * P:b * P], lhs, EB[:, d, c, a * P:b * P],
                                         start=(r == 0), stop=(r == len(runs) - 1))
                last.then_inc(num_done, 1)

            for e in range(8):
                h, d = e // 2, e % 2
                if e:
                    pe.wait_ge(ems, 8 * l + e)
                pe.matmul(PS[:, 4, t0:], pick[0:4, h * P:(h + 1) * P], CM[0:4, d, t0:],
                          start=True, stop=True).then_inc(nm_full, 1)
                pe.wait_ge(nms, 8 * l + e + 1)
                pe.matmul(PS[:, 4, t0:], pick[0:4, h * P:(h + 1) * P], TG[0:4, d, t0:],
                          start=True, stop=True).then_inc(em_full, 1)
                if d == 0:
                    if e:
                        pe.wait_ge(weighted, 8 * l + e)
                    for c in range(4):
                        a = max(t0, 2 * (c // 2) * P)
                        last = pe.matmul(PS[:, c, a:], YB[:, 2 * h + 1, c * P:(c + 1) * P], YB[:, 2 * h, a:],
                                         start=True, stop=True)
                    last.then_inc(st_done, 1)
                if e:
                    numerator(e - 1)
            numerator(7)

            def norm_groups(first, groups, wide):
                for g in range(groups):
                    x = first + g
                    pe.wait_ge(gsq, 12 * l + x + 1)
                    if x >= 2:
                        pe.wait_ge(grs, 12 * l + x - 1)
                    for w in range(wide):
                        last = pe.matmul(PS[:, 4 + x % 2, t0:], ones, SQN(x, w)[:, t0:],
                                         start=(w == 0), stop=(w == wide - 1))
                    last.then_inc(gms, 1)

            norm_groups(0, 4, 2)
            looped(pe, st["ao"], 8, 4, lambda i, j: feature_unit(st["ao"], i, j, moving, n))
            looped(pe, st["az"], 8, 4, lambda i, j: feature_unit(st["az"], i, j, moving, n))

            def merge(name, branch):
                b = st[name]

                def pair(i, j):
                    if j % 2:
                        feature_unit(b, i, j, ymoving, n)
                    else:
                        feature_unit(b, i, j, moving, n)

                pe.wait_ge(y_done, (3 * l + branch + 1) * KC)
                looped(pe, b, 16, 4, pair)

            merge("amerge", 0)
            looped(pe, st["bq"], 8, 4, lambda i, j: feature_unit(st["bq"], i, j, moving, n))
            looped(pe, st["bk"], 8, 4, lambda i, j: feature_unit(st["bk"], i, j, all_moving, 2 * T))

            def rotate(x):
                src = (YB if x < 8 else KB)[:, x % 8, T:2 * T]
                pe.wait_ge(pscaled, 16 * l + x + 1)
                if x >= 2:
                    pe.wait_ge(psin, 16 * l + x - 1)
                pe.matmul(PS[:, 6 + x % 2, 0:T], const("axrot"), src, start=True, stop=True).then_inc(prot, 1)

            for x in range(16):
                a = t0 if x < 8 else 0
                pe.wait_ge(psq, 16 * l + x + 1)
                if x >= 2:
                    pe.wait_ge(prs, 16 * l + x - 1)
                pe.matmul(PS[:, 4 + x % 2, a:], heads, SQB[:, x % 2, a:], start=True, stop=True).then_inc(pms, 1)
                if x:
                    rotate(x - 1)
            rotate(15)
            looped(pe, st["bv"], 8, 4, lambda i, j: token_unit(st["bv"], i, j, H2, 4))
            for j in range(4):
                pe.wait_ge(bank_read[(st["bz"] + j) % 4], earlier(st["bz"] + j))
            pe.wait_ge(p_done, 16 * (l + 1))
            steps = tiles(l)

            def score(f):
                h, q = steps[f]
                keys = 2 * T if q >= 2 else T
                if f >= 2:
                    pe.wait_ge(ex2, tile_base(l) + f - 1)
                for m in range(2):
                    rows = slice(64 * m, 64 * m + 64)
                    last = pe.matmul(PS[:, 2 * (f % 2) + m, 0:keys], YB[rows, h, q * P:(q + 1) * P],
                                     KB[rows, h, 0:keys], start=True, stop=True)
                last.then_inc(s2, 1)

            def turn(f):
                h, q = steps[f]
                pe.wait_ge(w2, tile_base(l) + f + 1)
                if f >= 2:
                    pe.wait_ge(wt2, tile_base(l) + f - 1)
                for c in range(4 if q >= 2 else 2):
                    last = pe.transpose(PS[:, 4 + f % 2, c * P:(c + 1) * P], PB[:, f % 2, 0, c * P:(c + 1) * P],
                                        ident)
                last.then_inc(t2, 1)

            def value(f):
                h, q = steps[f]
                blocks = 4 if q >= 2 else 2
                pe.wait_ge(wt2, tile_base(l) + f + 1)
                if q == 2 * l and h >= 2:
                    pe.wait_ge(ob2, 8 * l + h - 1)
                for c in range(blocks):
                    last = pe.matmul(PS[:, 6 + h % 2, q * P:(q + 1) * P], V2[:, c, h * P:(h + 1) * P],
                                     WT[:, f % 2, c, :], start=(c == 0), stop=(c == blocks - 1))
                last.then_inc(pv2, 1)

            score(0)
            score(1)
            for f in range(len(steps)):
                turn(f)
                if f + 2 < len(steps):
                    score(f + 2)
                if f:
                    value(f - 1)
            value(len(steps) - 1)
            norm_groups(4, 8, 1)
            looped(pe, st["bz"], 8, 4, lambda i, j: feature_unit(st["bz"], i, j, moving, n))
            merge("bmerge", 1)
            looped(pe, st["cu"], 8, 4, lambda i, j: token_unit(st["cu"], i, j, H2, 4, 2 * l))
            for j in range(4):
                pe.wait_ge(bank_read[(st["cz"] + j) % 4], earlier(st["cz"] + j))
            dft = const("dft", 1024).rearrange("p (m n) -> p m n", m=2)
            dftc = const("dftc", 2 * T).rearrange("p (m n) -> p m n", m=2)
            dfts = const("dfts", 2 * T).rearrange("p (m n) -> p m n", m=2)
            for p in parts(l):
                done = 8 * (p if l == 0 else 2)
                for x in range(8):
                    if done + x >= 2:
                        pe.wait_ge(f1_read, done + x - 1)
                    for m in range(2):
                        last = pe.matmul(PS[:, 4 + x % 2, :], V2[:, 2 * p + m, x * P:(x + 1) * P], dft[:, m, :],
                                         start=(m == 0), stop=(m == 1))
                    last.then_inc(f1, 1)
                pe.wait_ge(f1_read, done + 8)
                for x in range(8):
                    if done + x >= 2:
                        pe.wait_ge(f2_read, done + x - 1)
                    cut = slice((x % 2) * P, (x % 2 + 1) * P)
                    for m in range(2):
                        src = KB[:, x // 2 * 2 + m, :]
                        pe.matmul(PS[:, 6 + x % 2, 0:T], dftc[:, m, cut], src[:, 0:T], start=(m == 0), stop=False)
                        last = pe.matmul(PS[:, 6 + x % 2, 0:T], dfts[:, m, cut], src[:, T:], start=False,
                                         stop=(m == 1))
                    last.then_inc(f2, 1)
            looped(pe, st["cz"], 8, 4, lambda i, j: feature_unit(st["cz"], i, j, moving, n))
            merge("cmerge", 2)
            pe.wait_ge(a_done, (l + 1) * KC)
            looped(pe, st["out"], 8, 4, lambda i, j: feature_unit(st["out"], i, j, moving, n))

        return layer

    def SQN(x, w):
        return EB[:, x % 2, w, :] if x < 4 else SQB[:, x % 2, :]

    def second_act(act, next_high, inverse_root, chain):
        def layer(l):
            st, t0 = stages(l), l * T
            idx, n = 4 + l, 2 * T - l * T
            for k in range(KC):
                if l:
                    u = stages(l - 1)["out"] + k
                    act.wait_ge(bank_read[u % 4], earlier(u) + 1)
                else:
                    act.wait_ge(bank_read[k % 4], earlier(DEPTH * FIRST_UNITS - DOWN_UNITS) + k // 4 + 1)
                act.activation(SQ2[:, k, :], XX[:, k, :], ACT.Square).then_inc(sq_done, 1)
            act.wait_ge(sum_done, idx + 1)
            inverse_root(RS2[:, 1, :], RS2[:, 0, :], PS[:, 6, :], 1.0 / D, None, rstd_done)
            act.wait_ge(mod_read, 5)
            for k in range(KC):
                act.wait_ge(nx_done, idx * KC + k + 1)
                for c in range(2):
                    cut = slice((1 - c) * T, (2 - c) * T)
                    last = act.activation(H2[:, 0, k, cut], NX2[:, k % 4, cut], ACT.Identity,
                                          bias=M2[:, l, k, c:c + 1])
                last.then_inc(nhi_done, 1)
            b = st["aqk"]

            def copied(b, dst, lo, scale=1.0):
                def body(i, j):
                    next_high(b, i, j)
                    bank = (b + j) % 4
                    act.activation(dst[:, bass.ds(4 * i + j, 1), lo:], PS[:, bank:bank + 1, 0:2 * T - lo],
                                   ACT.Copy).then_inc(bank_read[bank], 1)
                return body

            def qk(i, j):
                next_high(b, i, j)
                bank = (b + j) % 4
                lo, scale = (0, float(P) ** -0.5) if j % 2 else (t0, 1.0)
                act.activation(YB[:, bass.ds(4 * i + j, 1), lo:], PS[:, bank:bank + 1, 0:2 * T - lo],
                               ACT.Copy, scale=scale).then_inc(bank_read[bank], 1)

            def values(b, first):
                def body(i, j):
                    next_high(b, i, j)
                    bank = (b + j) % 4
                    act.activation(V2[:, first:, bass.ds((4 * i + j) * P, P)],
                                   PS[:, bank, first * P:].rearrange("p (b c) -> p b c", b=4 - first),
                                   ACT.Copy).then_inc(bank_read[bank], 1)
                return body

            looped(act, b, 8, 4, qk)
            looped(act, st["av"], 8, 4, values(st["av"], 0))
            u = st["ag"]
            next_high(u, 0, 0)
            act.activation(GT, PS[:, u % 4, :], ACT.Identity,
                           bias=P2[:, l, PAR2["bif"]:PAR2["bif"] + 1]).then_inc(bank_read[u % 4], 1)
            act.wait_ge(bank_read[u % 4], earlier(u) + 1)
            for d in range(2):
                act.activation(GI[0:4, d, :], GT[64 * d:64 * d + 4, :], ACT.Copy)
                chain(act.activation(GF[0:4, d, :], GT[64 * d + 32:64 * d + 36, :], ACT.Copy))
            chain.wait()
            chain(act.activation(CF[0:4, :, :], GF[0:4, :, :], ACT.Abs))
            chain.wait()
            chain(act.activation(CF[0:4, :, :], CF[0:4, :, :], ACT.Exp, scale=-1.0))
            chain.wait()
            act.activation(CF[0:4, :, :], CF[0:4, :, :], ACT.Ln, bias=EPSC[0:4, 1:2]).then_inc(gprep, 1)
            act.wait_ge(gdve, l + 1)
            act.activation(TG[0:4, :, :], TG[0:4, :, :], ACT.Exp, scale=-1.0).then_inc(gexp, 1)
            act.wait_ge(uc_done, l + 1)
            for e in range(8):
                d, h = e % 2, e // 2
                act.wait_ge(nm_full, 8 * l + e + 1)
                if e >= 2:
                    act.wait_ge(nmd, 8 * l + e - 1)
                    act.wait_ge(decayed, 8 * l + e - 1)
                act.activation(NMS[:, d, t0:], PS[:, 4, t0:], ACT.Copy).then_inc(nms, 1)
                act.wait_ge(em_full, 8 * l + e + 1)
                if e >= 2:
                    act.wait_ge(post_done, 8 * l + e - 1)
                act.activation(EMS[:, d, t0:], PS[:, 4, t0:], ACT.Copy).then_inc(ems, 1)
                act.wait_ge(nmd, 8 * l + e + 1)
                act.wait_ge(nms, 8 * l + e + 1)
                if e >= 2:
                    act.wait_ge(num_done, 8 * l + e - 1)
                for c in range(4):
                    bias = UC[:, 4 * d + c, h:h + 1]
                    if c >= 2 * l:
                        cut = slice(c * P, (c + 1) * P)
                        last = act.activation(EB[:, d, c, cut], NMD[:, d, cut], ACT.Exp, bias=bias)
                    for a, z in beyond(d, c, l):
                        cut = slice(a * P, z * P)
                        last = act.activation(EB[:, d, c, cut], NMS[:, d, cut], ACT.Exp, bias=bias)
                last.then_inc(decayed, 1)

            def norm_groups(first, groups, wide, scale):
                for g in range(groups + 1):
                    x = first + g
                    if g < groups:
                        if x == 0:
                            act.wait_ge(post_done, 8 * (l + 1))
                            act.wait_ge(num_done, 8 * (l + 1))
                        if g >= 2:
                            act.wait_ge(gms, 12 * l + x - 1)
                        for w in range(wide):
                            last = act.activation(SQN(x, w)[:, t0:], YB[:, wide * g + w, t0:], ACT.Square)
                        last.then_inc(gsq, 1)
                    if g:
                        x -= 1
                        act.wait_ge(gms, 12 * l + x + 1)
                        if g >= 3:
                            act.wait_ge(gnorm, 12 * l + x - 1)
                        inverse_root(NRM(x)[:, t0:], VRM(x)[:, t0:], PS[:, 4 + x % 2, t0:], scale,
                                     (grs, 12 * l + x + 1), grx)

            norm_groups(0, 4, 2, 1.0 / 256)

            def output_gate(i, j):
                b = st["ao"]
                next_high(b, i, j)
                bank = (b + j) % 4
                act.wait_ge(o_gated, 4 * i + (8 * l + max(j - 1, 0)))
                act.activation(SG[:, j % 2, t0:], PS[:, bank, 0:n], ACT.Sigmoid).then_inc(bank_read[bank], 1)

            looped(act, st["ao"], 8, 4, output_gate)

            def z_gate(name, branch):
                b = st[name]

                def body(i, j):
                    next_high(b, i, j)
                    bank = (b + j) % 4
                    y = 4 * i + ((3 * l + branch) * KC + j)
                    act.activation(SG[:, j % 2, t0:], PS[:, bank, 0:n], ACT.Sigmoid).then_inc(sig_done, 1)
                    act.wait_ge(gated, y + 1)
                    act.activation(Y2[:, 0, bass.ds(4 * i + j, 1), t0:], YB[:, bass.ds(4 * i + j, 1), t0:],
                                   ACT.Copy).then_inc(yhi, 1)

                looped(act, b, 8, 4, body)

            def merge(name, branch):
                b = st[name]

                def body(i, j):
                    next_high(b, i, j)
                    bank = (b + j) % 4
                    if j % 2 == 0:
                        act.wait_ge(bank_read[(b + j - 1) % 4], i + (earlier(b + j - 1) + 1))
                        act.activation(SG[:, j // 2, t0:], PS[:, bank, 0:n], ACT.Sigmoid).then_inc(bank_read[bank], 1)

                looped(act, b, 16, 4, body)

            act.wait_ge(o_gated, KC * (l + 1))
            z_gate("az", 0)
            merge("amerge", 0)
            looped(act, st["bq"], 8, 4, copied(st["bq"], YB, t0))
            looped(act, st["bk"], 8, 4, copied(st["bk"], KB, 0))
            for j in range(4):
                act.wait_ge(bank_read[(st["bv"] + j) % 4], earlier(st["bv"] + j))
            for x in range(17):
                if x < 16:
                    a = t0 if x < 8 else 0
                    src = (YB if x < 8 else KB)[:, x % 8, a:]
                    if x >= 2:
                        act.wait_ge(pms, 16 * l + x - 1)
                    act.activation(SQB[:, x % 2, a:], src, ACT.Square).then_inc(psq, 1)
                if x:
                    y = x - 1
                    a = t0 if y < 8 else 0
                    act.wait_ge(pms, 16 * l + y + 1)
                    if y >= 2:
                        act.wait_ge(pscaled, 16 * l + y - 1)
                    inverse_root(RB[:, y % 2, a:], VP[:, y % 2, a:], PS[:, 4 + y % 2, a:], 1.0 / 64,
                                 (prs, 16 * l + y + 1), prx)
            looped(act, st["bv"], 8, 4, values(st["bv"], 0))
            steps, tb = tiles(l), tile_base(l)

            def exps(f):
                h, q = steps[f]
                keys = 2 * T if q >= 2 else T
                act.wait_ge(mx2, tb + f + 1)
                if f >= 2:
                    act.wait_ge(t2, tb + f - 1)
                for m in range(2):
                    last = act.activation(PB[:, f % 2, m, 0:keys], PS[:, 2 * (f % 2) + m, 0:keys], ACT.Exp,
                                          bias=BC[:, f % 2, 2 + m:3 + m], scale=0.125,
                                          accum_out=BC[:, f % 2, 4 + m:5 + m])
                last.then_inc(ex2, 1)

            def head_out(h):
                act.wait_ge(pv2, tb + (h + 1) * (4 - 2 * l))
                act.activation(YB[:, h, t0:], PS[:, 6 + h % 2, t0:], ACT.Copy).then_inc(ob2, 1)

            exps(0)
            per = 4 - 2 * l
            for f in range(len(steps)):
                if f + 1 < len(steps):
                    exps(f + 1)
                act.wait_ge(t2, tb + f + 1)
                if f >= 2:
                    act.wait_ge(pv2, tb + f - 1)
                blocks = 4 if steps[f][1] >= 2 else 2
                act.activation(WT[:, f % 2, 0:blocks, :],
                               PS[:, 4 + f % 2, 0:blocks * P].rearrange("p (a b) -> p a b", a=blocks),
                               ACT.Copy).then_inc(wt2, 1)
                if f and f % per == 0:
                    head_out(f // per - 1)
            head_out(7)
            act.wait_ge(ob2, 8 * (l + 1))
            norm_groups(4, 8, 1, 1.0 / 128)
            z_gate("bz", 1)
            merge("bmerge", 1)
            looped(act, st["cu"], 8, 4, values(st["cu"], 2 * l))
            for p in parts(l):
                done = 8 * (p if l == 0 else 2)
                for x in range(8):
                    act.wait_ge(f1, done + x + 1)
                    act.activation(KB[:, x, :], PS[:, 4 + x % 2, :], ACT.Copy).then_inc(f1_read, 1)
            z_gate("cz", 2)
            merge("cmerge", 2)
            act.wait_ge(unit_done, st["out"])
            for k in range(KC):
                act.wait_ge(acc_done, (2 * l + 1) * KC + k + 1)
                act.activation(H2[:, 0, k, t0:], ACC[:, k, t0:], ACT.Copy).then_inc(ahi, 1)
            if l == DEPTH - 1:
                for i in range(2):
                    for j in range(4):
                        next_high(st["out"], i, j)
            else:
                looped(act, st["out"], 8, 4, lambda i, j: next_high(st["out"], i, j))

        act.wait_ge(lam_r, 1)
        act.activation(LM[:, 0:4], LR[:, :, :].rearrange("p a b -> p (a b)"), ACT.Exp).then_inc(lam_e, 1)
        for l in range(DEPTH):
            layer(l)

    def VRM(x):
        return NMD[:, x % 2, :] if x < 4 else VB[:, x % 2, :]

    def NRM(x):
        return NMS[:, x % 2, :] if x < 4 else RB[:, x % 2, :]

    def second_dve(dve, next_low, refine, chain):
        def layer(l):
            st, t0 = stages(l), l * T
            idx, n = 4 + l, 2 * T - l * T
            dve.wait_ge(rstd_done, idx + 1)
            refine(RS2[:, 1, :], RS2[:, 0, :])

            def low(k):
                dve.wait_ge(nhi_done, idx * KC + k + 1)
                for c in range(2):
                    cut = slice((1 - c) * T, (2 - c) * T)
                    ins = dve.scalar_tensor_tensor(H2[:, 1, k, cut], NX2[:, k % 4, cut], M2[:, l, k, c:c + 1],
                                                   H2[:, 0, k, cut].bitcast(f32), ALU.add, ALU.subtract)
                ins.then_inc(norm_done, 1)

            for k in range(KC):
                if k >= 4:
                    dve.wait_ge(norm_done, idx * KC + k - 3)
                for c in range(2):
                    cut = slice((1 - c) * T, (2 - c) * T)
                    ins = dve.scalar_tensor_tensor(NX2[:, k % 4, cut], XX[:, k, cut], A2[:, l, k, c:c + 1],
                                                   RS2[:, 1, cut], ALU.mult, ALU.mult)
                ins.then_inc(nx_done, 1)
                if k >= 2:
                    low(k - 2)
            low(KC - 2)
            low(KC - 1)

            def lows(name, count=8):
                b = st[name]
                looped(dve, b, count, 4, lambda i, j: next_low(b, i, j))

            lows("aqk")
            lows("av")
            next_low(st["ag"], 0, 0)
            chain(dve.memset(TG[0:4, :, :], 0.0))
            dve.wait_ge(gprep, l + 1)
            chain(dve.scalar_tensor_tensor(GF[0:4, :, :], GF[0:4, :, :], 0.0, CF[0:4, :, :], ALU.min, ALU.subtract))
            chain.wait()

            def scans(dst, src, other, op):
                chain(dve.tensor_tensor_scan(dst[0:4, 0, :], src[0:4, 0, :], other(slice(0, 2 * T), 0), 0.0, op, op))
                chain(dve.tensor_tensor_scan(dst[0:4, 1, 0:T][:, ::-1], src[0:4, 1, 0:T][:, ::-1],
                                             other(slice(0, T), 1)[:, ::-1], 0.0, op, op))
                chain.wait()
                chain(dve.tensor_tensor_scan(dst[0:4, 1, T:][:, ::-1], src[0:4, 1, T:][:, ::-1],
                                             other(slice(T, 2 * T), 1)[:, ::-1], dst[0:4, 1, 0:1], op, op))
                chain.wait()

            scans(CF, GF, lambda cut, d: TG[0:4, d, cut], ALU.add)
            chain(dve.tensor_tensor(GI[0:4, :, :], GI[0:4, :, :], CF[0:4, :, :], ALU.subtract))
            chain.wait()
            scans(CM, GI, lambda cut, d: GI[0:4, d, cut], ALU.max)
            chain(dve.tensor_tensor(TG[0:4, :, :], CF[0:4, :, :], CM[0:4, :, :], ALU.add))
            chain.wait()
            dve.tensor_scalar(CM[0:4, :, :], CM[0:4, :, :], -1.0, None, ALU.mult).then_inc(gdve, 1)
            dve.wait_ge(gturn, l + 1)
            dve.tensor_copy(UC[:, :, :], PS[:, 4, 0:32].rearrange("p (a b) -> p a b", a=8)).then_inc(uc_done, 1)

            def mask(e):
                d = e % 2
                dve.wait_ge(nms, 8 * l + e + 1)
                tri = const("upper" if d else "lower")[:, None, :].broadcast_to([P, 4 - 2 * l, P])
                if e >= 2:
                    dve.wait_ge(decayed, 8 * l + e - 1)
                dve.tensor_tensor(NMD[:, d, t0:].rearrange("p (a b) -> p a b", b=P),
                                  NMS[:, d, t0:].rearrange("p (a b) -> p a b", b=P), tri, ALU.add).then_inc(nmd, 1)

            def post(e):
                d, h = e % 2, e // 2
                dve.wait_ge(num_done, 8 * l + e + 1)
                dve.wait_ge(ems, 8 * l + e + 1)
                if e:
                    dve.wait_ge(post_done, 8 * l + e)
                chain(dve.tensor_tensor(DN[:, t0:], PS[:, 7, t0:], EMS[:, d, t0:], ALU.max))
                chain.wait()
                chain(dve.scalar_tensor_tensor(DN[:, t0:], PS[:, 7, t0:], -1.0, DN[:, t0:], ALU.mult, ALU.max))
                chain.wait()
                chain(dve.reciprocal(DN[:, t0:], DN[:, t0:]))
                chain.wait()
                for v in range(2):
                    y = YB[:, 2 * h + v, t0:]
                    if d == 0:
                        ins = dve.tensor_tensor(y, PS[:, 5 + v, t0:], DN[:, t0:], ALU.mult)
                    else:
                        if v:
                            chain.wait()
                        chain(dve.tensor_tensor(TM2[:, t0:], PS[:, 5 + v, t0:], DN[:, t0:], ALU.mult))
                        chain.wait()
                        ins = dve.tensor_tensor(y, y, TM2[:, t0:], ALU.add)
                        if v == 0:
                            chain(ins)
                ins.then_inc(post_done, 1)

            mask(0)
            for e in range(8):
                d = e % 2
                if e + 1 < 8:
                    mask(e + 1)
                dve.wait_ge(decayed, 8 * l + e + 1)
                dve.wait_ge(st_done, 4 * l + e // 2 + 1)
                for c in range(4):
                    for a, z in cover(d, c, l):
                        cut = slice(a * P, z * P)
                        ins = dve.tensor_tensor(EB[:, d, c, cut], EB[:, d, c, cut], PS[:, c, cut], ALU.mult)
                ins.then_inc(weighted, 1)
                if e:
                    post(e - 1)
            post(7)

            def norm_groups(first, groups, wide, gain):
                for g in range(groups):
                    x = first + g
                    dve.wait_ge(grx, 12 * l + x + 1)
                    refine(NRM(x)[:, t0:], VRM(x)[:, t0:])
                    for w in range(wide):
                        y = YB[:, wide * g + w, t0:]
                        ins = dve.scalar_tensor_tensor(y, y, gain(wide * g + w), NRM(x)[:, t0:], ALU.mult, ALU.mult)
                    ins.then_inc(gnorm, 1)

            at = PAR2["anorm"]
            norm_groups(0, 4, 2, lambda k: P2[:, l, at + k:at + k + 1])
            dve.wait_ge(gnorm, 12 * l + 4)

            def output_gate(i, j):
                b = st["ao"]
                next_low(b, i, j)
                bank = (b + j) % 4
                dve.wait_ge(bank_read[bank], i + (earlier(b + j) + 1))
                y = YB[:, bass.ds(4 * i + j, 1), t0:]
                dve.tensor_tensor(y, y, SG[:, j % 2:j % 2 + 1, t0:], ALU.mult).then_inc(o_gated, 1)

            looped(dve, st["ao"], 8, 4, output_gate)

            def z_gate(name, branch):
                b = st[name]

                def body(i, j):
                    next_low(b, i, j)
                    bank = (b + j) % 4
                    y = 4 * i + ((3 * l + branch) * KC + j)
                    dve.wait_ge(sig_done, y + 1)
                    dve.wait_ge(gated, y)
                    dve.tensor_tensor(SZ[:, 0, t0:], SG[:, j % 2, t0:], PS[:, bank, 0:n], ALU.mult).then_inc(bank_read[bank], 1)
                    dve.wait_ge(bank_read[bank], i + (earlier(b + j) + 1))
                    yb = YB[:, bass.ds(4 * i + j, 1), t0:]
                    dve.tensor_tensor(yb, yb, SZ[:, 0:1, t0:], ALU.mult).then_inc(gated, 1)
                    dve.wait_ge(yhi, y + 1)
                    dve.tensor_tensor(Y2[:, 1, bass.ds(4 * i + j, 1), t0:], yb,
                                      Y2[:, 0, bass.ds(4 * i + j, 1), t0:].bitcast(f32), ALU.subtract).then_inc(y_done, 1)

                looped(dve, b, 8, 4, body)

            def merge(name, branch):
                b = st[name]

                def body(i, j):
                    next_low(b, i, j)
                    bank = (b + j) % 4
                    if j % 2:
                        m = 2 * i + ((2 * l + branch - 1) * KC + j // 2)
                        before = (b + j - 1) % 4
                        dve.wait_ge(bank_read[before], i + (earlier(b + j - 1) + 1))
                        acc = ACC[:, bass.ds(2 * i + j // 2, 1), t0:]
                        if branch == 0:
                            dve.tensor_tensor(acc, SG[:, j // 2:j // 2 + 1, t0:], PS[:, bank:bank + 1, 0:n],
                                              ALU.mult).then_inc(bank_read[bank], 1)
                        else:
                            dve.wait_ge(acc_done, m)
                            dve.tensor_tensor(SZ[:, 0, t0:], SG[:, j // 2, t0:], PS[:, bank, 0:n],
                                              ALU.mult).then_inc(bank_read[bank], 1)
                            dve.wait_ge(bank_read[bank], i + (earlier(b + j) + 1))
                            dve.tensor_tensor(acc, acc, SZ[:, 0:1, t0:], ALU.add).then_inc(acc_done, 1)

                looped(dve, b, 16, 4, body)

            z_gate("az", 0)
            merge("amerge", 0)
            lows("bq")
            lows("bk")
            cos, sin = const("axcos", T), const("axsin", T)

            def rotated(x):
                src = (YB if x < 8 else KB)[:, x % 8, T:]
                dve.wait_ge(prot, 16 * l + x + 1)
                dve.tensor_tensor(TS[:, x % 2, :], PS[:, 6 + x % 2, 0:T], sin, ALU.mult).then_inc(psin, 1)
                dve.wait_ge(psin, 16 * l + x + 1)
                dve.tensor_tensor(src, TC[:, x % 2, :], TS[:, x % 2, :], ALU.add).then_inc(p_done, 1)

            for x in range(16):
                a = t0 if x < 8 else 0
                whole = (YB if x < 8 else KB)[:, x % 8, a:]
                at = PAR2["qn" if x < 8 else "kn"]
                dve.wait_ge(prx, 16 * l + x + 1)
                refine(RB[:, x % 2, a:], VP[:, x % 2, a:])
                dve.scalar_tensor_tensor(whole, whole, P2[:, l, at:at + 1], RB[:, x % 2, a:], ALU.mult,
                                         ALU.mult).then_inc(pscaled, 1)
                dve.wait_ge(pscaled, 16 * l + x + 1)
                if x >= 2:
                    dve.wait_ge(p_done, 16 * l + x - 1)
                chain(dve.tensor_tensor(TC[:, x % 2, :], (YB if x < 8 else KB)[:, x % 8, T:], cos, ALU.mult))
                if x:
                    rotated(x - 1)
            chain.wait()
            rotated(15)
            lows("bv")
            steps, tb = tiles(l), tile_base(l)

            def top(f):
                h, q = steps[f]
                keys = 2 * T if q >= 2 else T
                c = f % 2
                dve.wait_ge(s2, tb + f + 1)
                chain(dve.reduce_max(BC[:, c, 0:2], PS[:, 2 * c:2 * c + 2, 0:keys], AX.X))
                chain.wait()
                dve.tensor_scalar(BC[:, c, 2:4], BC[:, c, 0:2], -0.125, None, ALU.mult).then_inc(mx2, 1)

            top(0)
            for f in range(len(steps)):
                if f + 1 < len(steps):
                    top(f + 1)
                h, q = steps[f]
                keys = 2 * T if q >= 2 else T
                c = f % 2
                dve.wait_ge(ex2, tb + f + 1)
                chain(dve.reciprocal(BC[:, c, 4:6], BC[:, c, 4:6]))
                chain.wait()
                chain(dve.tensor_tensor(BC[:, c, 5:6], BC[:, c, 5:6], LM[:, 4 + l:5 + l], ALU.mult))
                chain(dve.tensor_scalar(PB[:, c, 0, 0:keys], PB[:, c, 0, 0:keys], BC[:, c, 4:5], None, ALU.mult))
                chain.wait()
                dve.scalar_tensor_tensor(PB[:, c, 0, 0:keys], PB[:, c, 1, 0:keys], BC[:, c, 5:6],
                                         PB[:, c, 0, 0:keys], ALU.mult, ALU.add).then_inc(w2, 1)
            norm_groups(4, 8, 1, lambda k: LM[:, 6 + l:7 + l])
            dve.wait_ge(gnorm, 12 * l + 12)
            z_gate("bz", 1)
            merge("bmerge", 1)
            lows("cu")
            for p in parts(l):
                done = 8 * (p if l == 0 else 2)
                for x in range(8):
                    dve.wait_ge(f2, done + x + 1)
                    dve.tensor_copy(YB[:, x, p * T:(p + 1) * T], PS[:, 6 + x % 2, 0:T]).then_inc(f2_read, 1)
            dve.wait_ge(f2_read, 16 + 8 * l)
            z_gate("cz", 2)
            merge("cmerge", 2)
            for k in range(KC):
                dve.wait_ge(ahi, l * KC + k + 1)
                dve.tensor_tensor(H2[:, 1, k, t0:], ACC[:, k, t0:], H2[:, 0, k, t0:].bitcast(f32),
                                  ALU.subtract).then_inc(a_done, 1)
            b = st["out"]

            def residual(i, j):
                next_low(b, i, j)
                bank = (b + j) % 4
                for p in parts(l):
                    x = XX[:, bass.ds(4 * i + j, 1), p * T:(p + 1) * T]
                    ins = dve.scalar_tensor_tensor(x, PS[:, bank:bank + 1, p * T - t0:(p + 1) * T - t0],
                                                   M2[:, l, bass.ds(4 * i + (16 + j), 1), 1 - p], x, ALU.mult, ALU.add)
                ins.then_inc(bank_read[bank], 1)

            if l == DEPTH - 1:
                for i in range(2):
                    for j in range(4):
                        residual(i, j)
            else:
                looped(dve, b, 8, 4, residual)

        at = PAR2["lam"]
        for i in range(2):
            chain(dve.tensor_tensor(LT[:, i, :, :], P2[:, :, at + 128 * i:at + 128 * i + 64],
                                    P2[:, :, at + 128 * i + 64:at + 128 * i + 128], ALU.mult))
        chain.wait()
        dve.tensor_reduce(LR[:, :, :], LT, AX.X, ALU.add).then_inc(lam_r, 1)
        dve.wait_ge(lam_e, 1)
        chain(dve.tensor_tensor(LM[:, 4:6], LM[:, 2:4], LM[:, 0:2], ALU.subtract))
        chain.wait()
        for l in range(DEPTH):
            start = 0.8 - 0.6 * float(np.exp(-0.3 * l))
            chain(dve.tensor_scalar(LM[:, 4 + l:5 + l], LM[:, 4 + l:5 + l], -start, None, ALU.add))
            at = PAR2["subln"]
            chain(dve.tensor_scalar(LM[:, 6 + l:7 + l], P2[:, l, at:at + 1], 1.0 - start, None, ALU.mult))
        chain.wait()
        dve.wait_ge(consts2_in, 16)
        for l in range(DEPTH):
            layer(l)

    def finish(sp):
        for k in range(KC):
            u = stages(DEPTH - 1)["out"] + k
            sp.wait_ge(bank_read[u % 4], earlier(u) + 1)
        sp.dma_start(outT, X).then_inc(out_done, 16)
        sp.wait_ge(out_done, 16)

    @block.sync
    def _(sp):
        for dst, src in ((C[:, 0:COMMON_W + FIRST_W], consts), (CC[:, :, :], ccols), (P1[:, :, :], par1), (P2[:, :, :], par2),
                         (X, xT), (XX[:, :, 0:T], ctxT)):
            sp.dma_start(dst, src).then_inc(consts_in, 16)
        for u in range(4):
            sp.dma_start(RAW[:, u, :, :], stream[u]).then_inc(raw_full[u], 16)
        with sp.Fori(1, total // 4) as i:
            for j in range(4):
                sp.wait_ge(lo_done, 4 * i + (j - 3))
                sp.dma_start(RAW[:, j, :, :], stream[4 * i + j]).then_inc(raw_full[j], 16)
        for u in range(total // 4 * 4, total):
            sp.wait_ge(lo_done, u - 3)
            sp.dma_start(RAW[:, u % 4, :, :], stream[u]).then_inc(raw_full[u % 4], 16)
        finish(sp)

    @block.gpsimd
    def _(pool):
        def load(first, end):
            with pool.Fori(0, (end - first) // 4) as i:
                for j in range(4):
                    pool.wait_ge(mod_used, 4 * i + (first + j - 3))
                    pool.dma_start(GRING[:, j, :, :], mods[4 * i + (first + j)]).then_inc(mod_full[j], 16)

        def rope(l):
            cos = const("cos", T)[:, None, :].broadcast_to([P, 2, T])
            if l == 0:
                pool.wait_ge(consts_in, 16 * 6)
            for g in range(6):
                pool.wait_ge(rms_done, 9 * l + max(1, min(9, 2 * g - 1)))
                pool.tensor_tensor(RO[:, 2 * g:2 * g + 2, :], F[:, 2 * g:2 * g + 2, :], cos,
                                   ALU.mult).then_inc(cosd, 1)

        for u in range(4):
            pool.dma_start(GRING[:, u, :, :], mods[u]).then_inc(mod_full[u], 16)
        load(4, 36)
        rope(0)
        load(36, 100)
        rope(1)
        load(100, sum(BATCHES))
        pool.wait_ge(o_ready, 4 * DEPTH)
        pool.dma_start(C[:, COMMON_W:COMMON_W + SECOND_W], consts2).then_inc(consts2_in, 16)

    @block.tensor
    def _(pe):
        def modulate_begin(batch):
            if batch:
                pe.wait_ge(mod_read, batch)
            else:
                pe.wait_ge(cact, 1)

        def modulate(batch, i, j, done=0):
            first, wide = sum(BATCHES[:batch]) + done, 2 if batch == 4 else 1
            pe.wait_ge(mod_full[j], 16 * i + 16 * (first // 4 + 1))
            for k in range(KC):
                rhs = CA[:, 1:3, k] if wide == 2 else CA[:, 0:1, k]
                last = pe.matmul(PS[:, 7, bass.ds((4 * i + (j + done)) * wide, wide)], GRING[:, j, k, :], rhs,
                                 start=(k == 0), stop=(k == KC - 1))
            last.then_inc(mod_used, 1)

        def unit_wait(base, i, j):
            u = base + j
            pe.wait_ge(lo_done, 4 * i + (u + 1))
            if u >= 4:
                pe.wait_ge(bank_read[u % 4], i + earlier(u))
            return u

        def feature_unit(base, i, j, moving, n):
            u = unit_wait(base, i, j)
            for k in range(KC):
                out = PS[:, u % 4, 0:n]
                pe.matmul(out, WH[:, u % 2, k, :], moving[:, 0, k, :], start=(k == 0), stop=False)
                pe.matmul(out, WH[:, u % 2, k, :], moving[:, 1, k, :], start=False, stop=False)
                last = pe.matmul(out, WL[:, u % 2, k, :], moving[:, 0, k, :], start=False, stop=(k == KC - 1))
            last.then_inc(unit_done, 1)

        def token_unit(base, i, j, still, blocks, first=0):
            u = unit_wait(base, i, j)
            for b in range(first, blocks):
                out = PS[:, u % 4, b * P:(b + 1) * P]
                cut = slice(b * P, (b + 1) * P)
                for k in range(KC):
                    pe.matmul(out, still[:, 0, k, cut], WH[:, u % 2, k, :], start=(k == 0), stop=False)
                    pe.matmul(out, still[:, 0, k, cut], WL[:, u % 2, k, :], start=False, stop=False)
                    last = pe.matmul(out, still[:, 1, k, cut], WH[:, u % 2, k, :], start=False,
                                     stop=(k == KC - 1))
            last.then_inc(unit_done, 1)

        def down_unit(base, i, j):
            u, b = base + j, j // 3
            pe.wait_ge(lo_done, 12 * i + (u + 1))
            if j % 3 == 0:
                pe.wait_ge(bank_read[b], i + earlier(base))
            for k in range(KC if j % 3 < 2 else FC - 2 * KC):
                kk = (j % 3) * KC + k
                pe.matmul(PS[:, b, 0:T], WH[:, u % 2, k, :], HID[:, 0, kk, :], start=(kk == 0), stop=False)
                pe.matmul(PS[:, b, 0:T], WH[:, u % 2, k, :], HID[:, 1, kk, :], start=False, stop=False)
                last = pe.matmul(PS[:, b, 0:T], WL[:, u % 2, k, :], HID[:, 0, kk, :], start=False,
                                 stop=(kk == FC - 1))
            last.then_inc(unit_done, 1)

        second = second_pe(pe, feature_unit, token_unit)

        def first_layer(l):
            base = l * PER
            def norm_sums(half):
                for k in range(KC):
                    pe.wait_ge(sq_done, (2 * l + half) * KC + k + 1)
                    last = pe.matmul(PS[:, 6, 0:T], ones, SQ[:, k, :], start=(k == 0), stop=(k == KC - 1))
                last.then_inc(sum_done, 1)

            norm_sums(0)
            pe.wait_ge(norm_done, (2 * l + 1) * KC)
            looped(pe, base, V_UNITS, 4, lambda i, j: token_unit(base, i, j, H1, 2))
            b = base + V_UNITS
            if l == 0:
                modulate_begin(1)

                def both(i, j):
                    feature_unit(b, i, j, H1, T)
                    modulate(1, i, j)
            else:
                def both(i, j):
                    feature_unit(b, i, j, H1, T)
            looped(pe, b, QK_UNITS, 4, both)
            for g in range(5):
                pe.wait_ge(rsq_done, 5 * l + g + 1)
                if g >= 2:
                    pe.wait_ge(mr_done, 5 * l + g - 1)
                n = T if g == 4 else 2 * T
                pe.matmul(PS[:, 4 + g % 2, 0:n], heads, TMP[:, 2 * g:2 * g + n // T, :],
                          start=True, stop=True).then_inc(ms_done, 1)
            for g in range(6):
                pe.wait_ge(rms_done, 9 * l + max(1, min(9, 2 * g - 1)))
                if g >= 2:
                    pe.wait_ge(rot_read, 6 * l + g - 1)
                else:
                    pe.wait_ge(mr_done, 5 * l + 5)
                pe.matmul(PS[:, 4 + g % 2, 0:2 * T], const("rot"), F[:, 2 * g:2 * g + 2, :],
                          start=True, stop=True).then_inc(rot_done, 1)
            pe.wait_ge(rope_done, 6 * (l + 1))

            def score(s):
                n = s % 2
                w = P * (n + 1)
                if s >= 2:
                    pe.wait_ge(scores_read, 10 * l + s - 1)
                for p, h in enumerate(PLACE):
                    if s < 2:
                        q, k = h // 2, 2
                    elif s < 4:
                        q, k = 3 + h // 2, 5
                    elif s < 8:
                        g = (s - 4) // 2
                        q, k = 6 + 2 * g + h // 2, 10 + g
                    else:
                        q, k = 12 + h // 2, 14 + h // 2
                    r = slice(64 * (h % 2), 64 * (h % 2) + 64)
                    out = PS[:, 2 * (s % 2):2 * (s % 2) + 2, :].rearrange("p a (b t) -> p (a b) t", b=2)[:, p, 0:w]
                    last = pe.matmul(out, F[r, q, n * P:(n + 1) * P], F[r, k, 0:w], start=True, stop=True)
                last.then_inc(scores, 1)

            def turn(s):
                a = s - 2
                n = a % 2
                if s < 8:
                    pe.wait_ge(probs, 6 * l + a + 1)
                else:
                    pe.wait_ge(sticks, 2 * l + s - 8 + 1)
                if a:
                    pe.wait_ge(pt_ready, 8 * l + a)
                for kb in range(n + 1):
                    for h in range(4):
                        last = pe.transpose(PS[:, 4 + kb, h * P:(h + 1) * P],
                                            PR[:, s % 2, h, kb * P:(kb + 1) * P], ident)
                last.then_inc(turned, 1)

            def weigh(g):
                pe.wait_ge(pt_ready, 8 * l + 2 * g + 2)
                if g:
                    pe.wait_ge(o_ready, 4 * l + g)
                for p, h in sorted(enumerate(PLACE), key=lambda x: x[1]):
                    at = (0, 320, 384, 64 + h * 64)[g]
                    rows = slice(64 * (h % 2), 64 * (h % 2) + 64)
                    out = PS[rows, 6, (h // 2) * T:(h // 2 + 1) * T]
                    pe.matmul(out, V[:, 0, at:at + 64], PT[:, g % 2, 0:2, p, :], start=True, stop=False)
                    last = pe.matmul(out[:, P:T], V[:, 1, at:at + 64], PT[:, g % 2, 2, p, :],
                                     start=False, stop=True)
                last.then_inc(pv_done, 1)

            score(0)
            score(1)
            if l == 0:
                modulate_begin(2)
                looped(pe, 0, BATCHES[2], 4, lambda i, j: modulate(2, i, j))
            score(2)
            score(3)
            for s in range(2, 10):
                turn(s)
                if s + 2 < 10:
                    score(s + 2)
                if s % 2:
                    weigh((s - 2) // 2)
            for g in range(4):
                pe.wait_ge(osq, 4 * l + g + 1)
                pe.matmul(PS[:, g, 0:2 * T], heads, SQ[:, 2 * g:2 * g + 2, :], start=True, stop=True).then_inc(oms, 1)
            pe.wait_ge(olo, (l + 1) * KC)
            b = base + V_UNITS + QK_UNITS
            looped(pe, b, WO_UNITS, 4, lambda i, j: feature_unit(b, i, j, OS, T))
            norm_sums(1)
            pe.wait_ge(norm_done, (2 * l + 2) * KC)
            b2 = b + WO_UNITS
            modulate_begin(3 + l)

            def hidden(i, j):
                feature_unit(b2, i, j, H1, T)
                modulate(3 + l, i, j)

            looped(pe, b2, FF_UNITS, 4, hidden)
            for j in range(4):
                modulate(3 + l, 0, j, done=FF_UNITS)
            pe.wait_ge(ff_done, (l + 1) * FC)
            b3 = b2 + FF_UNITS
            looped(pe, b3, DOWN_UNITS, 12, lambda i, j: down_unit(b3, i, j))

        modulate_begin(0)
        looped(pe, 0, BATCHES[0], 4, lambda i, j: modulate(0, i, j))
        for l in range(DEPTH):
            first_layer(l)
        for l in range(DEPTH):
            second(l)

    @block.scalar
    def _(act):
        chain = Chain(act, act_chain)

        def split_high(u, i, rounds):
            act.wait_ge(raw_full[u % 4], 16 * rounds * i + 16 * (u // 4 + 1))
            act.activation(WH[:, u % 2, :, :], RAW[:, u % 4, :, :], ACT.Copy).then_inc(hi_done, 1)

        def next_high(base, i, j, rounds=1):
            act.wait_ge(unit_done, 4 * rounds * i + (base + j + 1))
            if isinstance(i, int) and 4 * rounds * i + base + j + 2 >= total:
                return
            split_high(base + j + 2, i, rounds)

        def inverse_root(y, v, sums, scale, read, done):
            ins = act.activation(v, sums, ACT.Identity, bias=EPSC[:, 0:1], scale=scale)
            if read is None:
                chain(ins)
                chain.wait()
            else:
                ins.then_inc(read[0], 1)
                act.wait_ge(read[0], read[1])
            chain(act.activation(y, v, ACT.Ln))
            chain.wait()
            act.activation(y, y, ACT.Exp, scale=-0.5).then_inc(done, 1)

        def norm(l, half):
            for k in range(KC):
                if half:
                    act.wait_ge(bank_read[k % 4], earlier(l * PER + V_UNITS + QK_UNITS + k) + 1)
                elif l:
                    act.wait_ge(bank_read[k % 4], earlier(l * PER - DOWN_UNITS) + k // 4 + 1)
                act.activation(SQ[:, k, :], X[:, k, :], ACT.Square).then_inc(sq_done, 1)
            act.wait_ge(sum_done, 2 * l + half + 1)
            inverse_root(RS[:, 1, :], RS[:, 0, :], PS[:, 6, 0:T], 1.0 / D, None, rstd_done)
            for k in range(KC):
                act.wait_ge(nx_done, (2 * l + half) * KC + k + 1)
                at = 24 * half + k
                act.activation(H1[:, 0, k, :], NX[:, k % 4, :], ACT.Identity,
                               bias=M1[:, l, at:at + 1]).then_inc(nhi_done, 1)

        def first_layer(l):
            base = l * PER
            norm(l, 0)

            def values(i, j):
                next_high(base, i, j)
                act.activation(V[:, :, bass.ds((4 * i + j) * P, P)],
                               PS[:, j, 0:2 * P].rearrange("p (b c) -> p b c", b=2),
                               ACT.Copy).then_inc(bank_read[j], 1)

            looped(act, base, V_UNITS, 4, values)
            b = base + V_UNITS

            def features(i, j):
                next_high(b, i, j)
                act.activation(F[:, bass.ds(4 * i + j, 1), :], PS[:, j:j + 1, 0:T],
                               ACT.Copy).then_inc(bank_read[j], 1)

            looped(act, b, QK_UNITS, 4, features)
            for j in range(4):
                act.wait_ge(bank_read[j], earlier(b + QK_UNITS + j))
            for g in range(5):
                n = 1 if g == 4 else 2
                act.activation(TMP[:, 2 * g:2 * g + n, :], F[:, 3 + 2 * g:3 + 2 * g + n, :],
                               ACT.Square).then_inc(rsq_done, 1)
            for g in range(5):
                n = 1 if g == 4 else 2
                act.wait_ge(ms_done, 5 * l + g + 1)
                inverse_root(TMP[:, 2 * g:2 * g + n, :], VM[:, 2 * g:2 * g + n, :],
                             PS[:, 4 + g % 2, 0:n * T].rearrange("p (a b) -> p a b", a=n), 1.0 / 64,
                             (mr_done, 5 * l + g + 1), rx_done)

            def stats(s):
                return 8 + 16 * (s % 2)

            def exps(s):
                a, w = s - 2, P * (s % 2 + 1)
                if a >= 2:
                    act.wait_ge(turned, 8 * l + a - 1)
                if s < 8:
                    act.wait_ge(masked, 6 * l + a + 1)
                    c = stats(s)
                    if s >= 4:
                        act.activation(COL[:, 40 + 4 * (s % 2):44 + 4 * (s % 2)],
                                       COL[:, 48 + 4 * (s % 2):52 + 4 * (s % 2)], ACT.Exp)
                    for h in range(4):
                        last = act.activation(PR[:, s % 2, h, 0:w], SM[:, s % 2, h, 0:w], ACT.Exp,
                                              bias=COL[:, c + 4 + h:c + 5 + h], scale=0.125,
                                              accum_out=COL[:, c + 8 + h:c + 9 + h])
                    last.then_inc(exped, 1)
                else:
                    act.wait_ge(scores_read, 10 * l + s + 1)
                    dst = PR[:, s % 2, :, 0:w]
                    chain(act.activation(dst, SM[:, s % 2, :, 0:w], ACT.Abs))
                    chain.wait()
                    chain(act.activation(dst, dst, ACT.Exp, scale=-1.0))
                    chain.wait()
                    act.activation(dst, dst, ACT.Ln, bias=EPSC[:, 1:2]).then_inc(bl, 1)

            exps(2)
            for s in range(2, 10):
                a, g, n = s - 2, (s - 2) // 2, s % 2
                w = P * (n + 1)
                if s + 1 < 10:
                    exps(s + 1)
                if s >= 8:
                    act.wait_ge(bq, 2 * l + s - 8 + 1)
                    act.activation(PR[:, n, :, 0:w], SM[:, n, :, 0:w], ACT.Exp).then_inc(sticks, 1)
                act.wait_ge(turned, 8 * l + a + 1)
                if g >= 2:
                    act.wait_ge(pv_done, 4 * l + g - 1)
                if n == 0:
                    act.activation(PT[:, g % 2, 0, :, :], PS[:, 4, :].rearrange("p (a b) -> p a b", a=4),
                                   ACT.Copy).then_inc(pt_ready, 1)
                else:
                    act.activation(PT[:, g % 2, 1:3, :, :],
                                   PS[:, 4:6, :].rearrange("p k (a b) -> p k a b", a=4),
                                   ACT.Copy).then_inc(pt_ready, 1)
                    o = (0, 4, 6, 2)[g]
                    act.wait_ge(pv_done, 4 * l + g + 1)
                    act.activation(O[:, o:o + 2, :], PS[:, 6, :].rearrange("p (a b) -> p a b", a=2),
                                   ACT.Copy).then_inc(o_ready, 1)
            act.wait_ge(o_ready, 4 * l + 4)
            for g in range(4):
                act.activation(SQ[:, 2 * g:2 * g + 2, :], O[:, 2 * g:2 * g + 2, :], ACT.Square).then_inc(osq, 1)
            for g in range(4):
                act.wait_ge(oms, 4 * l + g + 1)
                inverse_root(RSO[:, 2 * g:2 * g + 2, :], VO[:, 2 * g:2 * g + 2, :],
                             PS[:, g, :].rearrange("p (a b) -> p a b", a=2), 1.0 / 64, None, orr)
            for k in range(KC):
                act.wait_ge(ohf, l * KC + k + 1)
                act.activation(OS[:, 0, k, :], GATE[:, k % 4, :], ACT.Copy).then_inc(ohi, 1)
            b = b + QK_UNITS
            looped(act, b, WO_UNITS, 4, lambda i, j: next_high(b, i, j))
            norm(l, 1)
            b2 = b + WO_UNITS

            def hidden(i, j):
                next_high(b2, i, j)
                if j % 2 == 0:
                    act.activation(GATE[:, 0, :], PS[:, j, 0:T], ACT.Sigmoid).then_inc(ffsig, 1)
                else:
                    act.wait_ge(bank_read[j], i + (earlier(b2 + j) + 1))
                    act.activation(HID[:, 0, bass.ds(2 * i + j // 2, 1), :], GATE[:, 2:3, :],
                                   ACT.Copy).then_inc(ffhi, 1)

            looped(act, b2, FF_UNITS, 4, hidden)
            b3 = b2 + FF_UNITS
            if l == DEPTH - 1 and debug is not None:
                for i in range(2):
                    for j in range(12):
                        next_high(b3, i, j, 3)
            else:
                looped(act, b3, DOWN_UNITS, 12, lambda i, j: next_high(b3, i, j, 3))

        act.wait_ge(consts_in, 16 * 6)
        act.activation(CT[:, 0, :, :], CC[:, :, :], ACT.Exp, scale=-1.0).then_inc(cexp, 1)
        act.wait_ge(cexp, 2)
        for u in range(2):
            split_high(u, 0, 1)
        for l in range(DEPTH):
            first_layer(l)
        second_act(act, next_high, inverse_root, chain)

    @block.vector
    def _(dve):
        chain = Chain(dve, dve_chain)

        def split_low(u, i, rounds):
            dve.wait_ge(hi_done, 4 * rounds * i + (u + 1))
            dve.tensor_tensor(WL[:, u % 2, :, :], RAW[:, u % 4, :, :], WH[:, u % 2, :, :].bitcast(f32),
                              ALU.subtract).then_inc(lo_done, 1)

        def next_low(base, i, j, rounds=1):
            dve.wait_ge(unit_done, 4 * rounds * i + (base + j + 1))
            if isinstance(i, int) and 4 * rounds * i + base + j + 2 >= total:
                return
            split_low(base + j + 2, i, rounds)

        def refine(y, v):
            chain(dve.tensor_tensor(v, v, y, ALU.mult))
            chain.wait()
            chain(dve.scalar_tensor_tensor(v, v, -0.5, y, ALU.mult, ALU.mult))
            chain.wait()
            chain(dve.scalar_tensor_tensor(y, v, 1.5, y, ALU.add, ALU.mult))
            chain.wait()

        def norm(l, half):
            dve.wait_ge(rstd_done, 2 * l + half + 1)
            refine(RS[:, 1, :], RS[:, 0, :])

            def low(k):
                dve.wait_ge(nhi_done, (2 * l + half) * KC + k + 1)
                at = 24 * half + k
                dve.scalar_tensor_tensor(H1[:, 1, k, :], NX[:, k % 4, :], M1[:, l, at:at + 1],
                                         H1[:, 0, k, :].bitcast(f32), ALU.add, ALU.subtract).then_inc(norm_done, 1)

            for k in range(KC):
                if k >= 4:
                    dve.wait_ge(norm_done, (2 * l + half) * KC + k - 3)
                dve.scalar_tensor_tensor(NX[:, k % 4, :], X[:, k, :], A1[:, l, half, k:k + 1], RS[:, 1, :],
                                         ALU.mult, ALU.mult).then_inc(nx_done, 1)
                if k >= 2:
                    low(k - 2)
            low(KC - 2)
            low(KC - 1)

        def columns(batch, l, at):
            dve.wait_ge(mod_used, sum(BATCHES[:batch + 1]))
            n = BATCHES[batch]
            if batch < 4:
                dve.tensor_tensor(M1[:, l, at:at + n], PS[:, 7, 0:n],
                                  P1[:, l, PAR1["bmod"] + at:PAR1["bmod"] + at + n], ALU.add).then_inc(mod_read, 1)
                dve.wait_ge(mod_read, batch + 1)
                for half in range(2):
                    s = 24 * half + KC
                    if at <= s and s + KC <= at + n:
                        g = PAR1["ln2" if half else "ln1"]
                        chain(dve.scalar_tensor_tensor(A1[:, l, half, :], M1[:, l, s:s + KC], 1.0,
                                                       P1[:, l, g:g + KC], ALU.add, ALU.mult))
                        chain.wait()
            else:
                for c in range(2):
                    ins = dve.tensor_tensor(M2[:, :, :, c],
                                            PS[:, 7, 0:2 * n].rearrange("p (l m c) -> p l m c", l=DEPTH, c=2)[:, :, :, c],
                                            P2[:, :, PAR2["bada"]:PAR2["bada"] + MOD2], ALU.add)
                ins.then_inc(mod_read, 1)
                dve.wait_ge(mod_read, batch + 1)
                for c in range(2):
                    chain(dve.scalar_tensor_tensor(A2[:, :, :, c], M2[:, :, KC:2 * KC, c], 1.0,
                                                   P2[:, :, PAR2["norm"]:PAR2["norm"] + KC], ALU.add, ALU.mult))
                chain.wait()

        def first_layer(l):
            base = l * PER
            norm(l, 0)
            looped(dve, base, V_UNITS, 4, lambda i, j: next_low(base, i, j))
            b = base + V_UNITS
            looped(dve, b, QK_UNITS, 4, lambda i, j: next_low(b, i, j))
            if l == 0:
                columns(1, 0, 16)
            for j in range(4):
                dve.wait_ge(bank_read[j], earlier(b + QK_UNITS + j))
            for n in range(2):
                chain(dve.tensor_scalar(COL[:, 4 * n:4 * n + 4], V[:, n, 448:452], 1.0 / 16, None, ALU.mult))
            for c in range(9):
                if c % 2 == 0:
                    n = 1 if c == 8 else 2
                    dve.wait_ge(rx_done, 5 * l + c // 2 + 1)
                    refine(TMP[:, c:c + n, :], VM[:, c:c + n, :])
                g = PAR1["gain"] + c
                dve.scalar_tensor_tensor(F[:, 3 + c, :], F[:, 3 + c, :], P1[:, l, g:g + 1], TMP[:, c, :],
                                         ALU.mult, ALU.mult).then_inc(rms_done, 1)
            sin = const("sin", T)[:, None, :].broadcast_to([P, 2, T])
            for g in range(6):
                dve.wait_ge(rot_done, 6 * l + g + 1)
                dve.tensor_tensor(SN[:, g % 2, :, :], PS[:, 4 + g % 2, :].rearrange("p (a b) -> p a b", a=2),
                                  sin, ALU.mult).then_inc(rot_read, 1)
                dve.wait_ge(rot_read, 6 * l + g + 1)
                dve.wait_ge(cosd, 6 * l + g + 1)
                dve.tensor_tensor(F[:, 2 * g:2 * g + 2, :], RO[:, 2 * g:2 * g + 2, :], SN[:, g % 2, :, :],
                                  ALU.add).then_inc(rope_done, 1)

            def banks(s):
                return PS[:, 2 * (s % 2):2 * (s % 2) + 2, :].rearrange("p a (b t) -> p (a b) t", b=2)

            dve.wait_ge(rope_done, 6 * l + 6)
            for n in range(2):
                w = P * (n + 1)
                dve.wait_ge(scores, 10 * l + n + 1)
                for p, h in enumerate(PLACE):
                    ins = dve.tensor_scalar(SM[:, n, p, 0:w], banks(n)[:, p, 0:w], 0.0,
                                            COL[:, 4 * n + h:4 * n + h + 1], ALU.max, ALU.mult)
                ins.then_inc(scores_read, 1)
                dve.wait_ge(scores_read, 10 * l + n + 1)
                chain(dve.tensor_reduce(WK[:, n, 0:w], SM[:, n, :, 0:w].rearrange("p h t -> p t h"),
                                        AX.X, ALU.add))
            chain.wait()
            causal = const("causal", 2 * T).rearrange("p (n t) -> p n t", n=2)
            for n in range(2):
                w = P * (n + 1)
                chain(dve.tensor_tensor(WK[:, n, 0:w], WK[:, n, 0:w], causal[:, n, 0:w], ALU.add))
            for r in range(TOPK // 8):
                chain.wait()
                for n in range(2):
                    chain(dve.max(COL[:, 40 + 8 * n:48 + 8 * n], WK[:, n, 0:P * (n + 1)]))
                chain.wait()
                for n in range(2):
                    w = P * (n + 1)
                    chain(dve.match_replace(WK[:, n, 0:w], COL[:, 40 + 8 * n:48 + 8 * n], WK[:, n, 0:w], GONE))
            chain.wait()
            for n in range(2):
                w = P * (n + 1)
                chain(dve.tensor_scalar(SEL[:, n, 0:w], WK[:, n, 0:w], GONE * 0.5, -BIG, ALU.is_gt, ALU.mult))
            chain.wait()
            for n in range(2):
                w = P * (n + 1)
                chain(dve.tensor_tensor(SEL[:, n, 0:w], SEL[:, n, 0:w], causal[:, n, 0:w], ALU.add))
            chain.wait()
            if l == 0:
                columns(2, 0, 32)
            band = const("band", 2 * T).rearrange("p (n t) -> p n t", n=2)
            strict = const("strict", 2 * T).rearrange("p (n t) -> p n t", n=2)

            def begin(s):
                a, n = s - 2, s % 2
                w, c = P * (n + 1), 8 + 16 * n
                sm = SM[:, n, :, 0:w]
                dve.wait_ge(scores, 10 * l + s + 1)
                if s >= 8:
                    m = strict[:, n, 0:w][:, None, :].broadcast_to([P, 4, w])
                    dve.scalar_tensor_tensor(sm, banks(s)[:, :, 0:w], 0.125, m, ALU.mult, ALU.add).then_inc(scores_read, 1)
                    return
                m = (SEL if s < 4 else band)[:, n, 0:w][:, None, :].broadcast_to([P, 4, w])
                dve.tensor_tensor(sm, banks(s)[:, :, 0:w], m, ALU.add).then_inc(scores_read, 1)
                dve.wait_ge(scores_read, 10 * l + s + 1)
                chain(dve.reduce_max(COL[:, c:c + 4], sm, AX.X))
                chain.wait()
                if s < 4:
                    dve.tensor_scalar(COL[:, c + 4:c + 8], COL[:, c:c + 4], -0.125, None, ALU.mult).then_inc(masked, 1)
                else:
                    k = PAR1["sinks"] + 4 * ((s - 4) // 2)
                    sink = P1[:, l, k:k + 4]
                    chain(dve.scalar_tensor_tensor(COL[:, c:c + 4], COL[:, c:c + 4], 0.125, sink, ALU.mult, ALU.max))
                    chain.wait()
                    dve.tensor_scalar(COL[:, c + 4:c + 8], COL[:, c:c + 4], -1.0, None, ALU.mult)
                    dve.tensor_tensor(COL[:, 48 + 4 * n:52 + 4 * n], sink, COL[:, c:c + 4],
                                      ALU.subtract).then_inc(masked, 1)

            def end(s):
                a, n = s - 2, s % 2
                w, c = P * (n + 1), 8 + 16 * n
                if s < 8:
                    dve.wait_ge(exped, 6 * l + a + 1)
                    if s >= 4:
                        chain(dve.tensor_tensor(COL[:, c + 8:c + 12], COL[:, c + 8:c + 12],
                                                COL[:, 40 + 4 * n:44 + 4 * n], ALU.add))
                        chain.wait()
                    chain(dve.reciprocal(COL[:, c + 12:c + 16], COL[:, c + 8:c + 12]))
                    chain.wait()
                    r = COL[:, c + 12:c + 16][:, :, None].broadcast_to([P, 4, w])
                    dve.tensor_tensor(PR[:, n, :, 0:w], PR[:, n, :, 0:w], r, ALU.mult).then_inc(probs, 1)
                else:
                    dve.wait_ge(scores_read, 10 * l + s + 1)
                    dve.wait_ge(bq, 2 * l + s - 8)
                    chain(dve.tensor_scalar(STK[:, :, 0:w], SM[:, n, :, 0:w], 0.0, None, ALU.max))
                    dve.wait_ge(bl, 2 * l + s - 8 + 1)
                    chain.wait()
                    for h in range(4):
                        chain(dve.tensor_tensor_scan(STK[:, h, 0:w][:, ::-1], PR[:, n, h, 0:w][:, ::-1],
                                                     STK[:, h, 0:w][:, ::-1], 0.0, ALU.add, ALU.add))
                    chain.wait()
                    dve.tensor_tensor(SM[:, n, :, 0:w], SM[:, n, :, 0:w], STK[:, :, 0:w],
                                      ALU.subtract).then_inc(bq, 1)

            begin(2)
            for s in range(2, 10):
                if s + 1 < 10:
                    begin(s + 1)
                end(s)
            def low(k):
                dve.wait_ge(ohi, l * KC + k + 1)
                dve.tensor_tensor(OS[:, 1, k, :], GATE[:, k % 4, :], OS[:, 0, k, :].bitcast(f32),
                                  ALU.subtract).then_inc(olo, 1)

            for k in range(KC):
                if k % 2 == 0:
                    dve.wait_ge(orr, 4 * l + k // 2 + 1)
                    refine(RSO[:, k:k + 2, :], VO[:, k:k + 2, :])
                if k >= 4:
                    dve.wait_ge(olo, l * KC + k - 3)
                g = PAR1["gout"] + k
                dve.scalar_tensor_tensor(GATE[:, k % 4, :], O[:, k, :], P1[:, l, g:g + 1], RSO[:, k, :],
                                         ALU.mult, ALU.mult).then_inc(ohf, 1)
                if k >= 2:
                    low(k - 2)
            low(KC - 2)
            low(KC - 1)
            b = b + QK_UNITS

            def project(i, j):
                next_low(b, i, j)
                k = 4 * i + j
                dve.scalar_tensor_tensor(X[:, bass.ds(k, 1), :], PS[:, j:j + 1, 0:T],
                                         M1[:, l, bass.ds(16 + k, 1)], X[:, bass.ds(k, 1), :],
                                         ALU.mult, ALU.add).then_inc(bank_read[j], 1)

            looped(dve, b, WO_UNITS, 4, project)
            norm(l, 1)
            b2 = b + WO_UNITS

            def hidden(i, j):
                next_low(b2, i, j)
                if j % 2:
                    m = 2 * i + (l * FC + j // 2 + 1)
                    dve.wait_ge(ff_done, m - 1)
                    dve.wait_ge(ffsig, m)
                    dve.tensor_tensor(GATE[:, 1, :], GATE[:, 0, :], PS[:, j - 1, 0:T], ALU.mult).then_inc(bank_read[j - 1], 1)
                    dve.wait_ge(bank_read[j - 1], i + (earlier(b2 + j - 1) + 1))
                    dve.tensor_tensor(GATE[:, 2, :], GATE[:, 1, :], PS[:, j, 0:T], ALU.mult).then_inc(bank_read[j], 1)
                    dve.wait_ge(ffhi, m)
                    dve.tensor_tensor(HID[:, 1, bass.ds(2 * i + j // 2, 1), :], GATE[:, 2:3, :],
                                      HID[:, 0, bass.ds(2 * i + j // 2, 1), :].bitcast(f32),
                                      ALU.subtract).then_inc(ff_done, 1)

            looped(dve, b2, FF_UNITS, 4, hidden)
            columns(3 + l, 1, 0)
            b3 = b2 + FF_UNITS

            def down(i, j):
                next_low(b3, i, j, 3)
                if j % 3 == 2:
                    k, bank = 4 * i + j // 3, j // 3
                    dve.scalar_tensor_tensor(X[:, bass.ds(k, 1), :], PS[:, bank:bank + 1, 0:T],
                                             M1[:, l, bass.ds(40 + k, 1)], X[:, bass.ds(k, 1), :],
                                             ALU.mult, ALU.add).then_inc(bank_read[bank], 1)

            if l == DEPTH - 1 and debug is not None:
                for i in range(2):
                    for j in range(12):
                        down(i, j)
            else:
                looped(dve, b3, DOWN_UNITS, 12, down)

        chain(dve.memset(EPSC[:, 0:1], EPS))
        dve.memset(EPSC[:, 1:2], 1.0).then_inc(cexp, 1)
        dve.wait_ge(cexp, 2)
        chain(dve.tensor_scalar(CT[:, 1, :, :], CT[:, 0, :, :], 1.0, None, ALU.add))
        chain.wait()
        chain(dve.reciprocal(CT[:, 0, :, :], CT[:, 1, :, :]))
        chain.wait()
        dve.tensor_tensor(CA[:, :, :], CC[:, :, :], CT[:, 0, :, :], ALU.mult).then_inc(cact, 1)
        for u in range(2):
            split_low(u, 0, 1)
        columns(0, 0, 0)
        for l in range(DEPTH):
            first_layer(l)
        second_dve(dve, next_low, refine, chain)
    ctx.close()


def _units(w):
    k, n = w.shape
    return w.reshape(k // P, P, n // P, P).transpose(2, 1, 0, 3)


def _padded(w, n):
    out = np.zeros((w.shape[0], n), w.dtype)
    out[:, :w.shape[1]] = w
    return out


def _weights(a):
    total = DEPTH * (FIRST_UNITS + SECOND_UNITS)
    s = np.zeros((total, P, KC, P), np.float32)
    at = 0

    def put(w):
        nonlocal at
        u = _units(w)
        s[at:at + len(u)] = u
        at += len(u)

    for l in range(DEPTH):
        w = a["w_in"][l]
        cuts = np.cumsum([256, 64, 64, 256, 64, 4, 256, 256, 256, 512, 128])
        qa, ka, va, qi, ki, wi, qb, kb, vb, qc, kc, vc = np.split(w, cuts, axis=1)
        put(_padded(np.concatenate([va, vb, vc, wi], 1), 512))
        put(np.concatenate([qi, ki, ki, qa, ka, ka, qc, kc[:, :64], kc[:, :64], kc[:, 64:], kc[:, 64:], qb, kb], 1))
        put(a["w_o"][l])
        both = np.stack([a["w_gate"][l].reshape(D, FC, P), a["w_up"][l].reshape(D, FC, P)], 2)
        put(both.reshape(D, 2 * D_FF))
        down = _units(a["w_down"][l])
        for n in range(KC):
            for part in range(3):
                piece = down[n][:, part * KC:(part + 1) * KC]
                s[at, :, :piece.shape[1]] = piece
                at += 1
    for l in range(DEPTH):
        w = a["w_in_2"][l]
        cuts = np.cumsum([512, 512, 1024, 16, 1024, 1024, 1024, 1024, 1024, 1024, 1024, 1024])
        aq, ak, av, ag, ao, az, bq, bk, bv, bz, cu, cz, mg = np.split(w, cuts, axis=1)
        put(np.stack([aq.reshape(D, 4, P), ak.reshape(D, 4, P)], 2).reshape(D, D))
        put(av)
        g = np.zeros((D, P), np.float32)
        for i in range(4):
            g[:, 32 * i:32 * i + 4] = ag[:, 4 * i:4 * i + 4]
        put(g)
        put(ao)
        put(az)

        def pairs(i, out):
            m = mg[:, i * D:(i + 1) * D].reshape(D, KC, P)
            put(np.stack([m, out.reshape(D, KC, P)], 2).reshape(D, 2 * D))

        pairs(0, a["w_a_out_2"][l])
        put(bq)
        put(bk)
        put(bv)
        put(bz)
        pairs(1, a["w_b_out_2"][l])
        put(cu)
        put(cz)
        pairs(2, a["w_c_out_2"][l])
        put(a["w_out_2"][l])
    assert at == total
    return s


def _modulations(a):
    return np.concatenate([_units(a["w_mod"][l]) for l in range(DEPTH)]
                          + [_units(a["w_ada_2"][l]) for l in range(DEPTH)])


def _column(v):
    return v.reshape(-1, P).T


def _parameters(a):
    p1 = np.zeros((P, DEPTH, PAR1_W), np.float32)
    p2 = np.zeros((P, DEPTH, PAR2_W), np.float32)

    def put(dst, places, l, name, v):
        dst[:, l, places[name]:places[name] + v.shape[1]] = v

    twice = lambda v: np.tile(v, 2)[:, None]
    for l in range(DEPTH):
        put(p1, PAR1, l, "ln1", _column(a["ln1"][l]))
        put(p1, PAR1, l, "ln2", _column(a["ln2"][l]))
        put(p1, PAR1, l, "bmod", _column(a["b_mod"][l]))
        qa, ka, qc, kc = (twice(a[n][l]) for n in ("qn_a", "kn_a", "qn_c", "kn_c"))
        put(p1, PAR1, l, "gain", np.concatenate([qa, qa, ka, qc, qc, qc, qc, kc, kc], 1))
        put(p1, PAR1, l, "gout", _column(a["g_out"][l].reshape(-1)))
        put(p1, PAR1, l, "sinks", np.tile(a["sinks"][l].reshape(2, 4)[:, PLACE].reshape(1, 8), (P, 1)))
        put(p2, PAR2, l, "norm", _column(a["norm_w_2"][l]))
        put(p2, PAR2, l, "bada", _column(a["b_ada_2"][l]))
        b = np.zeros((P, 1), np.float32)
        for i in range(4):
            b[32 * i:32 * i + 4, 0] = a["b_if_2"][l][4 * i:4 * i + 4]
        put(p2, PAR2, l, "bif", b)
        put(p2, PAR2, l, "anorm", _column(a["a_norm_w_2"][l]))
        put(p2, PAR2, l, "qn", twice(a["q_norm_w_2"][l]))
        put(p2, PAR2, l, "kn", twice(a["k_norm_w_2"][l]))
        put(p2, PAR2, l, "subln", a["subln_w_2"][l][:, None])
        lam = np.concatenate([a[n][l] for n in ("lambda_q1_2", "lambda_k1_2", "lambda_q2_2", "lambda_k2_2")])
        put(p2, PAR2, l, "lam", np.tile(lam[None, :], (P, 1)))
    return p1, p2


def _laid_out(a):
    p1, p2 = _parameters(a)
    first, second = constants()
    cols = np.stack([_column(a["c"][0]), _column(a["c_2"][0]), _column(a["c_ctx_2"])], 1)
    chunked = lambda x: x.T.reshape(KC, P, T).transpose(1, 0, 2)
    return {"stream": _weights(a), "mods": _modulations(a), "consts": first, "consts2": second, "par1": p1, "par2": p2,
            "ccols": cols, "xT": chunked(a["x"][0]), "ctxT": chunked(a["ctx_2"][0])}


def kernel(**inputs):
    import concourse.bacc as bacc
    from concourse.bass_utils import run_bass_kernel_spmd

    a = {k: np.asarray(v) for k, v in inputs.items()}
    nc = bacc.Bacc("TRN2", target_bir_lowering=False, num_devices=1, dynamic_dma_scratch_size=2048)
    arrays = {k: np.ascontiguousarray(v) for k, v in _laid_out(a).items()}
    args = [nc.dram_tensor(k, v.shape, mybir.dt.from_np(v.dtype), kind="ExternalInput").ap()
            for k, v in arrays.items()]
    out = nc.dram_tensor("outT", (P, KC, T), mybir.dt.float32, kind="ExternalOutput").ap()
    build(nc, *args, out)
    r = run_bass_kernel_spmd(nc, [arrays], core_ids=[0])
    return r.results[0]["outT"].transpose(1, 0, 2).reshape(D, T).T[None]
```

```python
import numpy as np

import concourse.bass as bass
from concourse import mybir
from contextlib import ExitStack

P = 128
T = 256
D = 1024
KC = D // P
DEPTH = 2
D_FF = 2816
FC = D_FF // P
BIG = 1.0e30
GONE = -3.0e38
TOPK = T // 4
PLACE = (0, 2, 1, 3)
EPS = 1e-6

UNIT = KC * P
V_UNITS, QK_UNITS, WO_UNITS, FF_UNITS, DOWN_UNITS = 4, 16, KC, 2 * FC, 3 * KC
FIRST_UNITS = V_UNITS + QK_UNITS + WO_UNITS + FF_UNITS + DOWN_UNITS
SECOND = [("aqk", 8), ("av", 8), ("ag", 2), ("ao", 8), ("az", 8), ("amerge", 16),
          ("bq", 8), ("bk", 8), ("bv", 8), ("bz", 8), ("bmerge", 16),
          ("cu", 8), ("cz", 8), ("cmerge", 16), ("out", 8)]
SECOND_UNITS = sum(n for _, n in SECOND)
MOD1, MOD2 = 48, 24
EARLY = 32
MOD_UNITS = DEPTH * (MOD1 + MOD2)
SUMS = 8
FF_MODS = 32

def _places(sizes):
    at, out = 0, {}
    for name, n in sizes:
        out[name] = at
        at += n
    return out, at

CONST, COMMON_W = _places([("ident", P), ("ones", P), ("heads", P)])
FIRST_CONST, FIRST_W = _places([("rot", P), ("cos", T), ("sin", T), ("causal", 2 * T), ("strict", 2 * T),
                                ("band", 2 * T)])
SECOND_CONST, SECOND_W = _places([("axrot", P), ("axcos", T), ("axsin", T), ("lower", P), ("upper", P),
                                  ("dft", 2 * 512)])
CONST.update({k: COMMON_W + v for k, v in [*FIRST_CONST.items(), *SECOND_CONST.items()]})
CONST_W = COMMON_W + max(FIRST_W, SECOND_W)
PAR1, PAR1_W = _places([("ln1", KC), ("ln2", KC), ("bmod", MOD1), ("gain", 9), ("gout", KC),
                        ("sinks", 8)])
PAR2, PAR2_W = _places([("norm", KC), ("bada", MOD2), ("bif", 1), ("anorm", KC), ("qn", 1),
                        ("kn", 1), ("subln", 1)])


def constants():
    f = np.float32
    first, second = np.zeros((P, COMMON_W + FIRST_W), f), np.zeros((P, COMMON_W + SECOND_W), f)
    r = np.arange(P)

    def put(name, a):
        c = second if name in SECOND_CONST else first
        c[:a.shape[0], CONST[name]:CONST[name] + a.shape[1]] = a

    put("ident", np.eye(P, dtype=f))
    put("ones", np.ones((P, P), f))
    put("heads", (r[:, None] // 64 == r[None, :] // 64).astype(f))

    def rotation(half):
        m = np.zeros((P, P), f)
        for o in range(P):
            if o % (2 * half) < half:
                m[o + half, o] = -1.0
            else:
                m[o - half, o] = 1.0
        return m

    put("rot", rotation(32))
    put("axrot", rotation(16))
    inv = (1.0 / (f(10000.0) ** (np.arange(0, 64, 2, dtype=f) / f(64)))).astype(f)
    ang = inv[r % 32][:, None] * np.arange(T, dtype=f)[None, :]
    put("cos", np.cos(ang))
    put("sin", np.sin(ang))
    inv = (f(10000.0) ** (-np.arange(0, 32, 2, dtype=f) / f(32))).astype(f)
    t = np.arange(T)
    pos = np.where((r % 64 < 32)[:, None], (t // 64)[None, :], (t % 64)[None, :]).astype(f)
    ang = inv[r % 16][:, None] * pos
    put("axcos", np.cos(ang))
    put("axsin", np.sin(ang))
    q = (np.arange(2)[None, :, None] * P + r[:, None, None])
    s = np.arange(T)[None, None, :]
    put("causal", np.where(s <= q, 0, -BIG).astype(f).reshape(P, 2 * T))
    put("strict", np.where(s < q, 0, -BIG).astype(f).reshape(P, 2 * T))
    put("band", np.where((s <= q) & (q - s < 128), 0, -BIG).astype(f).reshape(P, 2 * T))
    put("lower", np.where(r[:, None] <= r[None, :], 0, -BIG).astype(f))
    put("upper", np.where(r[:, None] >= r[None, :], 0, -BIG).astype(f))
    w = 2 * np.pi * ((np.arange(T)[:, None] * np.arange(T)[None, :]) % T) / T
    cos, sin = (np.cos(w) / 16).astype(f), (np.sin(w) / 16).astype(f)
    both = np.concatenate([cos, sin], 1)
    put("dft", both.reshape(2, P, 512).transpose(1, 0, 2).reshape(P, -1))
    return first, second[:, COMMON_W:]


def build(nc, stream, mods, consts, consts2, par1, par2, lam, ccols, xT, ctxT, outT):
    f32, f32r = mybir.dt.float32, mybir.dt.float32r
    ALU, ACT, AX = mybir.AluOpType, mybir.ActivationFunctionType, mybir.AxisListType
    PER = FIRST_UNITS
    ctx = ExitStack()

    def sb(name, shape, dt=f32):
        return ctx.enter_context(nc.sbuf_tensor(name, shape, dt))

    def sem(name):
        return ctx.enter_context(nc.semaphore(name))

    C = sb("C", [P, CONST_W])
    XX = sb("XX", [P, KC, 2 * T])
    AR = sb("AR", [P, 16384], f32r)
    WH = sb("WH", [P, 4, KC, P], f32r)
    WL = sb("WL", [P, 4, KC, P], f32r)
    RAW = sb("RAW", [P, 4, KC // 2, P])
    P1 = sb("P1", [P, DEPTH, PAR1_W])
    P2 = sb("P2", [P, DEPTH, PAR2_W])
    CC = sb("CC", [P, 3, KC])
    CA = sb("CA", [P, 3, KC])
    CT = sb("CT", [P, 2, 3, KC])
    M1 = sb("M1", [P, DEPTH, MOD1])
    A1 = sb("A1", [P, DEPTH, 2, KC])
    M2 = sb("M2", [P, DEPTH, MOD2, 2])
    A2 = sb("A2", [P, DEPTH, KC, 2])
    COL = sb("COL", [P, 64])
    EPSC = sb("EPSC", [P, 2])
    WORK = sb("WORK", [P, 22528])

    def const(name, n=P):
        return C[:, CONST[name]:CONST[name] + n]

    ident, ones, heads = const("ident"), const("ones"), const("heads")
    X = XX[:, :, T:2 * T]
    CB = XX[:, 0:KC // 2, 0:T]
    H1 = AR[:, 0:2 * KC * T].rearrange("p (s k t) -> p s k t", s=2, k=KC)
    HID = AR[:, 2 * KC * T:2 * KC * T + 2 * FC * T].rearrange("p (s k t) -> p s k t", s=2, k=FC)
    OS = AR[:, 2 * KC * T:4 * KC * T].rearrange("p (s k t) -> p s k t", s=2, k=KC)

    def work(at, *shape):
        n = int(np.prod(shape))
        v = WORK[:, at:at + n]
        names = "abcd"[:len(shape)]
        if len(shape) > 1:
            v = v.rearrange(f"p ({' '.join(names)}) -> p {' '.join(names)}",
                            **{names[i]: shape[i] for i in range(len(shape))})
        return v

    F = work(0, QK_UNITS, T)
    V = work(4096, 2, 512)
    O = work(5120, KC, T)
    SM = work(7168, 2, 4, T)
    PR = work(9216, 2, 4, T)
    PT = work(11264, 2, 3, 4, P)
    WK = work(14336, 2, T)
    SEL = work(14848, 2, T)
    GATE = work(15360, 4, T)
    GRING = work(16384, 4, KC, P)
    MV = work(20992, DEPTH * MOD1, SUMS)
    RS = work(20480, 2, T)
    SQ = work(7168, KC, T)
    TMP = work(9216, 9, T)
    NX = work(9216, 4, T)
    VM = work(5120, 9, T)
    VO = work(11264, KC, T)
    SN = work(7680, 2, 2, T)
    RSO = work(9216, KC, T)
    STK = work(15360, 4, T)
    RO = work(11520, 12, T)

    H2 = AR[:, 0:8192].rearrange("p (s k t) -> p s k t", s=2, k=KC)
    Y2 = AR[:, 8192:16384].rearrange("p (s k t) -> p s k t", s=2, k=KC)
    YB = work(0, KC, 2 * T)
    KB = work(4096, KC, 2 * T)
    EB = work(4096, 2, 4, 2 * T)
    V2 = work(8192, 4, D)
    ACC = work(12288, KC, 2 * T)
    SQ2 = work(12288, KC, 2 * T)
    GT = work(12288, 2 * T)
    GI, GF, CF = work(12800, 2, 2 * T), work(13824, 2, 2 * T), work(14848, 2, 2 * T)
    CM, TG = work(16384, 2, 2 * T), work(17408, 2, 2 * T)
    NMS, NMD, EMS = (work(18432 + 1024 * i, 2, 2 * T) for i in range(3))
    DN, TM2 = work(21504, 2 * T), work(22016, 2 * T)
    NX2, RS2 = work(16384, 4, 2 * T), work(18432, 2, 2 * T)
    SG, SZ = work(20480, 2, 2 * T), work(21504, 2, 2 * T)
    SQB, RB = work(16384, 2, 2 * T), work(17408, 2, 2 * T)
    TC, TS = work(18432, 2, T), work(18944, 2, T)
    PB, WT = work(19456, 2, 2, 2 * T), work(21504, 2, 4, P)
    VB, VP = work(18432, 2, 2 * T), work(19456, 2, 2 * T)
    UC = sb("UC", [P, 8, 4])
    LM = sb("LM", [P, 2 * DEPTH + 2 * DEPTH])
    LT = work(16384, 2, DEPTH, 64)
    LAM = work(16640, DEPTH, 4, 64)
    LR = sb("LR", [P, 2, DEPTH])
    BC = sb("BC", [P, 2, 8])

    PS = ctx.enter_context(nc.psum_tensor("PS", [P, 8, 512], f32))

    consts_in, consts2_in = sem("consts_in"), sem("consts2_in")
    c_in, later_in = sem("c_in"), sem("later_in")
    raw_full = [sem(f"raw_full{i}") for i in range(4)]
    hi_done, lo_done = sem("hi_done"), sem("lo_done")
    unit_done = sem("unit_done")
    bank_read = [sem(f"bank_read{i}") for i in range(4)]
    mod_full = [sem(f"mod_full{i}") for i in range(4)]
    mod_used, wide_used, mod_read = sem("mod_used"), sem("wide_used"), sem("mod_read")
    spread, spread_read = sem("spread"), sem("spread_read")
    dve_chain, act_chain = sem("dve_chain"), sem("act_chain")
    cexp, cact = sem("cexp"), sem("cact")
    sq_done, sum_done, rstd_done = sem("sq_done"), sem("sum_done"), sem("rstd_done")
    nx_done, nhi_done, norm_done = sem("nx_done"), sem("nhi_done"), sem("norm_done")
    rsq_done, ms_done, mr_done, rms_done = sem("rsq_done"), sem("ms_done"), sem("mr_done"), sem("rms_done")
    rx_done = sem("rx_done")
    sticks, wk_done = sem("sticks"), sem("wk_done")
    ffg = sem("ffg")
    rot_done, cosd, rot_read = sem("rot_done"), sem("cosd"), sem("rot_read")
    rope_done = sem("rope_done")
    scores, scores_read = sem("scores"), sem("scores_read")
    masked, exped, probs = sem("masked"), sem("exped"), sem("probs")
    turned, pt_ready, pv_done, o_ready = sem("turned"), sem("pt_ready"), sem("pv_done"), sem("o_ready")
    wis_done = sem("wis_done")
    bl, bq = sem("bl"), sem("bq")
    osq, oms, orr, ohf, ohi, olo = (sem(n) for n in ("osq", "oms", "orr", "ohf", "ohi", "olo"))
    ffsig, ffhi, ff_done = sem("ffsig"), sem("ffhi"), sem("ff_done")
    out_done = sem("out_done")
    lam_r, lam_e, lam_done = sem("lam_r"), sem("lam_e"), sem("lam_done")
    gprep, gdve, gexp, gturn, uc_done = (sem(n) for n in ("gprep", "gdve", "gexp", "gturn", "uc_done"))
    st_done, nm_full, nms, em_full, ems = (sem(n) for n in ("st_done", "nm_full", "nms", "em_full", "ems"))
    nmd, decayed, weighted, num_done, post_done = (sem(n) for n in ("nmd", "decayed", "weighted", "num_done", "post_done"))
    gsq, gms, grs, grx, gnorm, prx = (sem(n) for n in ("gsq", "gms", "grs", "grx", "gnorm", "prx"))
    sig_done, gated, yhi, y_done = (sem(n) for n in ("sig_done", "gated", "yhi", "y_done"))
    o_gated = sem("o_gated")
    mg_done, m_mul, acc_done, ahi, a_done = (sem(n) for n in ("mg_done", "m_mul", "acc_done", "ahi", "a_done"))
    psq, pms, prs, pscaled, prot, pcos, psin, p_done = (
        sem(n) for n in ("psq", "pms", "prs", "pscaled", "prot", "pcos", "psin", "p_done"))
    s2, mx2, ex2, w2, t2, wt2, pv2, ob2 = (sem(n) for n in ("s2", "mx2", "ex2", "w2", "t2", "wt2", "pv2", "ob2"))
    f1, f1_read, f2, f2_read = (sem(n) for n in ("f1", "f1_read", "f2", "f2_read"))

    block = ctx.enter_context(nc.Block())
    total = DEPTH * PER + DEPTH * SECOND_UNITS

    class Chain:

        def __init__(self, eng, s):
            self.eng, self.s, self.n = eng, s, 0

        def __call__(self, ins):
            ins.then_inc(self.s, 1)
            self.n += 1

        def wait(self):
            self.eng.wait_ge(self.s, self.n)

    def earlier(u):
        layer = (FIRST_UNITS - DOWN_UNITS + KC) // 4
        done = min(u // FIRST_UNITS, DEPTH)
        return done * layer + (u - done * FIRST_UNITS) // 4

    def looped(eng, base, count, step, body):
        with eng.Fori(0, count // step) as i:
            for j in range(step):
                body(i, j)

    def stages(l):
        at, out = DEPTH * FIRST_UNITS + l * SECOND_UNITS, {}
        for name, n in SECOND:
            out[name] = at
            at += n
        return out

    def cover(d, c, l):
        low = 2 * l
        if d == 0:
            return [(max(c, low), 4)]
        found = {0: [(0, 1), (2, 4)], 1: [(0, 4)], 2: [(2, 3)], 3: [(2, 4)]}[c]
        return [(max(a, low), b) for a, b in found if b > low]

    def beyond(d, c, l):
        out = []
        for a, b in cover(d, c, l):
            if a <= c < b:
                out += [(a, c), (c + 1, b)]
            else:
                out.append((a, b))
        return [(a, b) for a, b in out if a < b]

    def tiles(l):
        return [(h, n) for h in range(8) for n in range(2 * l, 4)]

    def tile_base(l):
        return 32 * l

    def parts(l):
        return range(l, 2)

    def second_pe(pe, feature_unit, token_pair):
        def layer(l):
            st, t0 = stages(l), l * T
            idx = 4 + l
            moving, all_moving, ymoving = H2[:, :, :, t0:], H2, Y2[:, :, :, t0:]
            n = 2 * T - t0
            for k in range(KC):
                pe.wait_ge(sq_done, idx * KC + k + 1)
                last = pe.matmul(PS[:, 6, :], ones, SQ2[:, k, :], start=(k == 0), stop=(k == KC - 1))
            last.then_inc(sum_done, 1)
            pe.wait_ge(norm_done, (idx + 1) * KC)
            b = st["aqk"]

            def tokens(name, first):
                with pe.Fori(0, 2) as i:
                    for j in (0, 2):
                        token_pair(st[name], i, j, H2, first, 4)

            def qk(i, j):
                if j % 2:
                    feature_unit(b, i, j, all_moving, 2 * T)
                else:
                    feature_unit(b, i, j, moving, n)

            looped(pe, b, 8, 4, qk)
            tokens("av", 0)
            feature_unit(st["ag"], 0, 0, all_moving, 2 * T)
            pe.wait_ge(lo_done, 2 * (st["ag"] + 2))
            last = pe.matmul(PS[:, (st["ag"] + 1) % 4, 0:P], ident, ident, start=True, stop=True)
            last.then_inc(unit_done, 1)
            pe.wait_ge(gdve, l + 1)
            for d in range(2):
                for c in range(4):
                    at = (4 * d + c) * 4
                    last = pe.transpose(PS[:, 4, at:at + 4], GI[0:4, d, c * P:(c + 1) * P], ident[0:4, 0:4])
            last.then_inc(gturn, 1)
            pe.wait_ge(gexp, l + 1)
            pe.wait_ge(uc_done, l + 1)
            for j in range(4):
                pe.wait_ge(bank_read[(st["ao"] + j) % 4], earlier(st["ao"] + j))
            def pick(h):
                return ident[0:4, h:h + 1].broadcast_to([4, P])

            def numerator(e):
                h, d = e // 2, e % 2
                pe.wait_ge(weighted, 8 * l + e + 1)
                if 8 * l + e:
                    pe.wait_ge(post_done, 8 * l + e)
                order = [1, 0, 2, 3] if d else [0, 1, 2, 3]
                for v in range(3):
                    runs = [(c, a, b) for c in order for a, b in cover(d, c, l)]
                    for r, (c, a, b) in enumerate(runs):
                        lhs = ones if v == 2 else V2[:, c, (2 * h + v) * P:(2 * h + v + 1) * P]
                        last = pe.matmul(PS[:, 5 + v, a * P:b * P], lhs, EB[:, d, c, a * P:b * P],
                                         start=(r == 0), stop=(r == len(runs) - 1))
                last.then_inc(num_done, 1)

            for e in range(8):
                h, d = e // 2, e % 2
                if e:
                    pe.wait_ge(ems, 8 * l + e)
                pe.matmul(PS[:, 4, t0:], pick(h), CM[0:4, d, t0:],
                          start=True, stop=True).then_inc(nm_full, 1)
                pe.wait_ge(nms, 8 * l + e + 1)
                pe.matmul(PS[:, 4, t0:], pick(h), TG[0:4, d, t0:],
                          start=True, stop=True).then_inc(em_full, 1)
                if d == 0:
                    if e:
                        pe.wait_ge(weighted, 8 * l + e)
                    for c in range(4):
                        a = max(t0, 2 * (c // 2) * P)
                        last = pe.matmul(PS[:, c, a:], YB[:, 2 * h + 1, c * P:(c + 1) * P], YB[:, 2 * h, a:],
                                         start=True, stop=True)
                    last.then_inc(st_done, 1)
                if e:
                    numerator(e - 1)
            numerator(7)

            def norm_groups(first, groups, wide):
                for g in range(groups):
                    x = first + g
                    pe.wait_ge(gsq, 12 * l + x + 1)
                    if x >= 2:
                        pe.wait_ge(grs, 12 * l + x - 1)
                    for w in range(wide):
                        last = pe.matmul(PS[:, 4 + x % 2, t0:], ones, SQN(x, w)[:, t0:],
                                         start=(w == 0), stop=(w == wide - 1))
                    last.then_inc(gms, 1)

            norm_groups(0, 4, 2)
            looped(pe, st["ao"], 8, 4, lambda i, j: feature_unit(st["ao"], i, j, moving, n))
            looped(pe, st["az"], 8, 4, lambda i, j: feature_unit(st["az"], i, j, moving, n))

            def merge(name, branch):
                b = st[name]

                def pair(i, j):
                    if j % 2:
                        feature_unit(b, i, j, ymoving, n)
                    else:
                        feature_unit(b, i, j, moving, n)

                pe.wait_ge(y_done, (3 * l + branch + 1) * KC)
                looped(pe, b, 16, 4, pair)

            merge("amerge", 0)
            looped(pe, st["bq"], 8, 4, lambda i, j: feature_unit(st["bq"], i, j, moving, n))
            looped(pe, st["bk"], 8, 4, lambda i, j: feature_unit(st["bk"], i, j, all_moving, 2 * T))

            def rotate(x):
                src = (YB if x < 8 else KB)[:, x % 8, T:2 * T]
                pe.wait_ge(pscaled, 16 * l + x + 1)
                if x >= 2:
                    pe.wait_ge(psin, 16 * l + x - 1)
                pe.matmul(PS[:, 6 + x % 2, 0:T], const("axrot"), src, start=True, stop=True).then_inc(prot, 1)

            for x in range(16):
                a = t0 if x < 8 else 0
                pe.wait_ge(psq, 16 * l + x + 1)
                if x >= 2:
                    pe.wait_ge(prs, 16 * l + x - 1)
                pe.matmul(PS[:, 4 + x % 2, a:], heads, SQB[:, x % 2, a:], start=True, stop=True).then_inc(pms, 1)
                if x:
                    rotate(x - 1)
            rotate(15)
            tokens("bv", 0)
            for j in range(4):
                pe.wait_ge(bank_read[(st["bz"] + j) % 4], earlier(st["bz"] + j))
            pe.wait_ge(p_done, 16 * (l + 1))
            steps = tiles(l)

            def score(f):
                h, q = steps[f]
                keys = 2 * T if q >= 2 else T
                if f >= 2:
                    pe.wait_ge(ex2, tile_base(l) + f - 1)
                for m in range(2):
                    rows = slice(64 * m, 64 * m + 64)
                    last = pe.matmul(PS[:, 2 * (f % 2) + m, 0:keys], YB[rows, h, q * P:(q + 1) * P],
                                     KB[rows, h, 0:keys], start=True, stop=True)
                last.then_inc(s2, 1)

            def turn(f):
                h, q = steps[f]
                pe.wait_ge(w2, tile_base(l) + f + 1)
                if f >= 2:
                    pe.wait_ge(wt2, tile_base(l) + f - 1)
                for c in range(4 if q >= 2 else 2):
                    last = pe.transpose(PS[:, 4 + f % 2, c * P:(c + 1) * P], PB[:, f % 2, 0, c * P:(c + 1) * P],
                                        ident)
                last.then_inc(t2, 1)

            def value(f):
                h, q = steps[f]
                blocks = 4 if q >= 2 else 2
                pe.wait_ge(wt2, tile_base(l) + f + 1)
                if q == 2 * l and h >= 2:
                    pe.wait_ge(ob2, 8 * l + h - 1)
                for c in range(blocks):
                    last = pe.matmul(PS[:, 6 + h % 2, q * P:(q + 1) * P], V2[:, c, h * P:(h + 1) * P],
                                     WT[:, f % 2, c, :], start=(c == 0), stop=(c == blocks - 1))
                last.then_inc(pv2, 1)

            score(0)
            score(1)
            for f in range(len(steps)):
                turn(f)
                if f + 2 < len(steps):
                    score(f + 2)
                if f:
                    value(f - 1)
            value(len(steps) - 1)
            norm_groups(4, 8, 1)
            looped(pe, st["bz"], 8, 4, lambda i, j: feature_unit(st["bz"], i, j, moving, n))
            merge("bmerge", 1)
            tokens("cu", 2 * l)
            for j in range(4):
                pe.wait_ge(bank_read[(st["cz"] + j) % 4], earlier(st["cz"] + j))
            dft = const("dft", 1024).rearrange("p (m n) -> p m n", m=2)
            for p in parts(l):
                past = 8 * (p if l == 0 else 2)
                for x in range(8):
                    if past + x >= 2:
                        pe.wait_ge(f1_read, past + x - 1)
                    for m in range(2):
                        last = pe.matmul(PS[:, 4 + x % 2, :], V2[:, 2 * p + m, x * P:(x + 1) * P], dft[:, m, :],
                                         start=(m == 0), stop=(m == 1))
                    last.then_inc(f1, 1)
                pe.wait_ge(f1_read, past + 8)
                for x in range(8):
                    if past + x >= 2:
                        pe.wait_ge(f2_read, past + x - 1)
                    cut, sine = (slice(at + (x % 2) * P, at + (x % 2 + 1) * P) for at in (0, T))
                    for m in range(2):
                        src = KB[:, x // 2 * 2 + m, :]
                        pe.matmul(PS[:, 6 + x % 2, 0:T], dft[:, m, cut], src[:, 0:T], start=(m == 0), stop=False)
                        last = pe.matmul(PS[:, 6 + x % 2, 0:T], dft[:, m, sine], src[:, T:], start=False,
                                         stop=(m == 1))
                    last.then_inc(f2, 1)
            looped(pe, st["cz"], 8, 4, lambda i, j: feature_unit(st["cz"], i, j, moving, n))
            merge("cmerge", 2)
            pe.wait_ge(a_done, (l + 1) * KC)
            looped(pe, st["out"], 8, 4, lambda i, j: feature_unit(st["out"], i, j, moving, n))

        return layer

    def SQN(x, w):
        return EB[:, x % 2, w, :] if x < 4 else SQB[:, x % 2, :]

    def second_act(act, done, next_high, exponentials, sigmoids, inverse_root, chain):
        def layer(l):
            st, t0 = stages(l), l * T
            idx, n = 4 + l, 2 * T - l * T
            for k in range(KC):
                if l:
                    u = stages(l - 1)["out"] + k
                    act.wait_ge(bank_read[u % 4], earlier(u) + 1)
                else:
                    act.wait_ge(bank_read[k % 4], earlier(DEPTH * FIRST_UNITS - DOWN_UNITS) + k // 4 + 1)
                act.activation(SQ2[:, k, :], XX[:, k, :], ACT.Square).then_inc(sq_done, 1)
            act.wait_ge(sum_done, idx + 1)
            inverse_root(RS2[:, 1, :], RS2[:, 0, :], PS[:, 6, :], 1.0 / D, None, rstd_done)
            act.wait_ge(mod_read, 1)
            for k in range(KC):
                act.wait_ge(nx_done, idx * KC + k + 1)
                for c in range(2):
                    cut = slice((1 - c) * T, (2 - c) * T)
                    last = act.activation(H2[:, 0, k, cut], NX2[:, k % 4, cut], ACT.Identity,
                                          bias=M2[:, l, k, c:c + 1])
                last.then_inc(nhi_done, 1)
            b = st["aqk"]

            def copied(b, dst, lo, scale=1.0):
                def body(i, j):
                    done(b, i, j)
                    bank = (b + j) % 4
                    act.activation(dst[:, bass.ds(4 * i + j, 1), lo:], PS[:, bank:bank + 1, 0:2 * T - lo],
                                   ACT.Copy).then_inc(bank_read[bank], 1)
                    next_high(b, i, j)
                return body

            def qk(i, j):
                done(b, i, j)
                bank = (b + j) % 4
                lo, scale = (0, float(P) ** -0.5) if j % 2 else (t0, 1.0)
                act.activation(YB[:, bass.ds(4 * i + j, 1), lo:], PS[:, bank:bank + 1, 0:2 * T - lo],
                               ACT.Copy, scale=scale).then_inc(bank_read[bank], 1)
                next_high(b, i, j)

            def values(b, first):
                def body(i, j):
                    done(b, i, j)
                    bank, half = (b + j) % 4, (4 - first) // 2
                    row = first + (j % 2) * half
                    act.activation(V2[:, row:row + half, bass.ds((4 * i + j // 2 * 2) * P, 2 * P)],
                                   PS[:, bank, 0:half * 2 * P].rearrange("p (b c) -> p b c", b=half),
                                   ACT.Copy).then_inc(bank_read[bank], 1)
                    next_high(b, i, j)
                return body

            looped(act, b, 8, 4, qk)
            looped(act, st["av"], 8, 4, values(st["av"], 0))
            u = st["ag"]
            done(u, 0, 0)
            act.activation(GT, PS[:, u % 4, :], ACT.Identity,
                           bias=P2[:, l, PAR2["bif"]:PAR2["bif"] + 1]).then_inc(bank_read[u % 4], 1)
            next_high(u, 0, 0)
            next_high(u, 0, 1)
            act.wait_ge(bank_read[u % 4], earlier(u) + 1)
            for d in range(2):
                ins = act.activation(GI[0:4, d, :], GT[64 * d:64 * d + 4, :], ACT.Copy)
                if d:
                    ins.then_inc(bank_read[(u + 1) % 4], 1)
                chain(act.activation(GF[0:4, d, :], GT[64 * d + 32:64 * d + 36, :], ACT.Copy))
            chain.wait()
            chain(act.activation(CF[0:4, :, :], GF[0:4, :, :], ACT.Abs))
            chain.wait()
            chain(act.activation(CF[0:4, :, :], CF[0:4, :, :], ACT.Exp, scale=-1.0))
            chain.wait()
            act.activation(CF[0:4, :, :], CF[0:4, :, :], ACT.Ln, bias=EPSC[0:4, 1:2]).then_inc(gprep, 1)
            act.wait_ge(gdve, l + 1)
            act.activation(TG[0:4, :, :], TG[0:4, :, :], ACT.Exp, scale=-1.0).then_inc(gexp, 1)
            act.wait_ge(uc_done, l + 1)
            for e in range(8):
                d, h = e % 2, e // 2
                act.wait_ge(nm_full, 8 * l + e + 1)
                if e >= 2:
                    act.wait_ge(nmd, 8 * l + e - 1)
                    act.wait_ge(decayed, 8 * l + e - 1)
                act.activation(NMS[:, d, t0:], PS[:, 4, t0:], ACT.Copy).then_inc(nms, 1)
                act.wait_ge(em_full, 8 * l + e + 1)
                if e >= 2:
                    act.wait_ge(post_done, 8 * l + e - 1)
                act.activation(EMS[:, d, t0:], PS[:, 4, t0:], ACT.Copy).then_inc(ems, 1)
                act.wait_ge(nmd, 8 * l + e + 1)
                act.wait_ge(nms, 8 * l + e + 1)
                if e >= 2:
                    act.wait_ge(num_done, 8 * l + e - 1)
                for c in range(4):
                    bias = UC[:, 4 * d + c, h:h + 1]
                    if c >= 2 * l:
                        cut = slice(c * P, (c + 1) * P)
                        last = act.activation(EB[:, d, c, cut], NMD[:, d, cut], ACT.Exp, bias=bias)
                    for a, z in beyond(d, c, l):
                        cut = slice(a * P, z * P)
                        last = act.activation(EB[:, d, c, cut], NMS[:, d, cut], ACT.Exp, bias=bias)
                last.then_inc(decayed, 1)

            def norm_groups(first, groups, wide, scale):
                for g in range(groups + 1):
                    x = first + g
                    if g < groups:
                        if x == 0:
                            act.wait_ge(post_done, 8 * (l + 1))
                            act.wait_ge(num_done, 8 * (l + 1))
                        if g >= 2:
                            act.wait_ge(gms, 12 * l + x - 1)
                        for w in range(wide):
                            last = act.activation(SQN(x, w)[:, t0:], YB[:, wide * g + w, t0:], ACT.Square)
                        last.then_inc(gsq, 1)
                    if g:
                        x -= 1
                        act.wait_ge(gms, 12 * l + x + 1)
                        if g >= 3:
                            act.wait_ge(gnorm, 12 * l + x - 1)
                        inverse_root(NRM(x)[:, t0:], VRM(x)[:, t0:], PS[:, 4 + x % 2, t0:], scale,
                                     (grs, 12 * l + x + 1), grx)

            norm_groups(0, 4, 2, 1.0 / 256)

            def output_gate(i, j):
                b = st["ao"]
                done(b, i, j)
                bank = (b + j) % 4
                act.wait_ge(o_gated, 4 * i + (8 * l + max(j - 1, 0)))
                act.activation(SG[:, j % 2, t0:], PS[:, bank, 0:n], ACT.Sigmoid).then_inc(bank_read[bank], 1)
                next_high(b, i, j)

            sigmoids()
            looped(act, st["ao"], 8, 4, output_gate)

            def z_gate(name, branch):
                b = st[name]

                def body(i, j):
                    done(b, i, j)
                    bank = (b + j) % 4
                    y = 4 * i + ((3 * l + branch) * KC + j)
                    act.activation(SG[:, j % 2, t0:], PS[:, bank, 0:n], ACT.Sigmoid).then_inc(sig_done, 1)
                    next_high(b, i, j)
                    act.wait_ge(gated, y + 1)
                    act.activation(Y2[:, 0, bass.ds(4 * i + j, 1), t0:], YB[:, bass.ds(4 * i + j, 1), t0:],
                                   ACT.Copy).then_inc(yhi, 1)

                looped(act, b, 8, 4, body)

            def merge(name, branch):
                b = st[name]

                def body(i, j):
                    bank = (b + j) % 4
                    if j % 2 == 0:
                        done(b, i, j)
                        act.wait_ge(bank_read[(b + j - 1) % 4], i + (earlier(b + j - 1) + 1))
                        act.activation(SG[:, j // 2, t0:], PS[:, bank, 0:n], ACT.Sigmoid).then_inc(bank_read[bank], 1)
                    next_high(b, i, j)

                looped(act, b, 16, 4, body)

            act.wait_ge(o_gated, KC * (l + 1))
            z_gate("az", 0)
            merge("amerge", 0)
            exponentials()
            looped(act, st["bq"], 8, 4, copied(st["bq"], YB, t0))
            looped(act, st["bk"], 8, 4, copied(st["bk"], KB, 0))
            for j in range(4):
                act.wait_ge(bank_read[(st["bv"] + j) % 4], earlier(st["bv"] + j))
            for x in range(17):
                if x < 16:
                    a = t0 if x < 8 else 0
                    src = (YB if x < 8 else KB)[:, x % 8, a:]
                    if x >= 2:
                        act.wait_ge(pms, 16 * l + x - 1)
                    act.activation(SQB[:, x % 2, a:], src, ACT.Square).then_inc(psq, 1)
                if x:
                    y = x - 1
                    a = t0 if y < 8 else 0
                    act.wait_ge(pms, 16 * l + y + 1)
                    if y >= 2:
                        act.wait_ge(pscaled, 16 * l + y - 1)
                    inverse_root(RB[:, y % 2, a:], VP[:, y % 2, a:], PS[:, 4 + y % 2, a:], 1.0 / 64,
                                 (prs, 16 * l + y + 1), prx)
            looped(act, st["bv"], 8, 4, values(st["bv"], 0))
            steps, tb = tiles(l), tile_base(l)

            def exps(f):
                h, q = steps[f]
                keys = 2 * T if q >= 2 else T
                act.wait_ge(mx2, tb + f + 1)
                if f >= 2:
                    act.wait_ge(t2, tb + f - 1)
                for m in range(2):
                    last = act.activation(PB[:, f % 2, m, 0:keys], PS[:, 2 * (f % 2) + m, 0:keys], ACT.Exp,
                                          bias=BC[:, f % 2, 2 + m:3 + m], scale=0.125,
                                          accum_out=BC[:, f % 2, 4 + m:5 + m])
                last.then_inc(ex2, 1)

            def head_out(h):
                act.wait_ge(pv2, tb + (h + 1) * (4 - 2 * l))
                act.activation(YB[:, h, t0:], PS[:, 6 + h % 2, t0:], ACT.Copy).then_inc(ob2, 1)

            exps(0)
            per = 4 - 2 * l
            for f in range(len(steps)):
                if f + 1 < len(steps):
                    exps(f + 1)
                act.wait_ge(t2, tb + f + 1)
                if f >= 2:
                    act.wait_ge(pv2, tb + f - 1)
                blocks = 4 if steps[f][1] >= 2 else 2
                act.activation(WT[:, f % 2, 0:blocks, :],
                               PS[:, 4 + f % 2, 0:blocks * P].rearrange("p (a b) -> p a b", a=blocks),
                               ACT.Copy).then_inc(wt2, 1)
                if f and f % per == 0:
                    head_out(f // per - 1)
            head_out(7)
            act.wait_ge(ob2, 8 * (l + 1))
            norm_groups(4, 8, 1, 1.0 / 128)
            sigmoids()
            z_gate("bz", 1)
            merge("bmerge", 1)
            looped(act, st["cu"], 8, 4, values(st["cu"], 2 * l))
            for p in parts(l):
                past = 8 * (p if l == 0 else 2)
                for x in range(8):
                    act.wait_ge(f1, past + x + 1)
                    act.activation(KB[:, x, 0:T], PS[:, 4 + x % 2, 0:T], ACT.Copy)
                    act.activation(KB[:, x, T:], PS[:, 4 + x % 2, T:], ACT.Copy, scale=-1.0).then_inc(f1_read, 1)
            z_gate("cz", 2)
            merge("cmerge", 2)
            exponentials()
            act.wait_ge(unit_done, st["out"])
            for k in range(KC):
                act.wait_ge(acc_done, (2 * l + 1) * KC + k + 1)
                act.activation(H2[:, 0, k, t0:], ACC[:, k, t0:], ACT.Copy).then_inc(ahi, 1)
            if l == DEPTH - 1:
                for i in range(2):
                    for j in range(4):
                        next_high(st["out"], i, j)
            else:
                looped(act, st["out"], 8, 4, lambda i, j: next_high(st["out"], i, j))

        act.wait_ge(lam_r, 1)
        act.activation(LM[:, 0:4], LR[:, :, :].rearrange("p a b -> p (a b)"), ACT.Exp).then_inc(lam_e, 1)
        for l in range(DEPTH):
            layer(l)

    def VRM(x):
        return NMD[:, x % 2, :] if x < 4 else VB[:, x % 2, :]

    def NRM(x):
        return NMS[:, x % 2, :] if x < 4 else RB[:, x % 2, :]

    def second_dve(dve, done, next_low, refine, chain):
        def layer(l):
            st, t0 = stages(l), l * T
            idx, n = 4 + l, 2 * T - l * T
            dve.wait_ge(rstd_done, idx + 1)
            refine(RS2[:, 1, :], RS2[:, 0, :])

            def low(k):
                dve.wait_ge(nhi_done, idx * KC + k + 1)
                for c in range(2):
                    cut = slice((1 - c) * T, (2 - c) * T)
                    ins = dve.scalar_tensor_tensor(H2[:, 1, k, cut], NX2[:, k % 4, cut], M2[:, l, k, c:c + 1],
                                                   H2[:, 0, k, cut].bitcast(f32), ALU.add, ALU.subtract)
                ins.then_inc(norm_done, 1)

            for k in range(KC):
                if k >= 4:
                    dve.wait_ge(norm_done, idx * KC + k - 3)
                for c in range(2):
                    cut = slice((1 - c) * T, (2 - c) * T)
                    ins = dve.scalar_tensor_tensor(NX2[:, k % 4, cut], XX[:, k, cut], A2[:, l, k, c:c + 1],
                                                   RS2[:, 1, cut], ALU.mult, ALU.mult)
                ins.then_inc(nx_done, 1)
                if k >= 2:
                    low(k - 2)
            low(KC - 2)
            low(KC - 1)

            def lows(name, count=8):
                b = st[name]
                looped(dve, b, count, 4, lambda i, j: next_low(b, i, j))

            lows("aqk")
            lows("av")
            next_low(st["ag"], 0, 0)
            next_low(st["ag"], 0, 1)
            chain(dve.memset(TG[0:4, :, :], 0.0))
            dve.wait_ge(gprep, l + 1)
            chain(dve.scalar_tensor_tensor(GF[0:4, :, :], GF[0:4, :, :], 0.0, CF[0:4, :, :], ALU.min, ALU.subtract))
            chain.wait()

            def scans(dst, src, other, op):
                chain(dve.tensor_tensor_scan(dst[0:4, 0, :], src[0:4, 0, :], other(slice(0, 2 * T), 0), 0.0, op, op))
                chain(dve.tensor_tensor_scan(dst[0:4, 1, 0:T][:, ::-1], src[0:4, 1, 0:T][:, ::-1],
                                             other(slice(0, T), 1)[:, ::-1], 0.0, op, op))
                chain.wait()
                chain(dve.tensor_tensor_scan(dst[0:4, 1, T:][:, ::-1], src[0:4, 1, T:][:, ::-1],
                                             other(slice(T, 2 * T), 1)[:, ::-1], dst[0:4, 1, 0:1], op, op))
                chain.wait()

            scans(CF, GF, lambda cut, d: TG[0:4, d, cut], ALU.add)
            chain(dve.tensor_tensor(GI[0:4, :, :], GI[0:4, :, :], CF[0:4, :, :], ALU.subtract))
            chain.wait()
            scans(CM, GI, lambda cut, d: GI[0:4, d, cut], ALU.max)
            chain(dve.tensor_tensor(TG[0:4, :, :], CF[0:4, :, :], CM[0:4, :, :], ALU.add))
            chain.wait()
            dve.tensor_scalar(CM[0:4, :, :], CM[0:4, :, :], -1.0, None, ALU.mult).then_inc(gdve, 1)
            dve.wait_ge(gturn, l + 1)
            dve.tensor_copy(UC[:, :, :], PS[:, 4, 0:32].rearrange("p (a b) -> p a b", a=8)).then_inc(uc_done, 1)

            def mask(e):
                d = e % 2
                dve.wait_ge(nms, 8 * l + e + 1)
                tri = const("upper" if d else "lower")[:, None, :].broadcast_to([P, 4 - 2 * l, P])
                if e >= 2:
                    dve.wait_ge(decayed, 8 * l + e - 1)
                dve.tensor_tensor(NMD[:, d, t0:].rearrange("p (a b) -> p a b", b=P),
                                  NMS[:, d, t0:].rearrange("p (a b) -> p a b", b=P), tri, ALU.add).then_inc(nmd, 1)

            def post(e):
                d, h = e % 2, e // 2
                dve.wait_ge(num_done, 8 * l + e + 1)
                dve.wait_ge(ems, 8 * l + e + 1)
                if e:
                    dve.wait_ge(post_done, 8 * l + e)
                chain(dve.tensor_tensor(DN[:, t0:], PS[:, 7, t0:], EMS[:, d, t0:], ALU.max))
                chain.wait()
                chain(dve.scalar_tensor_tensor(DN[:, t0:], PS[:, 7, t0:], -1.0, DN[:, t0:], ALU.mult, ALU.max))
                chain.wait()
                chain(dve.reciprocal(DN[:, t0:], DN[:, t0:]))
                chain.wait()
                for v in range(2):
                    y = YB[:, 2 * h + v, t0:]
                    if d == 0:
                        ins = dve.tensor_tensor(y, PS[:, 5 + v, t0:], DN[:, t0:], ALU.mult)
                    else:
                        if v:
                            chain.wait()
                        chain(dve.tensor_tensor(TM2[:, t0:], PS[:, 5 + v, t0:], DN[:, t0:], ALU.mult))
                        chain.wait()
                        ins = dve.tensor_tensor(y, y, TM2[:, t0:], ALU.add)
                        if v == 0:
                            chain(ins)
                ins.then_inc(post_done, 1)

            mask(0)
            for e in range(8):
                d = e % 2
                if e + 1 < 8:
                    mask(e + 1)
                dve.wait_ge(decayed, 8 * l + e + 1)
                dve.wait_ge(st_done, 4 * l + e // 2 + 1)
                for c in range(4):
                    for a, z in cover(d, c, l):
                        cut = slice(a * P, z * P)
                        ins = dve.tensor_tensor(EB[:, d, c, cut], EB[:, d, c, cut], PS[:, c, cut], ALU.mult)
                ins.then_inc(weighted, 1)
                if e:
                    post(e - 1)
            post(7)

            def norm_groups(first, groups, wide, gain):
                for g in range(groups):
                    x = first + g
                    dve.wait_ge(grx, 12 * l + x + 1)
                    refine(NRM(x)[:, t0:], VRM(x)[:, t0:])
                    for w in range(wide):
                        y = YB[:, wide * g + w, t0:]
                        ins = dve.scalar_tensor_tensor(y, y, gain(wide * g + w), NRM(x)[:, t0:], ALU.mult, ALU.mult)
                    ins.then_inc(gnorm, 1)

            at = PAR2["anorm"]
            norm_groups(0, 4, 2, lambda k: P2[:, l, at + k:at + k + 1])
            dve.wait_ge(gnorm, 12 * l + 4)

            def output_gate(i, j):
                b = st["ao"]
                bank = (b + j) % 4
                dve.wait_ge(bank_read[bank], i + (earlier(b + j) + 1))
                y = YB[:, bass.ds(4 * i + j, 1), t0:]
                dve.tensor_tensor(y, y, SG[:, j % 2:j % 2 + 1, t0:], ALU.mult).then_inc(o_gated, 1)
                next_low(b, i, j)

            looped(dve, st["ao"], 8, 4, output_gate)

            def z_gate(name, branch):
                b = st[name]

                def body(i, j):
                    bank = (b + j) % 4
                    y = 4 * i + ((3 * l + branch) * KC + j)
                    dve.wait_ge(sig_done, y + 1)
                    dve.wait_ge(gated, y)
                    dve.tensor_tensor(SZ[:, 0, t0:], SG[:, j % 2, t0:], PS[:, bank, 0:n], ALU.mult).then_inc(bank_read[bank], 1)
                    dve.wait_ge(bank_read[bank], i + (earlier(b + j) + 1))
                    yb = YB[:, bass.ds(4 * i + j, 1), t0:]
                    dve.tensor_tensor(yb, yb, SZ[:, 0:1, t0:], ALU.mult).then_inc(gated, 1)
                    next_low(b, i, j)
                    dve.wait_ge(yhi, y + 1)
                    dve.tensor_tensor(Y2[:, 1, bass.ds(4 * i + j, 1), t0:], yb,
                                      Y2[:, 0, bass.ds(4 * i + j, 1), t0:].bitcast(f32), ALU.subtract).then_inc(y_done, 1)

                looped(dve, b, 8, 4, body)

            def merge(name, branch):
                b = st[name]

                def body(i, j):
                    bank = (b + j) % 4
                    if j % 2:
                        done(b, i, j)
                        m = 2 * i + ((2 * l + branch - 1) * KC + j // 2)
                        before = (b + j - 1) % 4
                        dve.wait_ge(bank_read[before], i + (earlier(b + j - 1) + 1))
                        acc = ACC[:, bass.ds(2 * i + j // 2, 1), t0:]
                        if branch == 0:
                            dve.tensor_tensor(acc, SG[:, j // 2:j // 2 + 1, t0:], PS[:, bank:bank + 1, 0:n],
                                              ALU.mult).then_inc(bank_read[bank], 1)
                        else:
                            dve.wait_ge(acc_done, m)
                            dve.tensor_tensor(SZ[:, 0, t0:], SG[:, j // 2, t0:], PS[:, bank, 0:n],
                                              ALU.mult).then_inc(bank_read[bank], 1)
                            dve.wait_ge(bank_read[bank], i + (earlier(b + j) + 1))
                            dve.tensor_tensor(acc, acc, SZ[:, 0:1, t0:], ALU.add).then_inc(acc_done, 1)
                    next_low(b, i, j)

                looped(dve, b, 16, 4, body)

            z_gate("az", 0)
            merge("amerge", 0)
            lows("bq")
            lows("bk")
            cos, sin = const("axcos", T), const("axsin", T)

            def rotated(x):
                src = (YB if x < 8 else KB)[:, x % 8, T:]
                dve.wait_ge(prot, 16 * l + x + 1)
                dve.tensor_tensor(TS[:, x % 2, :], PS[:, 6 + x % 2, 0:T], sin, ALU.mult).then_inc(psin, 1)
                dve.wait_ge(psin, 16 * l + x + 1)
                dve.tensor_tensor(src, TC[:, x % 2, :], TS[:, x % 2, :], ALU.add).then_inc(p_done, 1)

            for x in range(16):
                a = t0 if x < 8 else 0
                whole = (YB if x < 8 else KB)[:, x % 8, a:]
                at = PAR2["qn" if x < 8 else "kn"]
                dve.wait_ge(prx, 16 * l + x + 1)
                refine(RB[:, x % 2, a:], VP[:, x % 2, a:])
                dve.scalar_tensor_tensor(whole, whole, P2[:, l, at:at + 1], RB[:, x % 2, a:], ALU.mult,
                                         ALU.mult).then_inc(pscaled, 1)
                dve.wait_ge(pscaled, 16 * l + x + 1)
                if x >= 2:
                    dve.wait_ge(p_done, 16 * l + x - 1)
                chain(dve.tensor_tensor(TC[:, x % 2, :], (YB if x < 8 else KB)[:, x % 8, T:], cos, ALU.mult))
                if x:
                    rotated(x - 1)
            chain.wait()
            rotated(15)
            lows("bv")
            steps, tb = tiles(l), tile_base(l)

            def top(f):
                h, q = steps[f]
                keys = 2 * T if q >= 2 else T
                c = f % 2
                dve.wait_ge(s2, tb + f + 1)
                chain(dve.reduce_max(BC[:, c, 0:2], PS[:, 2 * c:2 * c + 2, 0:keys], AX.X))
                chain.wait()
                dve.tensor_scalar(BC[:, c, 2:4], BC[:, c, 0:2], -0.125, None, ALU.mult).then_inc(mx2, 1)

            top(0)
            for f in range(len(steps)):
                if f + 1 < len(steps):
                    top(f + 1)
                h, q = steps[f]
                keys = 2 * T if q >= 2 else T
                c = f % 2
                dve.wait_ge(ex2, tb + f + 1)
                chain(dve.reciprocal(BC[:, c, 4:6], BC[:, c, 4:6]))
                chain.wait()
                chain(dve.tensor_tensor(BC[:, c, 5:6], BC[:, c, 5:6], LM[:, 4 + l:5 + l], ALU.mult))
                chain(dve.tensor_scalar(PB[:, c, 0, 0:keys], PB[:, c, 0, 0:keys], BC[:, c, 4:5], None, ALU.mult))
                chain.wait()
                dve.scalar_tensor_tensor(PB[:, c, 0, 0:keys], PB[:, c, 1, 0:keys], BC[:, c, 5:6],
                                         PB[:, c, 0, 0:keys], ALU.mult, ALU.add).then_inc(w2, 1)
            norm_groups(4, 8, 1, lambda k: LM[:, 6 + l:7 + l])
            dve.wait_ge(gnorm, 12 * l + 12)
            z_gate("bz", 1)
            merge("bmerge", 1)
            lows("cu")
            for p in parts(l):
                past = 8 * (p if l == 0 else 2)
                for x in range(8):
                    dve.wait_ge(f2, past + x + 1)
                    dve.tensor_copy(YB[:, x, p * T:(p + 1) * T], PS[:, 6 + x % 2, 0:T]).then_inc(f2_read, 1)
            dve.wait_ge(f2_read, 16 + 8 * l)
            z_gate("cz", 2)
            merge("cmerge", 2)
            for k in range(KC):
                dve.wait_ge(ahi, l * KC + k + 1)
                dve.tensor_tensor(H2[:, 1, k, t0:], ACC[:, k, t0:], H2[:, 0, k, t0:].bitcast(f32),
                                  ALU.subtract).then_inc(a_done, 1)
            b = st["out"]

            def residual(i, j):
                done(b, i, j)
                bank = (b + j) % 4
                for p in parts(l):
                    x = XX[:, bass.ds(4 * i + j, 1), p * T:(p + 1) * T]
                    ins = dve.scalar_tensor_tensor(x, PS[:, bank:bank + 1, p * T - t0:(p + 1) * T - t0],
                                                   M2[:, l, bass.ds(4 * i + (16 + j), 1), 1 - p], x, ALU.mult, ALU.add)
                ins.then_inc(bank_read[bank], 1)
                next_low(b, i, j)

            if l == DEPTH - 1:
                for i in range(2):
                    for j in range(4):
                        residual(i, j)
            else:
                looped(dve, b, 8, 4, residual)

        for i in range(2):
            chain(dve.tensor_tensor(LT[:, i, :, :], LAM[:, :, 2 * i, :], LAM[:, :, 2 * i + 1, :], ALU.mult))
        chain.wait()
        dve.tensor_reduce(LR[:, :, :], LT, AX.X, ALU.add).then_inc(lam_r, 1)
        dve.wait_ge(lam_e, 1)
        chain(dve.tensor_tensor(LM[:, 4:6], LM[:, 2:4], LM[:, 0:2], ALU.subtract))
        chain.wait()
        for l in range(DEPTH):
            start = 0.8 - 0.6 * float(np.exp(-0.3 * l))
            chain(dve.tensor_scalar(LM[:, 4 + l:5 + l], LM[:, 4 + l:5 + l], -start, None, ALU.add))
            at = PAR2["subln"]
            chain(dve.tensor_scalar(LM[:, 6 + l:7 + l], P2[:, l, at:at + 1], 1.0 - start, None, ALU.mult))
        chain.wait()
        dve.wait_ge(consts2_in, 16)
        for l in range(DEPTH):
            layer(l)

    def finish(sp):
        for k in range(KC):
            u = stages(DEPTH - 1)["out"] + k
            sp.wait_ge(bank_read[u % 4], earlier(u) + 1)
        sp.dma_start(outT, X).then_inc(out_done, 16)
        sp.wait_ge(out_done, 16)

    @block.sync
    def _(sp):
        def modulation(q, i=0, step=4):
            used = q - 4
            if used >= EARLY + MOD2 + DEPTH * MOD1 - EARLY:
                sp.wait_ge(wide_used, step * i + (used - DEPTH * MOD1 + 1))
            elif used >= EARLY + MOD2 - 1:
                sp.wait_ge(mod_used, step * i + (used - MOD2 + 1))
            elif used >= EARLY:
                sp.wait_ge(wide_used, step * i + (used - EARLY + 1))
            elif used >= 0:
                sp.wait_ge(mod_used, step * i + (used + 1))
            sp.dma_start(GRING[:, q % 4, :, :], mods[step * i + q]).then_inc(mod_full[q % 4], 16)

        def modulations(first, end):
            with sp.Fori(0, (end - first) // 4) as i:
                for q in range(first, first + 4):
                    modulation(q, i)
            for q in range(first + (end - first) // 4 * 4, end):
                modulation(q)

        def unit(v, i=0):
            for half in range(2):
                g = 2 * v + half
                if g >= 4:
                    sp.wait_ge(lo_done, 8 * i + (g - 3))
                cut = slice(half * KC // 2, (half + 1) * KC // 2)
                sp.dma_start(RAW[:, g % 4, :, :], stream[4 * i + v, :, cut, :]).then_inc(raw_full[g % 4], 16)

        def units(first, end, beside=None):
            with sp.Fori(0, (end - first) // 4) as i:
                for j in range(4):
                    unit(first + j, i)
                    if beside is not None:
                        modulation(beside + j, i)

        sp.dma_start(CC[:, :, :], ccols).then_inc(c_in, 16)
        for q in range(4):
            modulation(q)
        for dst, src in ((X, xT), (P1[:, :, :], par1), (C[:, 0:COMMON_W + FIRST_W], consts)):
            sp.dma_start(dst, src).then_inc(consts_in, 16)
        for v in range(4):
            unit(v)
        modulations(4, 16 + 3)
        sp.dma_start(P2[:, :, :], par2).then_inc(later_in, 16)
        u = 4 + V_UNITS
        units(4, u)
        units(u, u + QK_UNITS, 16 + 3)
        modulation(EARLY + 3)
        modulations(EARLY + 4, EARLY + MOD2 + 3)
        u, q = u + QK_UNITS, EARLY + MOD2 + 3
        sp.wait_ge(wide_used, MOD2)
        for n in (WO_UNITS, FF_MODS):
            units(u, u + n, q)
            u, q = u + n, q + n
        units(u, u + FF_UNITS - FF_MODS)
        u += FF_UNITS - FF_MODS
        units(u, u + DOWN_UNITS, q)
        u, q = u + DOWN_UNITS, q + DOWN_UNITS
        units(u, u + V_UNITS + QK_UNITS)
        u += V_UNITS + QK_UNITS
        modulation(q)
        modulations(q + 1, MOD_UNITS)
        sp.wait_ge(mod_used, DEPTH * MOD1)
        sp.dma_start(XX[:, :, 0:T], ctxT).then_inc(later_in, 16)
        sp.wait_ge(wide_used, DEPTH * MOD2)
        sp.dma_start(LAM, lam).then_inc(later_in, 16)
        units(u, total)
        finish(sp)

    @block.gpsimd
    def _(pool):
        def rope(l):
            cos = const("cos", T)[:, None, :].broadcast_to([P, 2, T])
            if l == 0:
                pool.wait_ge(consts_in, 16 * 3)
            for g in range(6):
                pool.wait_ge(rms_done, 9 * l + max(1, min(9, 2 * g - 1)))
                pool.tensor_tensor(RO[:, 2 * g:2 * g + 2, :], F[:, 2 * g:2 * g + 2, :], cos,
                                   ALU.mult).then_inc(cosd, 1)

        for l in range(DEPTH):
            rope(l)
        pool.wait_ge(o_ready, 4 * DEPTH)
        pool.dma_start(C[:, COMMON_W:COMMON_W + SECOND_W], consts2).then_inc(consts2_in, 16)

    @block.tensor
    def _(pe):
        def modulate(n):
            q = EARLY + n if n < MOD2 else EARLY + MOD2 + DEPTH * MOD1 - EARLY + n - MOD2
            pe.wait_ge(mod_full[q % 4], 16 * (q // 4 + 1))
            for k in range(KC):
                last = pe.matmul(PS[:, 7, 2 * n:2 * n + 2], GRING[:, q % 4, k, :], CA[:, 1:3, k],
                                 start=(k == 0), stop=(k == KC - 1))
            last.then_inc(wide_used, 1)

        def unit_wait(base, i, j):
            u = base + j
            pe.wait_ge(lo_done, 8 * i + 2 * (u + 1))
            if u >= 4:
                pe.wait_ge(bank_read[u % 4], i + earlier(u))
            return u

        def feature_unit(base, i, j, moving, n):
            u = unit_wait(base, i, j)
            for k in range(KC):
                out = PS[:, u % 4, 0:n]
                pe.matmul(out, WH[:, u % 4, k, :], moving[:, 0, k, :], start=(k == 0), stop=False)
                pe.matmul(out, WH[:, u % 4, k, :], moving[:, 1, k, :], start=False, stop=False)
                last = pe.matmul(out, WL[:, u % 4, k, :], moving[:, 0, k, :], start=False, stop=(k == KC - 1))
            last.then_inc(unit_done, 1)

        def token_pair(base, i, j, still, first, end):
            u, half = base + j, (end - first) // 2
            pe.wait_ge(lo_done, 8 * i + 2 * (u + 2))
            for x in (u, u + 1):
                if x >= 4:
                    pe.wait_ge(bank_read[x % 4], i + earlier(x))
            for b in range(end - first):
                at = (b % half) * 2 * P
                out = PS[:, (u + b // half) % 4, at:at + 2 * P].rearrange("p (a c) -> p a c", a=2)
                cut = slice((first + b) * P, (first + b + 1) * P)
                both = slice(u % 4, u % 4 + 2)
                for k in range(KC):
                    pe.matmul(out, still[:, 0, k, cut], WH[:, both, k, :], start=(k == 0), stop=False)
                    pe.matmul(out, still[:, 0, k, cut], WL[:, both, k, :], start=False, stop=False)
                    last = pe.matmul(out, still[:, 1, k, cut], WH[:, both, k, :], start=False,
                                     stop=(k == KC - 1))
            last.then_inc(unit_done, 2)

        def down_unit(base, i, j):
            u, b = base + j, j // 3
            pe.wait_ge(lo_done, 24 * i + 2 * (u + 1))
            if j % 3 == 0:
                pe.wait_ge(bank_read[b], i + earlier(base))
            for k in range(KC if j % 3 < 2 else FC - 2 * KC):
                kk = (j % 3) * KC + k
                pe.matmul(PS[:, b, 0:T], WH[:, u % 4, k, :], HID[:, 0, kk, :], start=(kk == 0), stop=False)
                pe.matmul(PS[:, b, 0:T], WH[:, u % 4, k, :], HID[:, 1, kk, :], start=False, stop=False)
                last = pe.matmul(PS[:, b, 0:T], WL[:, u % 4, k, :], HID[:, 0, kk, :], start=False,
                                 stop=(kk == FC - 1))
            last.then_inc(unit_done, 1)

        second = second_pe(pe, feature_unit, token_pair)

        def first_layer(l):
            base = l * PER
            def norm_sums(half):
                for k in range(KC):
                    pe.wait_ge(sq_done, (2 * l + half) * KC + k + 1)
                    last = pe.matmul(PS[:, 6, 0:T], ones, SQ[:, k, :], start=(k == 0), stop=(k == KC - 1))
                last.then_inc(sum_done, 1)

            norm_sums(0)
            pe.wait_ge(norm_done, (2 * l + 1) * KC)
            for j in range(0, V_UNITS, 2):
                token_pair(base, 0, j, H1, 0, 2)
            b = base + V_UNITS
            looped(pe, b, QK_UNITS, 4, lambda i, j: feature_unit(b, i, j, H1, T))
            for g in range(5):
                pe.wait_ge(rsq_done, 5 * l + g + 1)
                if g >= 2:
                    pe.wait_ge(mr_done, 5 * l + g - 1)
                n = T if g == 4 else 2 * T
                pe.matmul(PS[:, 4 + g % 2, 0:n], heads, TMP[:, 2 * g:2 * g + n // T, :],
                          start=True, stop=True).then_inc(ms_done, 1)
            for g in range(6):
                pe.wait_ge(rms_done, 9 * l + max(1, min(9, 2 * g - 1)))
                if g >= 2:
                    pe.wait_ge(rot_read, 6 * l + g - 1)
                else:
                    pe.wait_ge(mr_done, 5 * l + 5)
                pe.matmul(PS[:, 4 + g % 2, 0:2 * T], const("rot"), F[:, 2 * g:2 * g + 2, :],
                          start=True, stop=True).then_inc(rot_done, 1)
            pe.wait_ge(rope_done, 6 * (l + 1))

            def score(s):
                n = s % 2
                w = P * (n + 1)
                if s >= 2:
                    pe.wait_ge(scores_read, 10 * l + s - 1)
                for p, h in enumerate(PLACE):
                    if s < 2:
                        q, k = h // 2, 2
                    elif s < 4:
                        q, k = 3 + h // 2, 5
                    elif s < 8:
                        g = (s - 4) // 2
                        q, k = 6 + 2 * g + h // 2, 10 + g
                    else:
                        q, k = 12 + h // 2, 14 + h // 2
                    r = slice(64 * (h % 2), 64 * (h % 2) + 64)
                    out = PS[:, 2 * (s % 2):2 * (s % 2) + 2, :].rearrange("p a (b t) -> p (a b) t", b=2)[:, p, 0:w]
                    last = pe.matmul(out, F[r, q, n * P:(n + 1) * P], F[r, k, 0:w], start=True, stop=True)
                last.then_inc(scores, 1)

            def turn(s):
                a = s - 2
                n = a % 2
                if s < 8:
                    pe.wait_ge(probs, 6 * l + a + 1)
                else:
                    pe.wait_ge(sticks, 2 * l + s - 8 + 1)
                if a:
                    pe.wait_ge(pt_ready, 8 * l + a)
                for kb in range(n + 1):
                    for h in range(4):
                        last = pe.transpose(PS[:, 4 + kb, h * P:(h + 1) * P],
                                            PR[:, s % 2, h, kb * P:(kb + 1) * P], ident)
                last.then_inc(turned, 1)

            def weigh(g):
                pe.wait_ge(pt_ready, 8 * l + 2 * g + 2)
                if g:
                    pe.wait_ge(o_ready, 4 * l + g)
                for p, h in sorted(enumerate(PLACE), key=lambda x: x[1]):
                    at = (0, 320, 384, 64 + h * 64)[g]
                    rows = slice(64 * (h % 2), 64 * (h % 2) + 64)
                    out = PS[rows, 6, (h // 2) * T:(h // 2 + 1) * T]
                    pe.matmul(out, V[:, 0, at:at + 64], PT[:, g % 2, 0:2, p, :], start=True, stop=False)
                    last = pe.matmul(out[:, P:T], V[:, 1, at:at + 64], PT[:, g % 2, 2, p, :],
                                     start=False, stop=True)
                last.then_inc(pv_done, 1)

            score(0)
            score(1)
            score(2)
            score(3)
            for s in range(2, 10):
                for m in range((s - 2) * MOD2 // 8, (s - 1) * MOD2 // 8):
                    modulate(l * MOD2 + m)
                turn(s)
                if s + 2 < 10:
                    score(s + 2)
                if s % 2:
                    weigh((s - 2) // 2)
            for g in range(4):
                pe.wait_ge(osq, 4 * l + g + 1)
                pe.matmul(PS[:, g, 0:2 * T], heads, SQ[:, 2 * g:2 * g + 2, :], start=True, stop=True).then_inc(oms, 1)
            pe.wait_ge(olo, (l + 1) * KC)
            b = base + V_UNITS + QK_UNITS
            looped(pe, b, WO_UNITS, 4, lambda i, j: feature_unit(b, i, j, OS, T))
            norm_sums(1)
            pe.wait_ge(norm_done, (2 * l + 2) * KC)
            b2 = b + WO_UNITS

            looped(pe, b2, FF_UNITS, 4, lambda i, j: feature_unit(b2, i, j, H1, T))
            pe.wait_ge(ff_done, (l + 1) * FC)
            b3 = b2 + FF_UNITS
            looped(pe, b3, DOWN_UNITS, 12, lambda i, j: down_unit(b3, i, j))

        pe.wait_ge(cact, 1)
        pe.wait_ge(consts_in, 16 * 3)
        for k in range(KC):
            last = pe.matmul(PS[:, 4 + k // 4, (k % 4) * P:(k % 4 + 1) * P], CA[:, 0, k:k + 1].broadcast_to([P, P]),
                             ident, start=True, stop=True)
        last.then_inc(spread, 1)
        for l in range(DEPTH):
            first_layer(l)
        for l in range(DEPTH):
            second(l)

    @block.scalar
    def _(act):
        chain = Chain(act, act_chain)

        def split_high(u, i, rounds):
            for half in range(2):
                g = 2 * u + half
                cut = slice(half * KC // 2, (half + 1) * KC // 2)
                act.wait_ge(raw_full[g % 4], 32 * rounds * i + 16 * (g // 4 + 1))
                act.activation(WH[:, u % 4, cut, :], RAW[:, g % 4, :, :], ACT.Copy).then_inc(hi_done, 1)

        def next_high(base, i, j, rounds=1):
            act.wait_ge(unit_done, 4 * rounds * i + (base + j + 1))
            if isinstance(i, int) and 4 * rounds * i + base + j + 4 >= total:
                return
            split_high(base + j + 4, i, rounds)

        def done(base, i, j, rounds=1):
            act.wait_ge(unit_done, 4 * rounds * i + (base + j + 1))

        def exponentials():
            act.preload_act_table_set("natural_log_exp_and_others")

        def sigmoids():
            act.preload_act_table(ACT.Sigmoid)

        def inverse_root(y, v, sums, scale, read, done):
            ins = act.activation(v, sums, ACT.Identity, bias=EPSC[:, 0:1], scale=scale)
            if read is None:
                chain(ins)
                chain.wait()
            else:
                ins.then_inc(read[0], 1)
                act.wait_ge(read[0], read[1])
            chain(act.activation(y, v, ACT.Ln))
            chain.wait()
            act.activation(y, y, ACT.Exp, scale=-0.5).then_inc(done, 1)

        def norm(l, half):
            for k in range(KC):
                if half:
                    act.wait_ge(bank_read[k % 4], earlier(l * PER + V_UNITS + QK_UNITS + k) + 1)
                elif l:
                    act.wait_ge(bank_read[k % 4], earlier(l * PER - DOWN_UNITS) + k // 4 + 1)
                act.activation(SQ[:, k, :], X[:, k, :], ACT.Square).then_inc(sq_done, 1)
            act.wait_ge(sum_done, 2 * l + half + 1)
            inverse_root(RS[:, 1, :], RS[:, 0, :], PS[:, 6, 0:T], 1.0 / D, None, rstd_done)
            for k in range(KC):
                act.wait_ge(nx_done, (2 * l + half) * KC + k + 1)
                at = 24 * half + k
                act.activation(H1[:, 0, k, :], NX[:, k % 4, :], ACT.Identity,
                               bias=M1[:, l, at:at + 1]).then_inc(nhi_done, 1)

        def first_layer(l):
            base = l * PER
            norm(l, 0)

            for j in range(V_UNITS):
                done(base, 0, j)
                act.activation(V[:, j % 2, (j // 2) * 2 * P:(j // 2 + 1) * 2 * P], PS[:, j, 0:2 * P],
                               ACT.Copy).then_inc(bank_read[j], 1)
                next_high(base, 0, j)
            b = base + V_UNITS

            def features(i, j):
                done(b, i, j)
                act.activation(F[:, bass.ds(4 * i + j, 1), :], PS[:, j:j + 1, 0:T],
                               ACT.Copy).then_inc(bank_read[j], 1)
                next_high(b, i, j)

            looped(act, b, QK_UNITS, 4, features)
            for j in range(4):
                act.wait_ge(bank_read[j], earlier(b + QK_UNITS + j))
            for g in range(5):
                n = 1 if g == 4 else 2
                act.activation(TMP[:, 2 * g:2 * g + n, :], F[:, 3 + 2 * g:3 + 2 * g + n, :],
                               ACT.Square).then_inc(rsq_done, 1)
            for g in range(5):
                n = 1 if g == 4 else 2
                act.wait_ge(ms_done, 5 * l + g + 1)
                inverse_root(TMP[:, 2 * g:2 * g + n, :], VM[:, 2 * g:2 * g + n, :],
                             PS[:, 4 + g % 2, 0:n * T].rearrange("p (a b) -> p a b", a=n), 1.0 / 64,
                             (mr_done, 5 * l + g + 1), rx_done)

            def stats(s):
                return 8 + 16 * (s % 2)

            def exps(s):
                a, w = s - 2, P * (s % 2 + 1)
                if a >= 2:
                    act.wait_ge(turned, 8 * l + a - 1)
                if s < 8:
                    act.wait_ge(masked, 6 * l + a + 1)
                    c = stats(s)
                    if s >= 4:
                        act.activation(COL[:, 40 + 4 * (s % 2):44 + 4 * (s % 2)],
                                       COL[:, 48 + 4 * (s % 2):52 + 4 * (s % 2)], ACT.Exp)
                    for h in range(4):
                        last = act.activation(PR[:, s % 2, h, 0:w], SM[:, s % 2, h, 0:w], ACT.Exp,
                                              bias=COL[:, c + 4 + h:c + 5 + h], scale=0.125,
                                              accum_out=COL[:, c + 8 + h:c + 9 + h])
                    last.then_inc(exped, 1)
                else:
                    act.wait_ge(scores_read, 10 * l + s + 1)
                    dst = PR[:, s % 2, :, 0:w]
                    chain(act.activation(dst, SM[:, s % 2, :, 0:w], ACT.Abs))
                    chain.wait()
                    chain(act.activation(dst, dst, ACT.Exp, scale=-1.0))
                    chain.wait()
                    act.activation(dst, dst, ACT.Ln, bias=EPSC[:, 1:2]).then_inc(bl, 1)

            exps(2)
            for s in range(2, 10):
                a, g, n = s - 2, (s - 2) // 2, s % 2
                w = P * (n + 1)
                if s + 1 < 10:
                    exps(s + 1)
                if s >= 8:
                    act.wait_ge(bq, 2 * l + s - 8 + 1)
                    act.activation(PR[:, n, :, 0:w], SM[:, n, :, 0:w], ACT.Exp).then_inc(sticks, 1)
                act.wait_ge(turned, 8 * l + a + 1)
                if g >= 2:
                    act.wait_ge(pv_done, 4 * l + g - 1)
                if n == 0:
                    act.activation(PT[:, g % 2, 0, :, :], PS[:, 4, :].rearrange("p (a b) -> p a b", a=4),
                                   ACT.Copy).then_inc(pt_ready, 1)
                else:
                    act.activation(PT[:, g % 2, 1:3, :, :],
                                   PS[:, 4:6, :].rearrange("p k (a b) -> p k a b", a=4),
                                   ACT.Copy).then_inc(pt_ready, 1)
                    o = (0, 4, 6, 2)[g]
                    act.wait_ge(pv_done, 4 * l + g + 1)
                    act.activation(O[:, o:o + 2, :], PS[:, 6, :].rearrange("p (a b) -> p a b", a=2),
                                   ACT.Copy).then_inc(o_ready, 1)
            act.wait_ge(o_ready, 4 * l + 4)
            for g in range(4):
                act.activation(SQ[:, 2 * g:2 * g + 2, :], O[:, 2 * g:2 * g + 2, :], ACT.Square).then_inc(osq, 1)
            for g in range(4):
                act.wait_ge(oms, 4 * l + g + 1)
                inverse_root(RSO[:, 2 * g:2 * g + 2, :], VO[:, 2 * g:2 * g + 2, :],
                             PS[:, g, :].rearrange("p (a b) -> p a b", a=2), 1.0 / 64, None, orr)
            for k in range(KC):
                act.wait_ge(ohf, l * KC + k + 1)
                act.activation(OS[:, 0, k, :], GATE[:, k % 4, :], ACT.Copy).then_inc(ohi, 1)
            b = b + QK_UNITS
            looped(act, b, WO_UNITS, 4, lambda i, j: next_high(b, i, j))
            norm(l, 1)
            b2 = b + WO_UNITS

            def hidden(i, j):
                done(b2, i, j)
                if j % 2 == 0:
                    act.activation(GATE[:, 0, :], PS[:, j, 0:T], ACT.Sigmoid).then_inc(ffsig, 1)
                    next_high(b2, i, j)
                else:
                    next_high(b2, i, j)
                    act.wait_ge(bank_read[j], i + (earlier(b2 + j) + 1))
                    act.activation(HID[:, 0, bass.ds(2 * i + j // 2, 1), :], GATE[:, 2:3, :],
                                   ACT.Copy).then_inc(ffhi, 1)

            sigmoids()
            looped(act, b2, FF_UNITS, 4, hidden)
            exponentials()
            b3 = b2 + FF_UNITS
            looped(act, b3, DOWN_UNITS, 12, lambda i, j: next_high(b3, i, j, 3))

        exponentials()
        act.wait_ge(c_in, 16)
        act.activation(CT[:, 0, :, :], CC[:, :, :], ACT.Exp, scale=-1.0).then_inc(cexp, 1)
        act.wait_ge(cexp, 2)
        for u in range(4):
            split_high(u, 0, 1)
        act.wait_ge(consts_in, 16 * 3)
        for l in range(DEPTH):
            first_layer(l)
        act.wait_ge(later_in, 16 * 3)
        second_act(act, done, next_high, exponentials, sigmoids, inverse_root, chain)

    @block.vector
    def _(dve):
        chain = Chain(dve, dve_chain)

        def split_low(u, i, rounds):
            for half in range(2):
                g = 2 * u + half
                cut = slice(half * KC // 2, (half + 1) * KC // 2)
                dve.wait_ge(hi_done, 8 * rounds * i + (g + 1))
                dve.tensor_tensor(WL[:, u % 4, cut, :], RAW[:, g % 4, :, :], WH[:, u % 4, cut, :].bitcast(f32),
                                  ALU.subtract).then_inc(lo_done, 1)

        def next_low(base, i, j, rounds=1):
            if isinstance(i, int) and 4 * rounds * i + base + j + 4 >= total:
                return
            split_low(base + j + 4, i, rounds)

        def done(base, i, j, rounds=1):
            dve.wait_ge(unit_done, 4 * rounds * i + (base + j + 1))

        def refine(y, v):
            chain(dve.tensor_tensor(v, v, y, ALU.mult))
            chain.wait()
            chain(dve.scalar_tensor_tensor(v, v, -0.5, y, ALU.mult, ALU.mult))
            chain.wait()
            chain(dve.scalar_tensor_tensor(y, v, 1.5, y, ALU.add, ALU.mult))
            chain.wait()

        def norm(l, half):
            dve.wait_ge(rstd_done, 2 * l + half + 1)
            refine(RS[:, 1, :], RS[:, 0, :])

            def low(k):
                dve.wait_ge(nhi_done, (2 * l + half) * KC + k + 1)
                at = 24 * half + k
                dve.scalar_tensor_tensor(H1[:, 1, k, :], NX[:, k % 4, :], M1[:, l, at:at + 1],
                                         H1[:, 0, k, :].bitcast(f32), ALU.add, ALU.subtract).then_inc(norm_done, 1)

            for k in range(KC):
                if k >= 4:
                    dve.wait_ge(norm_done, (2 * l + half) * KC + k - 3)
                dve.scalar_tensor_tensor(NX[:, k % 4, :], X[:, k, :], A1[:, l, half, k:k + 1], RS[:, 1, :],
                                         ALU.mult, ALU.mult).then_inc(nx_done, 1)
                if k >= 2:
                    low(k - 2)
            low(KC - 2)
            low(KC - 1)

        def modulate(q, i=0, step=4):
            m = q if q < EARLY else q + MOD2
            dve.wait_ge(mod_full[m % 4], 4 * step * i + 16 * (m // 4 + 1))
            for p in range(SUMS):
                w = GRING[:, m % 4, p, :]
                last = dve.scalar_tensor_tensor(w, w, 1.0, CB[:, p // 2, p % 2 * P:(p % 2 + 1) * P], ALU.mult, ALU.mult,
                                                accum_out=MV[:, bass.ds(step * i + q, 1), p])
            last.then_inc(mod_used, 1)

        def columns(l, at, n):
            q = l * MOD1 + at
            dve.wait_ge(mod_used, q + n)
            bias = PAR1["bmod"] + at
            chain(dve.tensor_reduce(M1[:, l, at:at + n], MV[:, q:q + n, :], AX.X, ALU.add))
            chain.wait()
            chain(dve.tensor_tensor(M1[:, l, at:at + n], M1[:, l, at:at + n], P1[:, l, bias:bias + n], ALU.add))
            chain.wait()
            for half in range(2):
                s = 24 * half + KC
                if at <= s and s + KC <= at + n:
                    g = PAR1["ln2" if half else "ln1"]
                    chain(dve.scalar_tensor_tensor(A1[:, l, half, :], M1[:, l, s:s + KC], 1.0,
                                                   P1[:, l, g:g + KC], ALU.add, ALU.mult))
                    chain.wait()

        def columns2():
            dve.wait_ge(wide_used, DEPTH * MOD2)
            for c in range(2):
                ins = dve.tensor_tensor(M2[:, :, :, c],
                                        PS[:, 7, 0:DEPTH * MOD2 * 2].rearrange("p (l m c) -> p l m c", l=DEPTH, c=2)[:, :, :, c],
                                        P2[:, :, PAR2["bada"]:PAR2["bada"] + MOD2], ALU.add)
            ins.then_inc(mod_read, 1)
            dve.wait_ge(mod_read, 1)
            for c in range(2):
                chain(dve.scalar_tensor_tensor(A2[:, :, :, c], M2[:, :, KC:2 * KC, c], 1.0,
                                               P2[:, :, PAR2["norm"]:PAR2["norm"] + KC], ALU.add, ALU.mult))
            chain.wait()

        def first_layer(l):
            base = l * PER
            norm(l, 0)
            for j in range(V_UNITS):
                next_low(base, 0, j)
            b = base + V_UNITS

            def beside(i, j):
                if l == 0:
                    modulate(16 + j, i)
                next_low(b, i, j)

            looped(dve, b, QK_UNITS, 4, beside)
            if l == 0:
                columns(0, 16, 16)
            for j in range(4):
                dve.wait_ge(bank_read[j], earlier(b + QK_UNITS + j))
            for n in range(2):
                chain(dve.tensor_scalar(COL[:, 4 * n:4 * n + 4], V[:, n, 448:452], 1.0 / 16, None, ALU.mult))
            for c in range(9):
                if c % 2 == 0:
                    n = 1 if c == 8 else 2
                    dve.wait_ge(rx_done, 5 * l + c // 2 + 1)
                    refine(TMP[:, c:c + n, :], VM[:, c:c + n, :])
                g = PAR1["gain"] + c
                dve.scalar_tensor_tensor(F[:, 3 + c, :], F[:, 3 + c, :], P1[:, l, g:g + 1], TMP[:, c, :],
                                         ALU.mult, ALU.mult).then_inc(rms_done, 1)
            sin = const("sin", T)[:, None, :].broadcast_to([P, 2, T])
            for g in range(6):
                dve.wait_ge(rot_done, 6 * l + g + 1)
                dve.tensor_tensor(SN[:, g % 2, :, :], PS[:, 4 + g % 2, :].rearrange("p (a b) -> p a b", a=2),
                                  sin, ALU.mult).then_inc(rot_read, 1)
                dve.wait_ge(rot_read, 6 * l + g + 1)
                dve.wait_ge(cosd, 6 * l + g + 1)
                dve.tensor_tensor(F[:, 2 * g:2 * g + 2, :], RO[:, 2 * g:2 * g + 2, :], SN[:, g % 2, :, :],
                                  ALU.add).then_inc(rope_done, 1)

            def banks(s):
                return PS[:, 2 * (s % 2):2 * (s % 2) + 2, :].rearrange("p a (b t) -> p (a b) t", b=2)

            dve.wait_ge(rope_done, 6 * l + 6)
            for n in range(2):
                w = P * (n + 1)
                dve.wait_ge(scores, 10 * l + n + 1)
                for p, h in enumerate(PLACE):
                    ins = dve.tensor_scalar(SM[:, n, p, 0:w], banks(n)[:, p, 0:w], 0.0,
                                            COL[:, 4 * n + h:4 * n + h + 1], ALU.max, ALU.mult)
                ins.then_inc(scores_read, 1)
                dve.wait_ge(scores_read, 10 * l + n + 1)
                chain(dve.tensor_reduce(WK[:, n, 0:w], SM[:, n, :, 0:w].rearrange("p h t -> p t h"),
                                        AX.X, ALU.add))
            chain.wait()
            causal = const("causal", 2 * T).rearrange("p (n t) -> p n t", n=2)
            for n in range(2):
                w = P * (n + 1)
                chain(dve.tensor_tensor(WK[:, n, 0:w], WK[:, n, 0:w], causal[:, n, 0:w], ALU.add))
            for r in range(TOPK // 8):
                chain.wait()
                for n in range(2):
                    chain(dve.max(COL[:, 40 + 8 * n:48 + 8 * n], WK[:, n, 0:P * (n + 1)]))
                chain.wait()
                for n in range(2):
                    w = P * (n + 1)
                    chain(dve.match_replace(WK[:, n, 0:w], COL[:, 40 + 8 * n:48 + 8 * n], WK[:, n, 0:w], GONE))
            chain.wait()
            for n in range(2):
                w = P * (n + 1)
                chain(dve.tensor_scalar(SEL[:, n, 0:w], WK[:, n, 0:w], GONE * 0.5, -BIG, ALU.is_gt, ALU.mult))
            chain.wait()
            for n in range(2):
                w = P * (n + 1)
                chain(dve.tensor_tensor(SEL[:, n, 0:w], SEL[:, n, 0:w], causal[:, n, 0:w], ALU.add))
            chain.wait()
            band = const("band", 2 * T).rearrange("p (n t) -> p n t", n=2)
            strict = const("strict", 2 * T).rearrange("p (n t) -> p n t", n=2)

            def begin(s):
                a, n = s - 2, s % 2
                w, c = P * (n + 1), 8 + 16 * n
                sm = SM[:, n, :, 0:w]
                dve.wait_ge(scores, 10 * l + s + 1)
                if s >= 8:
                    m = strict[:, n, 0:w][:, None, :].broadcast_to([P, 4, w])
                    dve.scalar_tensor_tensor(sm, banks(s)[:, :, 0:w], 0.125, m, ALU.mult, ALU.add).then_inc(scores_read, 1)
                    return
                m = (SEL if s < 4 else band)[:, n, 0:w][:, None, :].broadcast_to([P, 4, w])
                dve.tensor_tensor(sm, banks(s)[:, :, 0:w], m, ALU.add).then_inc(scores_read, 1)
                dve.wait_ge(scores_read, 10 * l + s + 1)
                chain(dve.reduce_max(COL[:, c:c + 4], sm, AX.X))
                chain.wait()
                if s < 4:
                    dve.tensor_scalar(COL[:, c + 4:c + 8], COL[:, c:c + 4], -0.125, None, ALU.mult).then_inc(masked, 1)
                else:
                    k = PAR1["sinks"] + 4 * ((s - 4) // 2)
                    sink = P1[:, l, k:k + 4]
                    chain(dve.scalar_tensor_tensor(COL[:, c:c + 4], COL[:, c:c + 4], 0.125, sink, ALU.mult, ALU.max))
                    chain.wait()
                    dve.tensor_scalar(COL[:, c + 4:c + 8], COL[:, c:c + 4], -1.0, None, ALU.mult)
                    dve.tensor_tensor(COL[:, 48 + 4 * n:52 + 4 * n], sink, COL[:, c:c + 4],
                                      ALU.subtract).then_inc(masked, 1)

            def end(s):
                a, n = s - 2, s % 2
                w, c = P * (n + 1), 8 + 16 * n
                if s < 8:
                    dve.wait_ge(exped, 6 * l + a + 1)
                    if s >= 4:
                        chain(dve.tensor_tensor(COL[:, c + 8:c + 12], COL[:, c + 8:c + 12],
                                                COL[:, 40 + 4 * n:44 + 4 * n], ALU.add))
                        chain.wait()
                    chain(dve.reciprocal(COL[:, c + 12:c + 16], COL[:, c + 8:c + 12]))
                    chain.wait()
                    r = COL[:, c + 12:c + 16][:, :, None].broadcast_to([P, 4, w])
                    dve.tensor_tensor(PR[:, n, :, 0:w], PR[:, n, :, 0:w], r, ALU.mult).then_inc(probs, 1)
                else:
                    dve.wait_ge(scores_read, 10 * l + s + 1)
                    dve.wait_ge(bq, 2 * l + s - 8)
                    chain(dve.tensor_scalar(STK[:, :, 0:w], SM[:, n, :, 0:w], 0.0, None, ALU.max))
                    dve.wait_ge(bl, 2 * l + s - 8 + 1)
                    chain.wait()
                    for h in range(4):
                        chain(dve.tensor_tensor_scan(STK[:, h, 0:w][:, ::-1], PR[:, n, h, 0:w][:, ::-1],
                                                     STK[:, h, 0:w][:, ::-1], 0.0, ALU.add, ALU.add))
                    chain.wait()
                    dve.tensor_tensor(SM[:, n, :, 0:w], SM[:, n, :, 0:w], STK[:, :, 0:w],
                                      ALU.subtract).then_inc(bq, 1)

            begin(2)
            for s in range(2, 10):
                if s + 1 < 10:
                    begin(s + 1)
                end(s)
            def low(k):
                dve.wait_ge(ohi, l * KC + k + 1)
                dve.tensor_tensor(OS[:, 1, k, :], GATE[:, k % 4, :], OS[:, 0, k, :].bitcast(f32),
                                  ALU.subtract).then_inc(olo, 1)

            for k in range(KC):
                if k % 2 == 0:
                    dve.wait_ge(orr, 4 * l + k // 2 + 1)
                    refine(RSO[:, k:k + 2, :], VO[:, k:k + 2, :])
                if k >= 4:
                    dve.wait_ge(olo, l * KC + k - 3)
                g = PAR1["gout"] + k
                dve.scalar_tensor_tensor(GATE[:, k % 4, :], O[:, k, :], P1[:, l, g:g + 1], RSO[:, k, :],
                                         ALU.mult, ALU.mult).then_inc(ohf, 1)
                if k >= 2:
                    low(k - 2)
            low(KC - 2)
            low(KC - 1)
            b = b + QK_UNITS

            def project(i, j):
                if l == 0:
                    modulate(EARLY + j, i)
                done(b, i, j)
                k = 4 * i + j
                dve.scalar_tensor_tensor(X[:, bass.ds(k, 1), :], PS[:, j:j + 1, 0:T],
                                         M1[:, l, bass.ds(16 + k, 1)], X[:, bass.ds(k, 1), :],
                                         ALU.mult, ALU.add).then_inc(bank_read[j], 1)
                next_low(b, i, j)

            looped(dve, b, WO_UNITS, 4, project)
            if l == 0:
                columns(0, EARLY, WO_UNITS)
            norm(l, 1)
            b2 = first = b + WO_UNITS

            def hidden(b2, i, j, mod=None):
                if mod is not None:
                    modulate(mod + j, i)
                if j % 2 == 0:
                    next_low(b2, i, j)
                else:
                    done(b2, i, j)
                    x = (b2 - first) // 2 + j // 2
                    m = 2 * i + (l * FC + x + 1)
                    dve.wait_ge(ff_done, m - 1)
                    dve.wait_ge(ffsig, m)
                    dve.tensor_tensor(GATE[:, 1, :], GATE[:, 0, :], PS[:, j - 1, 0:T], ALU.mult).then_inc(bank_read[j - 1], 1)
                    dve.wait_ge(bank_read[j - 1], i + (earlier(b2 + j - 1) + 1))
                    dve.tensor_tensor(GATE[:, 2, :], GATE[:, 1, :], PS[:, j, 0:T], ALU.mult).then_inc(bank_read[j], 1)
                    next_low(b2, i, j)
                    dve.wait_ge(ffhi, m)
                    dve.tensor_tensor(HID[:, 1, bass.ds(2 * i + x, 1), :], GATE[:, 2:3, :],
                                      HID[:, 0, bass.ds(2 * i + x, 1), :].bitcast(f32),
                                      ALU.subtract).then_inc(ff_done, 1)

            if l == 0:
                looped(dve, b2, FF_MODS, 4, lambda i, j: hidden(b2, i, j, EARLY + WO_UNITS))
                looped(dve, b2 + FF_MODS, FF_UNITS - FF_MODS, 4, lambda i, j: hidden(b2 + FF_MODS, i, j))
                columns(0, EARLY + WO_UNITS, MOD1 - EARLY - WO_UNITS)
            else:
                looped(dve, b2, FF_UNITS, 4, lambda i, j: hidden(b2, i, j))
            b3 = b2 + FF_UNITS

            def down(i, j):
                if l == 0:
                    modulate(EARLY + WO_UNITS + FF_MODS + j, i, 12)
                if j % 3 == 2:
                    done(b3, i, j, 3)
                    k, bank = 4 * i + j // 3, j // 3
                    dve.scalar_tensor_tensor(X[:, bass.ds(k, 1), :], PS[:, bank:bank + 1, 0:T],
                                             M1[:, l, bass.ds(40 + k, 1)], X[:, bass.ds(k, 1), :],
                                             ALU.mult, ALU.add).then_inc(bank_read[bank], 1)
                next_low(b3, i, j, 3)

            looped(dve, b3, DOWN_UNITS, 12, down)
            if l == 0:
                columns(1, 0, MOD1)
            else:
                dve.wait_ge(later_in, 16 * 3)
                columns2()

        chain(dve.memset(EPSC[:, 0:1], EPS))
        dve.memset(EPSC[:, 1:2], 1.0).then_inc(cexp, 1)
        dve.wait_ge(cexp, 2)
        chain(dve.tensor_scalar(CT[:, 1, :, :], CT[:, 0, :, :], 1.0, None, ALU.add))
        chain.wait()
        chain(dve.reciprocal(CT[:, 0, :, :], CT[:, 1, :, :]))
        chain.wait()
        dve.tensor_tensor(CA[:, :, :], CC[:, :, :], CT[:, 0, :, :], ALU.mult).then_inc(cact, 1)
        for u in range(4):
            split_low(u, 0, 1)
        dve.wait_ge(consts_in, 16 * 3)
        dve.wait_ge(spread, 1)
        dve.tensor_copy(CB, PS[:, 4:6, :].rearrange("p a (b c) -> p (a b) c", c=T)).then_inc(spread_read, 1)
        dve.wait_ge(spread_read, 1)
        looped(dve, 0, 16, 4, lambda i, j: modulate(j, i))
        columns(0, 0, 16)
        for l in range(DEPTH):
            first_layer(l)
        second_dve(dve, done, next_low, refine, chain)
    ctx.close()


def _units(w):
    k, n = w.shape
    return w.reshape(k // P, P, n // P, P).transpose(2, 1, 0, 3)


def _padded(w, n):
    out = np.zeros((w.shape[0], n), w.dtype)
    out[:, :w.shape[1]] = w
    return out


def _weights(a):
    total = DEPTH * (FIRST_UNITS + SECOND_UNITS)
    s = np.zeros((total, P, KC, P), np.float32)
    at = 0

    def put(w):
        nonlocal at
        u = _units(w)
        s[at:at + len(u)] = u
        at += len(u)

    for l in range(DEPTH):
        w = a["w_in"][l]
        cuts = np.cumsum([256, 64, 64, 256, 64, 4, 256, 256, 256, 512, 128])
        qa, ka, va, qi, ki, wi, qb, kb, vb, qc, kc, vc = np.split(w, cuts, axis=1)
        put(_padded(np.concatenate([va, vb, vc, wi], 1), 512))
        put(np.concatenate([qi, ki, ki, qa, ka, ka, qc, kc[:, :64], kc[:, :64], kc[:, 64:], kc[:, 64:], qb, kb], 1))
        put(a["w_o"][l])
        both = np.stack([a["w_gate"][l].reshape(D, FC, P), a["w_up"][l].reshape(D, FC, P)], 2)
        put(both.reshape(D, 2 * D_FF))
        down = _units(a["w_down"][l])
        for n in range(KC):
            for part in range(3):
                piece = down[n][:, part * KC:(part + 1) * KC]
                s[at, :, :piece.shape[1]] = piece
                at += 1
    for l in range(DEPTH):
        w = a["w_in_2"][l]
        cuts = np.cumsum([512, 512, 1024, 16, 1024, 1024, 1024, 1024, 1024, 1024, 1024, 1024])
        aq, ak, av, ag, ao, az, bq, bk, bv, bz, cu, cz, mg = np.split(w, cuts, axis=1)
        put(np.stack([aq.reshape(D, 4, P), ak.reshape(D, 4, P)], 2).reshape(D, D))
        put(av)
        g = np.zeros((D, 2 * P), np.float32)
        for i in range(4):
            g[:, 32 * i:32 * i + 4] = ag[:, 4 * i:4 * i + 4]
        put(g)
        put(ao)
        put(az)

        def pairs(i, out):
            m = mg[:, i * D:(i + 1) * D].reshape(D, KC, P)
            put(np.stack([m, out.reshape(D, KC, P)], 2).reshape(D, 2 * D))

        pairs(0, a["w_a_out_2"][l])
        put(bq)
        put(bk)
        put(bv)
        put(bz)
        pairs(1, a["w_b_out_2"][l])
        put(cu)
        put(cz)
        pairs(2, a["w_c_out_2"][l])
        put(a["w_out_2"][l])
    assert at == total
    return s


def _modulations(a):
    turned = np.concatenate([_units(a["w_mod"][l]) for l in range(DEPTH)])
    turned = np.ascontiguousarray(turned.transpose(0, 3, 2, 1))
    wide = [_units(a["w_ada_2"][l]) for l in range(DEPTH)]
    return np.concatenate([turned[:EARLY], wide[0], turned[EARLY:], wide[1]])


def _column(v):
    return v.reshape(-1, P).T


def _parameters(a):
    p1 = np.zeros((P, DEPTH, PAR1_W), np.float32)
    p2 = np.zeros((P, DEPTH, PAR2_W), np.float32)

    def put(dst, places, l, name, v):
        dst[:, l, places[name]:places[name] + v.shape[1]] = v

    twice = lambda v: np.tile(v, 2)[:, None]
    for l in range(DEPTH):
        put(p1, PAR1, l, "ln1", _column(a["ln1"][l]))
        put(p1, PAR1, l, "ln2", _column(a["ln2"][l]))
        put(p1, PAR1, l, "bmod", _column(a["b_mod"][l]))
        qa, ka, qc, kc = (twice(a[n][l]) for n in ("qn_a", "kn_a", "qn_c", "kn_c"))
        put(p1, PAR1, l, "gain", np.concatenate([qa, qa, ka, qc, qc, qc, qc, kc, kc], 1))
        put(p1, PAR1, l, "gout", _column(a["g_out"][l].reshape(-1)))
        put(p1, PAR1, l, "sinks", np.tile(a["sinks"][l].reshape(2, 4)[:, PLACE].reshape(1, 8), (P, 1)))
        put(p2, PAR2, l, "norm", _column(a["norm_w_2"][l]))
        put(p2, PAR2, l, "bada", _column(a["b_ada_2"][l]))
        b = np.zeros((P, 1), np.float32)
        for i in range(4):
            b[32 * i:32 * i + 4, 0] = a["b_if_2"][l][4 * i:4 * i + 4]
        put(p2, PAR2, l, "bif", b)
        put(p2, PAR2, l, "anorm", _column(a["a_norm_w_2"][l]))
        put(p2, PAR2, l, "qn", twice(a["q_norm_w_2"][l]))
        put(p2, PAR2, l, "kn", twice(a["k_norm_w_2"][l]))
        put(p2, PAR2, l, "subln", a["subln_w_2"][l][:, None])
    lam = np.stack([a[n] for n in ("lambda_q1_2", "lambda_k1_2", "lambda_q2_2", "lambda_k2_2")], 1)
    return p1, p2, np.tile(lam[None], (P, 1, 1, 1))


def _laid_out(a):
    p1, p2, lam = _parameters(a)
    first, second = constants()
    cols = np.stack([_column(a["c"][0]), _column(a["c_2"][0]), _column(a["c_ctx_2"])], 1)
    chunked = lambda x: x.T.reshape(KC, P, T).transpose(1, 0, 2)
    return {"stream": _weights(a), "mods": _modulations(a), "consts": first, "consts2": second, "par1": p1, "par2": p2, "lam": lam,
            "ccols": cols, "xT": chunked(a["x"][0]), "ctxT": chunked(a["ctx_2"][0])}


def kernel(**inputs):
    import concourse.bacc as bacc
    from concourse.bass_utils import run_bass_kernel_spmd

    a = {k: np.asarray(v) for k, v in inputs.items()}
    nc = bacc.Bacc("TRN2", target_bir_lowering=False, num_devices=1, dynamic_dma_scratch_size=2048)
    arrays = {k: np.ascontiguousarray(v) for k, v in _laid_out(a).items()}
    args = [nc.dram_tensor(k, v.shape, mybir.dt.from_np(v.dtype), kind="ExternalInput").ap()
            for k, v in arrays.items()]
    out = nc.dram_tensor("outT", (P, KC, T), mybir.dt.float32, kind="ExternalOutput").ap()
    build(nc, *args, out)
    r = run_bass_kernel_spmd(nc, [arrays], core_ids=[0])
    return r.results[0]["outT"].transpose(1, 0, 2).reshape(D, T).T[None]
```

```python
import numpy as np

import concourse.bass as bass
from concourse import mybir
from contextlib import ExitStack

P = 128
T = 256
D = 1024
KC = D // P
DEPTH = 2
D_FF = 2816
FC = D_FF // P
BEGUN = 1
BIG = 1.0e30
GONE = -3.0e38
TOPK = T // 4
PLACE = (0, 2, 1, 3)
EPS = 1e-6

V_UNITS, QK_UNITS, WO_UNITS, FF_UNITS, DOWN_UNITS = 4, 16, KC, 2 * FC, 3 * KC
FIRST_UNITS = V_UNITS + QK_UNITS + WO_UNITS + FF_UNITS + DOWN_UNITS
SECOND = [("aqk", 8), ("av", 8), ("ag", 2), ("ao", 8), ("az", 8), ("amerge", 16),
          ("bq", 8), ("bk", 8), ("bv", 8), ("bz", 8), ("bmerge", 16),
          ("cu", 8), ("cz", 8), ("cmerge", 16), ("out", 8)]
SECOND_UNITS = sum(n for _, n in SECOND)
MOD1, MOD2 = 48, 24
FIRST_MODS, WIDE_MODS = DEPTH * MOD1, DEPTH * MOD2
SUMS = 8
FF_MODS = 32

def _places(sizes):
    at, out = 0, {}
    for name, n in sizes:
        out[name] = at
        at += n
    return out, at

CONST, COMMON_W = _places([("ident", P), ("ones", P), ("heads", P)])
FIRST_CONST, FIRST_W = _places([("rot", P), ("cos", T), ("sin", T), ("causal", 2 * T), ("strict", 2 * T),
                                ("band", 2 * T)])
SECOND_CONST, SECOND_W = _places([("axrot", P), ("axcos", T), ("axsin", T), ("lower", P), ("upper", P),
                                  ("dft", 2 * 512)])
CONST.update({k: COMMON_W + v for k, v in [*FIRST_CONST.items(), *SECOND_CONST.items()]})
CONST_W = COMMON_W + max(FIRST_W, SECOND_W)
PAR1, PAR1_W = _places([("ln1", KC), ("ln2", KC), ("bmod", MOD1), ("gain", 9), ("gout", KC),
                        ("sinks", 8)])
PAR2, PAR2_W = _places([("norm", KC), ("bada", MOD2), ("bif", 1), ("anorm", KC), ("qn", 1),
                        ("kn", 1), ("subln", 1)])


def constants():
    f = np.float32
    first, second = np.zeros((P, COMMON_W + FIRST_W), f), np.zeros((P, COMMON_W + SECOND_W), f)
    r = np.arange(P)

    def put(name, a):
        c = second if name in SECOND_CONST else first
        c[:a.shape[0], CONST[name]:CONST[name] + a.shape[1]] = a

    put("ident", np.eye(P, dtype=f))
    put("ones", np.ones((P, P), f))
    put("heads", (r[:, None] // 64 == r[None, :] // 64).astype(f))

    def rotation(half):
        m = np.zeros((P, P), f)
        for o in range(P):
            if o % (2 * half) < half:
                m[o + half, o] = -1.0
            else:
                m[o - half, o] = 1.0
        return m

    put("rot", rotation(32))
    put("axrot", rotation(16))
    inv = (1.0 / (f(10000.0) ** (np.arange(0, 64, 2, dtype=f) / f(64)))).astype(f)
    ang = inv[r % 32][:, None] * np.arange(T, dtype=f)[None, :]
    put("cos", np.cos(ang))
    put("sin", np.sin(ang))
    inv = (f(10000.0) ** (-np.arange(0, 32, 2, dtype=f) / f(32))).astype(f)
    t = np.arange(T)
    pos = np.where((r % 64 < 32)[:, None], (t // 64)[None, :], (t % 64)[None, :]).astype(f)
    ang = inv[r % 16][:, None] * pos
    put("axcos", np.cos(ang))
    put("axsin", np.sin(ang))
    q = (np.arange(2)[None, :, None] * P + r[:, None, None])
    s = np.arange(T)[None, None, :]
    put("causal", np.where(s <= q, 0, -BIG).astype(f).reshape(P, 2 * T))
    put("strict", np.where(s < q, 0, -BIG).astype(f).reshape(P, 2 * T))
    put("band", np.where((s <= q) & (q - s < 128), 0, -BIG).astype(f).reshape(P, 2 * T))
    put("lower", np.where(r[:, None] <= r[None, :], 0, -BIG).astype(f))
    put("upper", np.where(r[:, None] >= r[None, :], 0, -BIG).astype(f))
    w = 2 * np.pi * ((np.arange(T)[:, None] * np.arange(T)[None, :]) % T) / T
    cos, sin = (np.cos(w) / 16).astype(f), (np.sin(w) / 16).astype(f)
    both = np.concatenate([cos, sin], 1)
    put("dft", both.reshape(2, P, 512).transpose(1, 0, 2).reshape(P, -1))
    return first, second[:, COMMON_W:]


def build(nc, stream, mods, consts, consts2, par1, par2, lam, ccols, xT, ctxT, outT):
    f32, f32r = mybir.dt.float32, mybir.dt.float32r
    ALU, ACT, AX = mybir.AluOpType, mybir.ActivationFunctionType, mybir.AxisListType
    PER = FIRST_UNITS
    ctx = ExitStack()

    def sb(name, shape, dt=f32):
        return ctx.enter_context(nc.sbuf_tensor(name, shape, dt))

    def sem(name):
        return ctx.enter_context(nc.semaphore(name))

    C = sb("C", [P, CONST_W])
    XX = sb("XX", [P, KC, 2 * T])
    AR = sb("AR", [P, 16384], f32r)
    WH = sb("WH", [P, 4, KC, P], f32r)
    WL = sb("WL", [P, 4, KC, P], f32r)
    RAW = sb("RAW", [P, 4, KC // 2, P])
    P1 = sb("P1", [P, DEPTH, PAR1_W])
    P2 = sb("P2", [P, DEPTH, PAR2_W])
    CC = sb("CC", [P, 3, KC])
    CA = sb("CA", [P, 3, KC])
    CT = sb("CT", [P, 2, 3, KC])
    M1 = sb("M1", [P, DEPTH, MOD1])
    A1 = sb("A1", [P, DEPTH, 2, KC])
    M2 = sb("M2", [P, DEPTH, MOD2, 2])
    A2 = sb("A2", [P, DEPTH, KC, 2])
    COL = sb("COL", [P, 64])
    EPSC = sb("EPSC", [P, 2])
    WORK = sb("WORK", [P, 22528])

    def const(name, n=P):
        return C[:, CONST[name]:CONST[name] + n]

    ident, ones, heads = const("ident"), const("ones"), const("heads")
    X = XX[:, :, T:2 * T]
    CB = XX[:, :, 0:T].rearrange("p (c k) t -> p c k t", c=2)
    H1 = AR[:, 0:2 * KC * T].rearrange("p (s k t) -> p s k t", s=2, k=KC)
    HID = AR[:, 2 * KC * T:2 * KC * T + 2 * FC * T].rearrange("p (s k t) -> p s k t", s=2, k=FC)
    OS = AR[:, 2 * KC * T:4 * KC * T].rearrange("p (s k t) -> p s k t", s=2, k=KC)

    def work(at, *shape):
        n = int(np.prod(shape))
        v = WORK[:, at:at + n]
        names = "abcd"[:len(shape)]
        if len(shape) > 1:
            v = v.rearrange(f"p ({' '.join(names)}) -> p {' '.join(names)}",
                            **{names[i]: shape[i] for i in range(len(shape))})
        return v

    F = work(0, QK_UNITS, T)
    V = work(4096, 2, 512)
    O = work(5120, KC, T)
    SM = work(7168, 2, 4, T)
    PR = work(9216, 2, 4, T)
    PT = work(11264, 2, 3, 4, P)
    WK = work(14336, 2, T)
    SEL = work(14848, 2, T)
    GATE = work(15360, 4, T)
    GRING = work(16384, 4, KC, P)
    MV = work(20992, FIRST_MODS, SUMS)
    MV2 = work(20992, WIDE_MODS, 2, SUMS)
    RS = work(20480, 2, T)
    SQ = work(7168, KC, T)
    TMP = work(9216, 9, T)
    NX = work(9216, 4, T)
    VM = work(5120, 9, T)
    VO = work(11264, KC, T)
    SN = work(7680, 2, 2, T)
    RSO = work(9216, KC, T)
    STK = work(15360, 4, T)
    RO = work(11520, 12, T)

    H2 = AR[:, 0:8192].rearrange("p (s k t) -> p s k t", s=2, k=KC)
    Y2 = AR[:, 8192:16384].rearrange("p (s k t) -> p s k t", s=2, k=KC)
    YB = work(0, KC, 2 * T)
    KB = work(4096, KC, 2 * T)
    EB = work(4096, 2, 4, 2 * T)
    V2 = work(8192, 4, D)
    ACC = work(12288, KC, 2 * T)
    SQ2 = work(12288, KC, 2 * T)
    GT = work(12288, 2 * T)
    GI, GF, CF = work(12800, 2, 2 * T), work(13824, 2, 2 * T), work(14848, 2, 2 * T)
    CM, TG = work(16384, 2, 2 * T), work(17408, 2, 2 * T)
    NMS, NMD, EMS = (work(18432 + 1024 * i, 2, 2 * T) for i in range(3))
    DN, TM2 = work(21504, 2 * T), work(22016, 2 * T)
    NX2, RS2 = work(16384, 4, 2 * T), work(18432, 2, 2 * T)
    SG, SZ = work(20480, 2, 2 * T), work(21504, 2, 2 * T)
    SQB, RB = work(16384, 2, 2 * T), work(17408, 2, 2 * T)
    TC, TS = work(18432, 2, T), work(18944, 2, T)
    PB, WT = work(19456, 2, 2, 2 * T), work(21504, 2, 4, P)
    YS = work(21504, 2, 2 * T)
    SINES = work(20224, 2, P)
    VB, VP = work(18432, 2, 2 * T), work(19456, 2, 2 * T)
    UC = sb("UC", [P, 8, 4])
    LM = sb("LM", [P, 2 * DEPTH + 2 * DEPTH])
    LT = work(16384, 2, DEPTH, 64)
    LAM = work(16640, DEPTH, 4, 64)
    LR = sb("LR", [P, 2, DEPTH])
    BC = sb("BC", [P, 2, 8])

    PS = ctx.enter_context(nc.psum_tensor("PS", [P, 8, 512], f32))

    def sems(names):
        return [sem(n) for n in names.split()]

    common_in, consts_in, consts2_in, c_in, later_in = sems("common_in consts_in consts2_in c_in later_in")
    raw_full = [sem(f"raw_full{i}") for i in range(4)]
    hi_done = sem("hi_done")
    lo_done = [sem("lo_done_dve"), sem("lo_done_pool")]
    unit_done = sem("unit_done")
    bank_read = [sem(f"bank_read{i}") for i in range(4)]
    mod_full = [sem(f"mod_full{i}") for i in range(4)]
    wide_full = [sem(f"wide_full{i}") for i in range(2)]
    mod_used, wide_used, mod_read = sems("mod_used wide_used mod_read")
    spread, spread_read = sems("spread spread_read")
    dve_chain, act_chain = sems("dve_chain act_chain")
    c_exped, c_done = sems("c_exped c_done")
    sq_done, sum_done, rstd_done, nx_done, nhi_done, norm_done = sems(
        "sq_done sum_done rstd_done nx_done nhi_done norm_done")
    rsq_done, ms_done, ms_read, rms_roots, rms_done = sems("rsq_done ms_done ms_read rms_roots rms_done")
    rot_done, rope_cosine, rot_read, rope_done = sems("rot_done rope_cosine rot_read rope_done")
    scores, scores_read, masked, exped, probs = sems("scores scores_read masked exped probs")
    stick_logs, stick_sums, sticks = sems("stick_logs stick_sums sticks")
    turned, pt_ready, pv_done, o_ready = sems("turned pt_ready pv_done o_ready")
    out_squared, out_sums, out_roots, out_scaled, out_hi, out_lo = sems(
        "out_squared out_sums out_roots out_scaled out_hi out_lo")
    ff_sigmoid, ff_hi, ff_done = sems("ff_sigmoid ff_hi ff_done")
    out_done = sem("out_done")
    lam_r, lam_e = sems("lam_r lam_e")
    gates_ready, gates_summed, gates_exped, gates_turned, gate_columns = sems(
        "gates_ready gates_summed gates_exped gates_turned gate_columns")
    a_scores, row_full, row_read, row_masked, floor_full, floor_read = sems(
        "a_scores row_full row_read row_masked floor_full floor_read")
    decayed, weighted, den_done, den_read, num_done, post_done = sems(
        "decayed weighted den_done den_read num_done post_done")
    g_squared, g_sums, g_sums_read, g_roots, g_scaled = sems("g_squared g_sums g_sums_read g_roots g_scaled")
    o_gated = sem("o_gated")
    sig_done, gated, y_hi, y_done = sems("sig_done gated y_hi y_done")
    acc_done, acc_hi, a_done = sems("acc_done acc_hi a_done")
    p_squared, p_sums, p_sums_read, p_roots, p_scaled, p_rotated, p_cosine, p_sine, p_done = sems(
        "p_squared p_sums p_sums_read p_roots p_scaled p_rotated p_cosine p_sine p_done")
    b_scores, b_max, b_exped, b_weights, b_turned, b_turned_read, b_values, b_out_read = sems(
        "b_scores b_max b_exped b_weights b_turned b_turned_read b_values b_out_read")
    dft1, dft1_read, dft2, dft2_read = sems("dft1 dft1_read dft2 dft2_read")

    block = ctx.enter_context(nc.Block())
    total = DEPTH * PER + DEPTH * SECOND_UNITS

    class Chain:

        def __init__(self, eng, s):
            self.eng, self.s, self.n = eng, s, 0

        def __call__(self, ins):
            ins.then_inc(self.s, 1)
            self.n += 1

        def wait(self):
            self.eng.wait_ge(self.s, self.n)

    def earlier(u):
        layer = (FIRST_UNITS - DOWN_UNITS + KC) // 4
        done = min(u // FIRST_UNITS, DEPTH)
        return done * layer + (u - done * FIRST_UNITS) // 4

    def looped(eng, base, count, step, body):
        with eng.Fori(0, count // step) as i:
            for j in range(step):
                body(i, j)

    def stages(l):
        at, out = DEPTH * FIRST_UNITS + l * SECOND_UNITS, {}
        for name, n in SECOND:
            out[name] = at
            at += n
        return out

    def cover(d, c, l):
        low = 2 * l
        if d == 0:
            return [(max(c, low), 4)]
        found = {0: [(0, 1), (2, 4)], 1: [(0, 4)], 2: [(2, 3)], 3: [(2, 4)]}[c]
        return [(max(a, low), b) for a, b in found if b > low]

    def beyond(d, c, l):
        out = []
        for a, b in cover(d, c, l):
            if a <= c < b:
                out += [(a, c), (c + 1, b)]
            else:
                out.append((a, b))
        return [(a, b) for a, b in out if a < b]

    def tiles(l):
        return [(h, n) for h in range(8) for n in range(2 * l, 4)]

    def tile_base(l):
        return 32 * l

    def parts(l):
        return range(l, 2)

    def second_pe(pe, feature_unit, token_pair):
        def layer(l):
            st, t0 = stages(l), l * T
            idx = 4 + l
            moving, all_moving, ymoving = H2[:, :, :, t0:], H2, Y2[:, :, :, t0:]
            n = 2 * T - t0
            for k in range(KC):
                pe.wait_ge(sq_done, idx * KC + k + 1)
                last = pe.matmul(PS[:, 6, :], ones, SQ2[:, k, :], start=(k == 0), stop=(k == KC - 1))
            last.then_inc(sum_done, 1)
            ready = (norm_done, idx * KC)
            b = st["aqk"]

            def tokens(name, first):
                with pe.Fori(0, 2) as i:
                    for j in (0, 2):
                        token_pair(st[name], i, j, H2, first, 4)

            def qk(i, j):
                if j % 2:
                    feature_unit(b, i, j, all_moving, 2 * T, ready)
                else:
                    feature_unit(b, i, j, moving, n, ready)

            looped(pe, b, 8, 4, qk)
            tokens("av", 0)
            feature_unit(st["ag"], 0, 0, all_moving, 2 * T)
            for half in range(2):
                pe.wait_ge(lo_done[half], st["ag"] + 2)
            last = pe.matmul(PS[:, (st["ag"] + 1) % 4, 0:P], ident, ident, start=True, stop=True)
            last.then_inc(unit_done, 1)
            pe.wait_ge(gates_summed, l + 1)
            for d in range(2):
                for c in range(4):
                    at = (4 * d + c) * 4
                    last = pe.transpose(PS[:, 4, at:at + 4], GI[0:4, d, c * P:(c + 1) * P], ident[0:4, 0:4])
            last.then_inc(gates_turned, 1)
            pe.wait_ge(gates_exped, l + 1)
            pe.wait_ge(gate_columns, l + 1)
            for j in range(4):
                pe.wait_ge(bank_read[(st["ao"] + j) % 4], earlier(st["ao"] + j))
            def pick(h):
                return ident[0:4, h:h + 1].broadcast_to([4, P])

            def numerator(e):
                h, d = e // 2, e % 2
                pe.wait_ge(weighted, 8 * l + e + 1)
                order = [1, 0, 2, 3] if d else [0, 1, 2, 3]
                for v in (2, 0, 1):
                    if 8 * l + e and v == 2:
                        pe.wait_ge(den_read, 8 * l + e)
                    if 8 * l + e and v == 0:
                        pe.wait_ge(post_done, 8 * l + e)
                    runs = [(c, a, b) for c in order for a, b in cover(d, c, l)]
                    for r, (c, a, b) in enumerate(runs):
                        lhs = ones if v == 2 else V2[:, c, (2 * h + v) * P:(2 * h + v + 1) * P]
                        last = pe.matmul(PS[:, 5 + v, a * P:b * P], lhs, EB[:, d, c, a * P:b * P],
                                         start=(r == 0), stop=(r == len(runs) - 1))
                    if v == 2:
                        last.then_inc(den_done, 1)
                last.then_inc(num_done, 1)

            def spread_row(rows, e):
                return pe.matmul(PS[:, 4, t0:], pick(e // 2), rows[0:4, e % 2, t0:], start=True, stop=True)

            for e in range(9):
                if e < 8:
                    if e >= 2:
                        pe.wait_ge(floor_read, 8 * l + e - 1)
                    elif e == 1:
                        pe.wait_ge(row_read, 8 * l + 1)
                    spread_row(CM, e).then_inc(row_full, 1)
                if e:
                    if e < 8:
                        pe.wait_ge(row_read, 8 * l + e + 1)
                    else:
                        pe.wait_ge(floor_read, 8 * l + e - 1)
                    spread_row(TG, e - 1).then_inc(floor_full, 1)
                if e < 8 and e % 2 == 0:
                    h = e // 2
                    if e:
                        pe.wait_ge(weighted, 8 * l + e)
                    for c in range(4):
                        a = max(t0, 2 * (c // 2) * P)
                        last = pe.matmul(PS[:, c, a:], YB[:, 2 * h + 1, c * P:(c + 1) * P], YB[:, 2 * h, a:],
                                         start=True, stop=True)
                    last.then_inc(a_scores, 1)
                if e:
                    numerator(e - 1)

            def norm_groups(first, groups, wide, name):
                for g in range(groups):
                    x = first + g
                    pe.wait_ge(g_squared, 12 * l + x + 1)
                    if x >= 2:
                        pe.wait_ge(g_sums_read, 12 * l + x - 1)
                    for w in range(wide):
                        last = pe.matmul(PS[:, 4 + x % 2, t0:], ones, SQN(x, w)[:, t0:],
                                         start=(w == 0), stop=(w == wide - 1))
                    last.then_inc(g_sums, 1)
                    if g % (groups // 4) == groups // 4 - 1:
                        feature_unit(st[name], 0, g * 4 // groups, moving, n)
                for j in range(4, 8):
                    feature_unit(st[name], 0, j, moving, n)

            norm_groups(0, 4, 2, "ao")
            looped(pe, st["az"], 8, 4, lambda i, j: feature_unit(st["az"], i, j, moving, n))

            def merge(name, branch):
                b = st[name]

                def pair(i, j):
                    if j % 2:
                        feature_unit(b, i, j, ymoving, n, (y_done, (3 * l + branch) * KC))
                    else:
                        feature_unit(b, i, j, moving, n)

                looped(pe, b, 16, 4, pair)

            merge("amerge", 0)
            looped(pe, st["bq"], 8, 4, lambda i, j: feature_unit(st["bq"], i, j, moving, n))
            looped(pe, st["bk"], 8, 4, lambda i, j: feature_unit(st["bk"], i, j, all_moving, 2 * T))

            def rotate(x):
                src = (YB if x < 8 else KB)[:, x % 8, T:2 * T]
                pe.wait_ge(p_scaled, 16 * l + x + 1)
                if x >= 2:
                    pe.wait_ge(p_sine, 16 * l + x - 1)
                pe.matmul(PS[:, 6 + x % 2, 0:T], const("axrot"), src, start=True, stop=True).then_inc(p_rotated, 1)

            for x in range(16):
                a = t0 if x < 8 else 0
                pe.wait_ge(p_squared, 16 * l + x + 1)
                if x >= 2:
                    pe.wait_ge(p_sums_read, 16 * l + x - 1)
                pe.matmul(PS[:, 4 + x % 2, a:], heads, SQB[:, x % 2, a:], start=True, stop=True).then_inc(p_sums, 1)
                if x:
                    rotate(x - 1)
                token_pair(st["bv"], 0, x // 4 * 2, H2, 0, 4, only=x % 4)
            rotate(15)
            for j in range(4):
                pe.wait_ge(bank_read[(st["bz"] + j) % 4], earlier(st["bz"] + j))
            pe.wait_ge(p_done, 16 * (l + 1))
            steps = tiles(l)

            def score(f):
                h, q = steps[f]
                keys = 2 * T if q >= 2 else T
                if f >= 2:
                    pe.wait_ge(b_exped, tile_base(l) + f - 1)
                for m in range(2):
                    rows = slice(64 * m, 64 * m + 64)
                    last = pe.matmul(PS[:, 2 * (f % 2) + m, 0:keys], YB[rows, h, q * P:(q + 1) * P],
                                     KB[rows, h, 0:keys], start=True, stop=True)
                last.then_inc(b_scores, 1)

            def turn(f):
                h, q = steps[f]
                pe.wait_ge(b_weights, tile_base(l) + f + 1)
                if f >= 2:
                    pe.wait_ge(b_turned_read, tile_base(l) + f - 1)
                for c in range(4 if q >= 2 else 2):
                    last = pe.transpose(PS[:, 4 + f % 2, c * P:(c + 1) * P], PB[:, f % 2, 0, c * P:(c + 1) * P],
                                        ident)
                last.then_inc(b_turned, 1)

            def value(f):
                h, q = steps[f]
                blocks = 4 if q >= 2 else 2
                pe.wait_ge(b_turned_read, tile_base(l) + f + 1)
                if q == 2 * l and h >= 2:
                    pe.wait_ge(b_out_read, 8 * l + h - 1)
                for c in range(blocks):
                    last = pe.matmul(PS[:, 6 + h % 2, q * P:(q + 1) * P], V2[:, c, h * P:(h + 1) * P],
                                     WT[:, f % 2, c, :], start=(c == 0), stop=(c == blocks - 1))
                last.then_inc(b_values, 1)

            score(0)
            score(1)
            for f in range(len(steps)):
                if f + 2 < len(steps):
                    score(f + 2)
                turn(f)
                if f:
                    value(f - 1)
            value(len(steps) - 1)
            norm_groups(4, 8, 1, "bz")
            merge("bmerge", 1)
            tokens("cu", 2 * l)
            for j in range(4):
                pe.wait_ge(bank_read[(st["cz"] + j) % 4], earlier(st["cz"] + j))
            dft = const("dft", 1024).rearrange("p (m n) -> p m n", m=2)
            for p in parts(l):
                past = 8 * (p if l == 0 else 2)
                for x in range(8):
                    if past + x >= 2:
                        pe.wait_ge(dft1_read, past + x - 1)
                    for to, table in ((slice(0, P + 1), slice(0, P + 1)), (slice(P + 1, T), slice(T + 1, T + P))):
                        for m in range(2):
                            last = pe.matmul(PS[:, 4 + x % 2, to], V2[:, 2 * p + m, x * P:(x + 1) * P],
                                             dft[:, m, table], start=(m == 0), stop=(m == 1))
                    last.then_inc(dft1, 1)
                pe.wait_ge(dft1_read, past + 8)
                for x in range(8):
                    if past + x >= 2:
                        pe.wait_ge(dft2_read, past + x - 1)
                    cut, sine = (slice(at + (x % 2) * P, at + (x % 2 + 1) * P) for at in (0, T))
                    for to, table, part in ((slice(0, P + 1), cut, slice(0, P + 1)),
                                            (slice(T, T + P - 1), sine, slice(P + 1, T))):
                        for m in range(2):
                            last = pe.matmul(PS[:, 6 + x % 2, to], dft[:, m, table], KB[:, x // 2 * 2 + m, part],
                                             start=(m == 0), stop=(m == 1))
                    last.then_inc(dft2, 1)
            looped(pe, st["cz"], 8, 4, lambda i, j: feature_unit(st["cz"], i, j, moving, n))
            merge("cmerge", 2)
            looped(pe, st["out"], 8, 4, lambda i, j: feature_unit(st["out"], i, j, moving, n, (a_done, l * KC)))

        return layer

    def SQN(x, w):
        return EB[:, x % 2, w, :] if x < 4 else SQB[:, x % 2, :]

    def second_pool(pool, lows, first):
        for l in range(DEPTH):
            end = stages(l)["bv"] + 4
            lows(first, end)
            first = end
            for x in range(16):
                pool.wait_ge(p_scaled, 16 * l + x + 1)
                if x >= 2:
                    pool.wait_ge(p_done, 16 * l + x - 1)
                pool.tensor_tensor(TC[:, x % 2, :], (YB if x < 8 else KB)[:, x % 8, T:], const("axcos", T),
                                   ALU.mult).then_inc(p_cosine, 1)
                if x >= 6 and x % 4 == 2:
                    lows(first, first + 2)
                    first += 2
        lows(first, total)

    def second_act(act, done, next_high, exponentials, sigmoids, inverse_root, chain):
        def layer(l):
            st, t0 = stages(l), l * T
            idx, n = 4 + l, 2 * T - l * T
            for k in range(KC):
                if l:
                    u = stages(l - 1)["out"] + k
                    act.wait_ge(bank_read[u % 4], earlier(u) + 1)
                else:
                    act.wait_ge(bank_read[k % 4], earlier(DEPTH * FIRST_UNITS - DOWN_UNITS) + k // 4 + 1)
                act.activation(SQ2[:, k, :], XX[:, k, :], ACT.Square).then_inc(sq_done, 1)
            act.wait_ge(sum_done, idx + 1)
            inverse_root(RS2[:, 1, :], RS2[:, 0, :], PS[:, 6, :], 1.0 / D, None, rstd_done)
            act.wait_ge(mod_read, 1)
            for k in range(KC):
                act.wait_ge(nx_done, idx * KC + k + 1)
                for c in range(2):
                    cut = slice((1 - c) * T, (2 - c) * T)
                    last = act.activation(H2[:, 0, k, cut], NX2[:, k % 4, cut], ACT.Identity,
                                          bias=M2[:, l, k, c:c + 1])
                last.then_inc(nhi_done, 1)
            b = st["aqk"]

            def copied(b, dst, lo, scale=1.0):
                def body(i, j):
                    done(b, i, j)
                    bank = (b + j) % 4
                    act.activation(dst[:, bass.ds(4 * i + j, 1), lo:], PS[:, bank:bank + 1, 0:2 * T - lo],
                                   ACT.Copy).then_inc(bank_read[bank], 1)
                    next_high(b, i, j)
                return body

            def qk(i, j):
                done(b, i, j)
                bank = (b + j) % 4
                lo, scale = (0, float(P) ** -0.5) if j % 2 else (t0, 1.0)
                act.activation(YB[:, bass.ds(4 * i + j, 1), lo:], PS[:, bank:bank + 1, 0:2 * T - lo],
                               ACT.Copy, scale=scale).then_inc(bank_read[bank], 1)
                next_high(b, i, j)

            def values(b, first):
                def body(i, j):
                    done(b, i, j)
                    bank, half = (b + j) % 4, (4 - first) // 2
                    row = first + (j % 2) * half
                    act.activation(V2[:, row:row + half, bass.ds((4 * i + j // 2 * 2) * P, 2 * P)],
                                   PS[:, bank, 0:half * 2 * P].rearrange("p (b c) -> p b c", b=half),
                                   ACT.Copy).then_inc(bank_read[bank], 1)
                    next_high(b, i, j)
                return body

            looped(act, b, 8, 4, qk)
            looped(act, st["av"], 8, 4, values(st["av"], 0))
            u = st["ag"]
            done(u, 0, 0)
            act.activation(GT, PS[:, u % 4, :], ACT.Identity,
                           bias=P2[:, l, PAR2["bif"]:PAR2["bif"] + 1]).then_inc(bank_read[u % 4], 1)
            next_high(u, 0, 0)
            next_high(u, 0, 1)
            act.wait_ge(bank_read[u % 4], earlier(u) + 1)
            for d in range(2):
                ins = act.activation(GI[0:4, d, :], GT[64 * d:64 * d + 4, :], ACT.Copy)
                if d:
                    ins.then_inc(bank_read[(u + 1) % 4], 1)
                chain(act.activation(GF[0:4, d, :], GT[64 * d + 32:64 * d + 36, :], ACT.Copy))
            chain.wait()
            chain(act.activation(CF[0:4, :, :], GF[0:4, :, :], ACT.Abs))
            chain.wait()
            chain(act.activation(CF[0:4, :, :], CF[0:4, :, :], ACT.Exp, scale=-1.0))
            chain.wait()
            act.activation(CF[0:4, :, :], CF[0:4, :, :], ACT.Ln, bias=EPSC[0:4, 1:2]).then_inc(gates_ready, 1)
            act.wait_ge(gates_summed, l + 1)
            act.activation(TG[0:4, :, :], TG[0:4, :, :], ACT.Exp, scale=-1.0).then_inc(gates_exped, 1)
            act.wait_ge(gate_columns, l + 1)
            for e in range(9):
                d, h = e % 2, e // 2
                if e < 8:
                    act.wait_ge(row_full, 8 * l + e + 1)
                    if e >= 2:
                        act.wait_ge(row_masked, 8 * l + e - 1)
                        act.wait_ge(decayed, 8 * l + e - 1)
                    act.activation(NMS[:, d, t0:], PS[:, 4, t0:], ACT.Copy).then_inc(row_read, 1)
                if e:
                    act.wait_ge(floor_full, 8 * l + e)
                    if e >= 3:
                        act.wait_ge(den_read, 8 * l + e - 2)
                    act.activation(EMS[:, 1 - d, t0:], PS[:, 4, t0:], ACT.Copy).then_inc(floor_read, 1)
                if e == 8:
                    break
                act.wait_ge(row_masked, 8 * l + e + 1)
                act.wait_ge(row_read, 8 * l + e + 1)
                if e >= 2:
                    act.wait_ge(num_done, 8 * l + e - 1)
                for c in range(4):
                    bias = UC[:, 4 * d + c, h:h + 1]
                    if c >= 2 * l:
                        cut = slice(c * P, (c + 1) * P)
                        last = act.activation(EB[:, d, c, cut], NMD[:, d, cut], ACT.Exp, bias=bias)
                    for a, z in beyond(d, c, l):
                        cut = slice(a * P, z * P)
                        last = act.activation(EB[:, d, c, cut], NMS[:, d, cut], ACT.Exp, bias=bias)
                last.then_inc(decayed, 1)

            def norm_groups(first, groups, wide, scale):
                for g in range(groups + 1):
                    x = first + g
                    if g < groups:
                        if x == 0:
                            act.wait_ge(post_done, 8 * (l + 1))
                            act.wait_ge(num_done, 8 * (l + 1))
                        if g >= 2:
                            act.wait_ge(g_sums, 12 * l + x - 1)
                        for w in range(wide):
                            last = act.activation(SQN(x, w)[:, t0:], YB[:, wide * g + w, t0:], ACT.Square)
                        last.then_inc(g_squared, 1)
                    if g:
                        x -= 1
                        act.wait_ge(g_sums, 12 * l + x + 1)
                        if g >= 3:
                            act.wait_ge(g_scaled, 12 * l + x - 1)
                        inverse_root(NRM(x)[:, t0:], VRM(x)[:, t0:], PS[:, 4 + x % 2, t0:], scale,
                                     (g_sums_read, 12 * l + x + 1), g_roots)

            norm_groups(0, 4, 2, 1.0 / 256)

            def output_gate(i, j):
                b = st["ao"]
                done(b, i, j)
                bank = (b + j) % 4
                act.wait_ge(o_gated, 4 * i + (8 * l + max(j - 1, 0) + BEGUN))
                act.activation(SG[:, j % 2, t0:], PS[:, bank, 0:n], ACT.Sigmoid).then_inc(bank_read[bank], 1)
                next_high(b, i, j)

            sigmoids()
            looped(act, st["ao"], 8, 4, output_gate)

            def z_gate(name, branch):
                b = st[name]

                def body(i, j):
                    done(b, i, j)
                    bank = (b + j) % 4
                    y = 4 * i + ((3 * l + branch) * KC + j)
                    act.activation(SG[:, j % 2, t0:], PS[:, bank, 0:n], ACT.Sigmoid).then_inc(sig_done, 1)
                    next_high(b, i, j)
                    act.wait_ge(gated, y + 1 + BEGUN)
                    act.activation(Y2[:, 0, bass.ds(4 * i + j, 1), t0:], YB[:, bass.ds(4 * i + j, 1), t0:],
                                   ACT.Copy).then_inc(y_hi, 1)

                looped(act, b, 8, 4, body)

            def merge(name, branch):
                b = st[name]

                def body(i, j):
                    bank = (b + j) % 4
                    if j % 2 == 0:
                        done(b, i, j)
                        act.wait_ge(bank_read[(b + j - 1) % 4], i + (earlier(b + j - 1) + 1))
                        act.activation(SG[:, j // 2, t0:], PS[:, bank, 0:n], ACT.Sigmoid).then_inc(bank_read[bank], 1)
                    next_high(b, i, j)

                looped(act, b, 16, 4, body)

            act.wait_ge(o_gated, KC * (l + 1) + BEGUN)
            z_gate("az", 0)
            merge("amerge", 0)
            exponentials()
            looped(act, st["bq"], 8, 4, copied(st["bq"], YB, t0))
            looped(act, st["bk"], 8, 4, copied(st["bk"], KB, 0))
            for j in range(4):
                act.wait_ge(bank_read[(st["bv"] + j) % 4], earlier(st["bv"] + j))
            take = values(st["bv"], 0)
            for x in range(17):
                if x < 16:
                    a = t0 if x < 8 else 0
                    src = (YB if x < 8 else KB)[:, x % 8, a:]
                    if x >= 2:
                        act.wait_ge(p_sums, 16 * l + x - 1)
                    act.activation(SQB[:, x % 2, a:], src, ACT.Square).then_inc(p_squared, 1)
                if x:
                    y = x - 1
                    a = t0 if y < 8 else 0
                    act.wait_ge(p_sums, 16 * l + y + 1)
                    if y >= 2:
                        act.wait_ge(p_scaled, 16 * l + y - 1)
                    inverse_root(RB[:, y % 2, a:], VP[:, y % 2, a:], PS[:, 4 + y % 2, a:], 1.0 / 64,
                                 (p_sums_read, 16 * l + y + 1), p_roots, YS[:, y % 2, a:])
                if x >= 5 and x % 4 == 1:
                    for j in range((x - 5) // 2, (x - 5) // 2 + 2):
                        take(0, j)
            for j in range(6, 8):
                take(0, j)
            steps, tb = tiles(l), tile_base(l)

            def exps(f):
                h, q = steps[f]
                keys = 2 * T if q >= 2 else T
                act.wait_ge(b_max, tb + f + 1)
                if f >= 2:
                    act.wait_ge(b_turned, tb + f - 1)
                for m in range(2):
                    last = act.activation(PB[:, f % 2, m, 0:keys], PS[:, 2 * (f % 2) + m, 0:keys], ACT.Exp,
                                          bias=BC[:, f % 2, 2 + m:3 + m], scale=0.125,
                                          accum_out=BC[:, f % 2, 4 + m:5 + m])
                last.then_inc(b_exped, 1)

            def head_out(h):
                act.wait_ge(b_values, tb + (h + 1) * (4 - 2 * l))
                act.activation(YB[:, h, t0:], PS[:, 6 + h % 2, t0:], ACT.Copy).then_inc(b_out_read, 1)

            exps(0)
            per = 4 - 2 * l
            for f in range(len(steps)):
                if f + 1 < len(steps):
                    exps(f + 1)
                act.wait_ge(b_turned, tb + f + 1)
                if f >= 2:
                    act.wait_ge(b_values, tb + f - 1)
                blocks = 4 if steps[f][1] >= 2 else 2
                act.activation(WT[:, f % 2, 0:blocks, :],
                               PS[:, 4 + f % 2, 0:blocks * P].rearrange("p (a b) -> p a b", a=blocks),
                               ACT.Copy).then_inc(b_turned_read, 1)
                if f and f % per == 0:
                    head_out(f // per - 1)
            head_out(7)
            act.wait_ge(b_out_read, 8 * (l + 1))
            norm_groups(4, 8, 1, 1.0 / 128)
            sigmoids()
            z_gate("bz", 1)
            merge("bmerge", 1)
            looped(act, st["cu"], 8, 4, values(st["cu"], 2 * l))
            for p in parts(l):
                past = 8 * (p if l == 0 else 2)
                for x in range(8):
                    act.wait_ge(dft1, past + x + 1)
                    act.activation(KB[:, x, 0:T], PS[:, 4 + x % 2, 0:T], ACT.Copy).then_inc(dft1_read, 1)
            z_gate("cz", 2)
            merge("cmerge", 2)
            exponentials()
            act.wait_ge(unit_done, st["out"])
            for k in range(KC):
                act.wait_ge(acc_done, (2 * l + 1) * KC + k + 1 + BEGUN)
                act.activation(H2[:, 0, k, t0:], ACC[:, k, t0:], ACT.Copy).then_inc(acc_hi, 1)
            if l == DEPTH - 1:
                for i in range(2):
                    for j in range(4):
                        next_high(st["out"], i, j)
            else:
                looped(act, st["out"], 8, 4, lambda i, j: next_high(st["out"], i, j))

        act.wait_ge(lam_r, 1)
        act.activation(LM[:, 0:4], LR[:, :, :].rearrange("p a b -> p (a b)"), ACT.Exp).then_inc(lam_e, 1)
        for l in range(DEPTH):
            layer(l)

    def VRM(x):
        return NMD[:, x % 2, :] if x < 4 else VB[:, x % 2, :]

    def NRM(x):
        return NMS[:, x % 2, :] if x < 4 else RB[:, x % 2, :]

    def second_dve(dve, done, next_low, refine, chain):
        def layer(l):
            st, t0 = stages(l), l * T
            idx, n = 4 + l, 2 * T - l * T
            dve.wait_ge(rstd_done, idx + 1)
            refine(RS2[:, 1, :], RS2[:, 0, :])

            def low(k):
                dve.wait_ge(nhi_done, idx * KC + k + 1)
                for c in range(2):
                    cut = slice((1 - c) * T, (2 - c) * T)
                    ins = dve.scalar_tensor_tensor(H2[:, 1, k, cut], NX2[:, k % 4, cut], M2[:, l, k, c:c + 1],
                                                   H2[:, 0, k, cut].bitcast(f32), ALU.add, ALU.subtract)
                ins.then_inc(norm_done, 1)

            for k in range(KC):
                if k >= 4:
                    dve.wait_ge(norm_done, idx * KC + k - 3)
                for c in range(2):
                    cut = slice((1 - c) * T, (2 - c) * T)
                    ins = dve.scalar_tensor_tensor(NX2[:, k % 4, cut], XX[:, k, cut], A2[:, l, k, c:c + 1],
                                                   RS2[:, 1, cut], ALU.mult, ALU.mult)
                ins.then_inc(nx_done, 1)
                if k >= 2:
                    low(k - 2)
            low(KC - 2)
            low(KC - 1)

            def lows(name, count=8):
                b = st[name]
                looped(dve, b, count, 4, lambda i, j: next_low(b, i, j))

            lows("aqk")
            lows("av")
            next_low(st["ag"], 0, 0)
            next_low(st["ag"], 0, 1)
            chain(dve.memset(TG[0:4, :, :], 0.0))
            dve.wait_ge(gates_ready, l + 1)
            chain(dve.scalar_tensor_tensor(GF[0:4, :, :], GF[0:4, :, :], 0.0, CF[0:4, :, :], ALU.min, ALU.subtract))
            chain.wait()

            def scans(dst, src, other, op):
                chain(dve.tensor_tensor_scan(dst[0:4, 0, :], src[0:4, 0, :], other(slice(0, 2 * T), 0), 0.0, op, op))
                chain(dve.tensor_tensor_scan(dst[0:4, 1, 0:T][:, ::-1], src[0:4, 1, 0:T][:, ::-1],
                                             other(slice(0, T), 1)[:, ::-1], 0.0, op, op))
                chain.wait()
                chain(dve.tensor_tensor_scan(dst[0:4, 1, T:][:, ::-1], src[0:4, 1, T:][:, ::-1],
                                             other(slice(T, 2 * T), 1)[:, ::-1], dst[0:4, 1, 0:1], op, op))
                chain.wait()

            scans(CF, GF, lambda cut, d: TG[0:4, d, cut], ALU.add)
            chain(dve.tensor_tensor(GI[0:4, :, :], GI[0:4, :, :], CF[0:4, :, :], ALU.subtract))
            chain.wait()
            scans(CM, GI, lambda cut, d: GI[0:4, d, cut], ALU.max)
            chain(dve.tensor_tensor(TG[0:4, :, :], CF[0:4, :, :], CM[0:4, :, :], ALU.add))
            chain.wait()
            dve.tensor_scalar(CM[0:4, :, :], CM[0:4, :, :], -1.0, None, ALU.mult).then_inc(gates_summed, 1)
            dve.wait_ge(gates_turned, l + 1)
            dve.tensor_copy(UC[:, :, :], PS[:, 4, 0:32].rearrange("p (a b) -> p a b", a=8)).then_inc(gate_columns, 1)

            def mask(e):
                d = e % 2
                dve.wait_ge(row_read, 8 * l + e + 1)
                tri = const("upper" if d else "lower")[:, None, :].broadcast_to([P, 4 - 2 * l, P])
                if e >= 2:
                    dve.wait_ge(decayed, 8 * l + e - 1)
                dve.tensor_tensor(NMD[:, d, t0:].rearrange("p (a b) -> p a b", b=P),
                                  NMS[:, d, t0:].rearrange("p (a b) -> p a b", b=P), tri, ALU.add).then_inc(row_masked, 1)

            def denominator(e):
                dve.wait_ge(den_done, 8 * l + e + 1)
                dve.wait_ge(floor_read, 8 * l + e + 1)
                if e:
                    dve.wait_ge(post_done, 8 * l + e)
                chain(dve.tensor_tensor(DN[:, t0:], PS[:, 7, t0:], EMS[:, e % 2, t0:], ALU.max))
                chain.wait()
                dve.scalar_tensor_tensor(DN[:, t0:], PS[:, 7, t0:], -1.0, DN[:, t0:], ALU.mult,
                                         ALU.max).then_inc(den_read, 1)
                dve.wait_ge(den_read, 8 * l + e + 1)
                chain(dve.reciprocal(DN[:, t0:], DN[:, t0:]))

            def post(e):
                d, h = e % 2, e // 2
                dve.wait_ge(num_done, 8 * l + e + 1)
                chain.wait()
                for v in range(2):
                    y = YB[:, 2 * h + v, t0:]
                    if d == 0:
                        ins = dve.tensor_tensor(y, PS[:, 5 + v, t0:], DN[:, t0:], ALU.mult)
                    else:
                        if v:
                            chain.wait()
                        chain(dve.tensor_tensor(TM2[:, t0:], PS[:, 5 + v, t0:], DN[:, t0:], ALU.mult))
                        chain.wait()
                        ins = dve.tensor_tensor(y, y, TM2[:, t0:], ALU.add)
                        if v == 0:
                            chain(ins)
                ins.then_inc(post_done, 1)

            mask(0)
            for e in range(8):
                d = e % 2
                dve.wait_ge(decayed, 8 * l + e + 1)
                dve.wait_ge(a_scores, 4 * l + e // 2 + 1)
                for c in range(4):
                    for a, z in cover(d, c, l):
                        cut = slice(a * P, z * P)
                        ins = dve.tensor_tensor(EB[:, d, c, cut], EB[:, d, c, cut], PS[:, c, cut], ALU.mult)
                ins.then_inc(weighted, 1)
                if e:
                    post(e - 1)
                if e + 1 < 8:
                    mask(e + 1)
                denominator(e)
            post(7)

            def norm_groups(first, groups, wide, gain):
                for g in range(groups):
                    x = first + g
                    dve.wait_ge(g_roots, 12 * l + x + 1)
                    refine(NRM(x)[:, t0:], VRM(x)[:, t0:])
                    for w in range(wide):
                        y = YB[:, wide * g + w, t0:]
                        ins = dve.scalar_tensor_tensor(y, y, gain(wide * g + w), NRM(x)[:, t0:], ALU.mult, ALU.mult)
                    ins.then_inc(g_scaled, 1)

            at = PAR2["anorm"]
            norm_groups(0, 4, 2, lambda k: P2[:, l, at + k:at + k + 1])
            dve.wait_ge(g_scaled, 12 * l + 4)

            def output_gate(i, j):
                b = st["ao"]
                bank = (b + j) % 4
                dve.wait_ge(bank_read[bank], i + (earlier(b + j) + 1))
                y = YB[:, bass.ds(4 * i + j, 1), t0:]
                dve.tensor_tensor(y, y, SG[:, j % 2:j % 2 + 1, t0:], ALU.mult).then_inc(o_gated, 1)
                next_low(b, i, j)

            looped(dve, st["ao"], 8, 4, output_gate)

            def z_gate(name, branch):
                b = st[name]

                def body(i, j):
                    bank = (b + j) % 4
                    y = 4 * i + ((3 * l + branch) * KC + j)
                    dve.wait_ge(sig_done, y + 1)
                    dve.wait_ge(gated, y + BEGUN)
                    dve.tensor_tensor(SZ[:, 0, t0:], SG[:, j % 2, t0:], PS[:, bank, 0:n], ALU.mult).then_inc(bank_read[bank], 1)
                    dve.wait_ge(bank_read[bank], i + (earlier(b + j) + 1))
                    yb = YB[:, bass.ds(4 * i + j, 1), t0:]
                    dve.tensor_tensor(yb, yb, SZ[:, 0:1, t0:], ALU.mult).then_inc(gated, 1)
                    next_low(b, i, j)
                    dve.wait_ge(y_hi, y + 1)
                    dve.tensor_tensor(Y2[:, 1, bass.ds(4 * i + j, 1), t0:], yb,
                                      Y2[:, 0, bass.ds(4 * i + j, 1), t0:].bitcast(f32), ALU.subtract).then_inc(y_done, 1)

                looped(dve, b, 8, 4, body)

            def merge(name, branch):
                b = st[name]

                def body(i, j):
                    bank = (b + j) % 4
                    if j % 2:
                        done(b, i, j)
                        m = 2 * i + ((2 * l + branch - 1) * KC + j // 2)
                        before = (b + j - 1) % 4
                        dve.wait_ge(bank_read[before], i + (earlier(b + j - 1) + 1))
                        acc = ACC[:, bass.ds(2 * i + j // 2, 1), t0:]
                        if branch == 0:
                            dve.tensor_tensor(acc, SG[:, j // 2:j // 2 + 1, t0:], PS[:, bank:bank + 1, 0:n],
                                              ALU.mult).then_inc(bank_read[bank], 1)
                        else:
                            dve.wait_ge(acc_done, m + BEGUN)
                            dve.tensor_tensor(SZ[:, 0, t0:], SG[:, j // 2, t0:], PS[:, bank, 0:n],
                                              ALU.mult).then_inc(bank_read[bank], 1)
                            dve.wait_ge(bank_read[bank], i + (earlier(b + j) + 1))
                            dve.tensor_tensor(acc, acc, SZ[:, 0:1, t0:], ALU.add).then_inc(acc_done, 1)
                    next_low(b, i, j)

                looped(dve, b, 16, 4, body)

            z_gate("az", 0)
            merge("amerge", 0)
            lows("bq")
            lows("bk")
            sin = const("axsin", T)

            def rotated(x):
                src = (YB if x < 8 else KB)[:, x % 8, T:]
                dve.wait_ge(p_rotated, 16 * l + x + 1)
                dve.tensor_tensor(TS[:, x % 2, :], PS[:, 6 + x % 2, 0:T], sin, ALU.mult).then_inc(p_sine, 1)
                dve.wait_ge(p_sine, 16 * l + x + 1)
                dve.wait_ge(p_cosine, 16 * l + x + 1)
                dve.tensor_tensor(src, TC[:, x % 2, :], TS[:, x % 2, :], ALU.add).then_inc(p_done, 1)

            for x in range(16):
                a = t0 if x < 8 else 0
                whole = (YB if x < 8 else KB)[:, x % 8, a:]
                at = PAR2["qn" if x < 8 else "kn"]
                dve.wait_ge(p_roots, 16 * l + x + 1)
                refine(RB[:, x % 2, a:], VP[:, x % 2, a:], YS[:, x % 2, a:])
                dve.scalar_tensor_tensor(whole, whole, P2[:, l, at:at + 1], RB[:, x % 2, a:], ALU.mult,
                                         ALU.mult).then_inc(p_scaled, 1)
                if x:
                    rotated(x - 1)
                if x >= 6 and x % 4 == 2:
                    for j in range((x - 6) // 2, (x - 6) // 2 + 2):
                        next_low(st["bv"], 0, j)
            rotated(15)
            for j in range(6, 8):
                next_low(st["bv"], 0, j)
            steps, tb = tiles(l), tile_base(l)

            def top(f):
                h, q = steps[f]
                keys = 2 * T if q >= 2 else T
                c = f % 2
                dve.wait_ge(b_scores, tb + f + 1)
                chain(dve.reduce_max(BC[:, c, 0:2], PS[:, 2 * c:2 * c + 2, 0:keys], AX.X))
                chain.wait()
                dve.tensor_scalar(BC[:, c, 2:4], BC[:, c, 0:2], -0.125, None, ALU.mult).then_inc(b_max, 1)

            top(0)
            for f in range(len(steps)):
                if f + 1 < len(steps):
                    top(f + 1)
                h, q = steps[f]
                keys = 2 * T if q >= 2 else T
                c = f % 2
                dve.wait_ge(b_exped, tb + f + 1)
                chain(dve.reciprocal(BC[:, c, 4:6], BC[:, c, 4:6]))
                chain.wait()
                chain(dve.tensor_tensor(BC[:, c, 5:6], BC[:, c, 5:6], LM[:, 4 + l:5 + l], ALU.mult))
                chain(dve.tensor_scalar(PB[:, c, 0, 0:keys], PB[:, c, 0, 0:keys], BC[:, c, 4:5], None, ALU.mult))
                chain.wait()
                dve.scalar_tensor_tensor(PB[:, c, 0, 0:keys], PB[:, c, 1, 0:keys], BC[:, c, 5:6],
                                         PB[:, c, 0, 0:keys], ALU.mult, ALU.add).then_inc(b_weights, 1)
            norm_groups(4, 8, 1, lambda k: LM[:, 6 + l:7 + l])
            dve.wait_ge(g_scaled, 12 * l + 12)
            z_gate("bz", 1)
            merge("bmerge", 1)
            lows("cu")
            for p in parts(l):
                past = 8 * (p if l == 0 else 2)
                for x in range(8):
                    dve.wait_ge(dft2, past + x + 1)
                    both, sines = PS[:, 6 + x % 2, 1:P], SINES[:, x % 2, 0:P - 1]
                    chain(dve.tensor_copy(sines, PS[:, 6 + x % 2, T:T + P - 1]))
                    chain.wait()
                    dve.tensor_copy(YB[:, x, p * T:(p + 1) * T:P], PS[:, 6 + x % 2, 0:P + 1:P])
                    dve.tensor_tensor(YB[:, x, p * T + 1:p * T + P], both, sines, ALU.subtract)
                    dve.tensor_tensor(YB[:, x, p * T + P + 1:(p + 1) * T][:, ::-1], both, sines,
                                      ALU.add).then_inc(dft2_read, 1)
            dve.wait_ge(dft2_read, 16 + 8 * l)
            z_gate("cz", 2)
            merge("cmerge", 2)
            for k in range(KC):
                dve.wait_ge(acc_hi, l * KC + k + 1)
                dve.tensor_tensor(H2[:, 1, k, t0:], ACC[:, k, t0:], H2[:, 0, k, t0:].bitcast(f32),
                                  ALU.subtract).then_inc(a_done, 1)
            b = st["out"]

            def residual(i, j):
                done(b, i, j)
                bank = (b + j) % 4
                for p in parts(l):
                    x = XX[:, bass.ds(4 * i + j, 1), p * T:(p + 1) * T]
                    ins = dve.scalar_tensor_tensor(x, PS[:, bank:bank + 1, p * T - t0:(p + 1) * T - t0],
                                                   M2[:, l, bass.ds(4 * i + (16 + j), 1), 1 - p], x, ALU.mult, ALU.add)
                ins.then_inc(bank_read[bank], 1)
                next_low(b, i, j)

            if l == DEPTH - 1:
                for i in range(2):
                    for j in range(4):
                        residual(i, j)
            else:
                looped(dve, b, 8, 4, residual)

        for i in range(2):
            chain(dve.tensor_tensor(LT[:, i, :, :], LAM[:, :, 2 * i, :], LAM[:, :, 2 * i + 1, :], ALU.mult))
        chain.wait()
        dve.tensor_reduce(LR[:, :, :], LT, AX.X, ALU.add).then_inc(lam_r, 1)
        dve.wait_ge(lam_e, 1)
        chain(dve.tensor_tensor(LM[:, 4:6], LM[:, 2:4], LM[:, 0:2], ALU.subtract))
        chain.wait()
        for l in range(DEPTH):
            start = 0.8 - 0.6 * float(np.exp(-0.3 * l))
            chain(dve.tensor_scalar(LM[:, 4 + l:5 + l], LM[:, 4 + l:5 + l], -start, None, ALU.add))
            at = PAR2["subln"]
            chain(dve.tensor_scalar(LM[:, 6 + l:7 + l], P2[:, l, at:at + 1], 1.0 - start, None, ALU.mult))
        chain.wait()
        dve.wait_ge(consts2_in, 16)
        for l in range(DEPTH):
            layer(l)

    def finish(sp):
        for k in range(KC):
            u = stages(DEPTH - 1)["out"] + k
            sp.wait_ge(bank_read[u % 4], earlier(u) + 1)
        sp.dma_start(outT, X).then_inc(out_done, 16)
        sp.wait_ge(out_done, 16)

    @block.sync
    def _(sp):
        def modulation(q, i=0, step=4):
            if q >= 4:
                sp.wait_ge(mod_used, step * i + (q - 3))
            sp.dma_start(GRING[:, q % 4, :, :], mods[step * i + q]).then_inc(mod_full[q % 4], 16)

        def wide_modulation(w, i=0):
            if w >= 2:
                sp.wait_ge(wide_used, 4 * i + (2 * w - 2))
            else:
                sp.wait_ge(mod_used, FIRST_MODS - 3 + w)
            sp.dma_start(GRING[:, w % 2, :, :], mods[2 * i + (FIRST_MODS + w)]).then_inc(wide_full[w % 2], 16)

        def modulations(first, end):
            with sp.Fori(0, (end - first) // 4) as i:
                for q in range(first, first + 4):
                    modulation(q, i)
            for q in range(first + (end - first) // 4 * 4, end):
                modulation(q)

        def unit(v, i=0):
            for half in range(2):
                g = 2 * v + half
                if g >= 4:
                    sp.wait_ge(lo_done[half], 4 * i + (v - 1))
                cut = slice(half * KC // 2, (half + 1) * KC // 2)
                sp.dma_start(RAW[:, g % 4, :, :], stream[4 * i + v, :, cut, :]).then_inc(raw_full[g % 4], 16)

        def units(first, end, beside=None):
            with sp.Fori(0, (end - first) // 4) as i:
                for j in range(4):
                    unit(first + j, i)
                    if beside is not None:
                        modulation(beside + j, i)

        sp.dma_start(CC[:, :, :], ccols).then_inc(c_in, 16)
        sp.dma_start(C[:, 0:COMMON_W], consts[:, 0:COMMON_W]).then_inc(common_in, 16)
        for q in range(4):
            modulation(q)
        for v in range(2):
            unit(v)
        for dst, src in ((P1[:, :, :], par1), (X, xT), (C[:, COMMON_W:COMMON_W + FIRST_W], consts[:, COMMON_W:])):
            sp.dma_start(dst, src).then_inc(consts_in, 16)
        for v in range(2, 4):
            unit(v)
        q = 16 + 3
        modulations(4, q)
        sp.dma_start(P2[:, :, :], par2).then_inc(later_in, 16)
        u = 4 + V_UNITS
        units(4, u)
        for n in (QK_UNITS, WO_UNITS, FF_MODS):
            units(u, u + n, q)
            u, q = u + n, q + n
        units(u, u + FF_UNITS - FF_MODS)
        u += FF_UNITS - FF_MODS
        units(u, u + DOWN_UNITS - 4, q)
        u, q = u + DOWN_UNITS - 4, q + DOWN_UNITS - 4
        modulation(q)
        units(u, u + 4)
        u += 4
        wide_modulation(0)
        for v in range(u, u + 4):
            unit(v)
            if v % 2:
                wide_modulation((v - u + 1) // 2)
        with sp.Fori(0, PER // 4 - 2) as i:
            for j in range(4):
                unit(u + 4 + j, i)
                if j % 2:
                    wide_modulation(2 + (j + 1) // 2, i)
        u += PER - 4
        for v in range(u, u + 6):
            unit(v)
            if v == u + 1:
                wide_modulation(WIDE_MODS - 1)
        sp.wait_ge(wide_used, 2 * WIDE_MODS)
        sp.dma_start(XX[:, :, 0:T], ctxT).then_inc(later_in, 16)
        sp.dma_start(LAM, lam).then_inc(later_in, 16)
        for v in range(u + 6, u + 8):
            unit(v)
        units(u + 8, total)
        finish(sp)

    @block.gpsimd
    def _(pool):
        def rope(l):
            cos = const("cos", T)[:, None, :].broadcast_to([P, 2, T])
            if l == 0:
                pool.wait_ge(consts_in, 16 * 3)
            for g in range(6):
                pool.wait_ge(rms_done, 9 * l + max(1, min(9, 2 * g - 1)))
                pool.tensor_tensor(RO[:, 2 * g:2 * g + 2, :], F[:, 2 * g:2 * g + 2, :], cos,
                                   ALU.mult).then_inc(rope_cosine, 1)

        cut = slice(KC // 2, KC)

        def low(u, i=0):
            pool.wait_ge(hi_done, 8 * i + (2 * u + 2))
            pool.tensor_tensor(WL[:, u % 4, cut, :], RAW[:, (2 * u + 1) % 4, :, :],
                               WH[:, u % 4, cut, :].bitcast(f32), ALU.subtract).then_inc(lo_done[1], 1)

        def lows(first, end):
            rounds = (end - first) // 4
            if rounds:
                with pool.Fori(0, rounds) as i:
                    for u in range(first, first + 4):
                        low(u, i)
            for u in range(first + 4 * rounds, end):
                low(u)

        def hidden(l, first):
            with pool.Fori(0, FF_UNITS // 4) as i:
                for j in range(4):
                    low(first + j, i)
                    if j % 2:
                        pool.wait_ge(ff_hi, 2 * i + (l * FC + j // 2 + 1))
                        chunk = bass.ds(2 * i + j // 2, 1)
                        pool.tensor_tensor(HID[:, 1, chunk, :], GATE[:, 2:3, :], HID[:, 0, chunk, :].bitcast(f32),
                                           ALU.subtract).then_inc(ff_done, 1)

        first = 0
        for l in range(DEPTH):
            end = l * PER + V_UNITS + QK_UNITS + 4
            lows(first, end)
            rope(l)
            if l == DEPTH - 1:
                pool.wait_ge(o_ready, 4 * DEPTH)
                pool.dma_start(C[:, COMMON_W:COMMON_W + SECOND_W], consts2).then_inc(consts2_in, 16)
            lows(end, end + WO_UNITS)
            hidden(l, end + WO_UNITS)
            first = end + WO_UNITS + FF_UNITS
        second_pool(pool, lows, first)

    @block.tensor
    def _(pe):
        def spread_vector(v):
            if v:
                pe.wait_ge(spread_read, v)
            for k in range(KC):
                out = PS[:, 4 + k // 4, (k % 4) * P:(k % 4 + 1) * P]
                last = pe.matmul(out, CA[:, v, k:k + 1].broadcast_to([P, P]), ident, start=True, stop=True)
            last.then_inc(spread, 1)

        def unit_wait(base, i, j):
            u = base + j
            for half in range(2):
                pe.wait_ge(lo_done[half], 4 * i + (u + 1))
            if u >= 4:
                pe.wait_ge(bank_read[u % 4], i + earlier(u))
            return u

        def feature_unit(base, i, j, moving, n, ready=None):
            u = unit_wait(base, i, j)
            for k in range(KC):
                if ready is not None:
                    pe.wait_ge(ready[0], ready[1] + k + 1)
                out = PS[:, u % 4, 0:n]
                pe.matmul(out, WH[:, u % 4, k, :], moving[:, 0, k, :], start=(k == 0), stop=False)
                pe.matmul(out, WH[:, u % 4, k, :], moving[:, 1, k, :], start=False, stop=False)
                last = pe.matmul(out, WL[:, u % 4, k, :], moving[:, 0, k, :], start=False, stop=(k == KC - 1))
            last.then_inc(unit_done, 1)

        def token_pair(base, i, j, still, first, end, ready=None, only=None):
            u, half = base + j, (end - first) // 2
            blocks = range(end - first) if only is None else [only]
            for part in range(2):
                pe.wait_ge(lo_done[part], 4 * i + (u + 2))
            for x in (u, u + 1):
                if x >= 4:
                    pe.wait_ge(bank_read[x % 4], i + earlier(x))
            for b in blocks:
                at = (b % half) * 2 * P
                out = PS[:, (u + b // half) % 4, at:at + 2 * P].rearrange("p (a c) -> p a c", a=2)
                cut = slice((first + b) * P, (first + b + 1) * P)
                both = slice(u % 4, u % 4 + 2)
                for k in range(KC):
                    if ready is not None:
                        pe.wait_ge(ready[0], ready[1] + k + 1)
                    pe.matmul(out, still[:, 0, k, cut], WH[:, both, k, :], start=(k == 0), stop=False)
                    pe.matmul(out, still[:, 0, k, cut], WL[:, both, k, :], start=False, stop=False)
                    last = pe.matmul(out, still[:, 1, k, cut], WH[:, both, k, :], start=False,
                                     stop=(k == KC - 1))
            if end - first - 1 in blocks:
                last.then_inc(unit_done, 2)

        def down_unit(l, base, i, j):
            u, b = base + j, j // 3
            for half in range(2):
                pe.wait_ge(lo_done[half], 12 * i + (u + 1))
            if j % 3 == 0:
                pe.wait_ge(bank_read[b], i + earlier(base))
            for k in range(KC if j % 3 < 2 else FC - 2 * KC):
                kk = (j % 3) * KC + k
                pe.wait_ge(ff_done, l * FC + kk + 1 + BEGUN)
                pe.matmul(PS[:, b, 0:T], WH[:, u % 4, k, :], HID[:, 0, kk, :], start=(kk == 0), stop=False)
                pe.matmul(PS[:, b, 0:T], WH[:, u % 4, k, :], HID[:, 1, kk, :], start=False, stop=False)
                last = pe.matmul(PS[:, b, 0:T], WL[:, u % 4, k, :], HID[:, 0, kk, :], start=False,
                                 stop=(kk == FC - 1))
            last.then_inc(unit_done, 1)

        second = second_pe(pe, feature_unit, token_pair)

        def first_layer(l):
            base = l * PER
            def norm_sums(half):
                for k in range(KC):
                    pe.wait_ge(sq_done, (2 * l + half) * KC + k + 1)
                    last = pe.matmul(PS[:, 6, 0:T], ones, SQ[:, k, :], start=(k == 0), stop=(k == KC - 1))
                last.then_inc(sum_done, 1)

            if l:
                spread_vector(1)
            norm_sums(0)
            if l:
                spread_vector(2)
            for j in range(0, V_UNITS, 2):
                token_pair(base, 0, j, H1, 0, 2, (norm_done, 2 * l * KC))
            b = base + V_UNITS
            looped(pe, b, QK_UNITS, 4, lambda i, j: feature_unit(b, i, j, H1, T))
            for g in range(5):
                pe.wait_ge(rsq_done, 5 * l + g + 1)
                if g >= 2:
                    pe.wait_ge(ms_read, 5 * l + g - 1)
                n = T if g == 4 else 2 * T
                pe.matmul(PS[:, 4 + g % 2, 0:n], heads, TMP[:, 2 * g:2 * g + n // T, :],
                          start=True, stop=True).then_inc(ms_done, 1)
            for g in range(6):
                pe.wait_ge(rms_done, 9 * l + max(1, min(9, 2 * g - 1)))
                if g >= 2:
                    pe.wait_ge(rot_read, 6 * l + g - 1)
                else:
                    pe.wait_ge(ms_read, 5 * l + 5)
                pe.matmul(PS[:, 4 + g % 2, 0:2 * T], const("rot"), F[:, 2 * g:2 * g + 2, :],
                          start=True, stop=True).then_inc(rot_done, 1)
            pe.wait_ge(rope_done, 6 * (l + 1))

            def score(s):
                n = s % 2
                w = P * (n + 1)
                if s >= 2:
                    pe.wait_ge(scores_read, 10 * l + s - 1)
                for p, h in enumerate(PLACE):
                    if s < 2:
                        q, k = h // 2, 2
                    elif s < 4:
                        q, k = 3 + h // 2, 5
                    elif s < 8:
                        g = (s - 4) // 2
                        q, k = 6 + 2 * g + h // 2, 10 + g
                    else:
                        q, k = 12 + h // 2, 14 + h // 2
                    r = slice(64 * (h % 2), 64 * (h % 2) + 64)
                    out = PS[:, 2 * (s % 2):2 * (s % 2) + 2, :].rearrange("p a (b t) -> p (a b) t", b=2)[:, p, 0:w]
                    last = pe.matmul(out, F[r, q, n * P:(n + 1) * P], F[r, k, 0:w], start=True, stop=True)
                last.then_inc(scores, 1)

            def turn(s):
                a = s - 2
                n = a % 2
                if s < 8:
                    pe.wait_ge(probs, 6 * l + a + 1)
                else:
                    pe.wait_ge(sticks, 2 * l + s - 8 + 1)
                if a:
                    pe.wait_ge(pt_ready, 8 * l + a)
                for kb in range(n + 1):
                    for h in range(4):
                        last = pe.transpose(PS[:, 4 + kb, h * P:(h + 1) * P],
                                            PR[:, s % 2, h, kb * P:(kb + 1) * P], ident)
                last.then_inc(turned, 1)

            def weigh(g):
                pe.wait_ge(pt_ready, 8 * l + 2 * g + 2)
                if g:
                    pe.wait_ge(o_ready, 4 * l + g)
                for p, h in sorted(enumerate(PLACE), key=lambda x: x[1]):
                    at = (0, 320, 384, 64 + h * 64)[g]
                    rows = slice(64 * (h % 2), 64 * (h % 2) + 64)
                    out = PS[rows, 6, (h // 2) * T:(h // 2 + 1) * T]
                    pe.matmul(out, V[:, 0, at:at + 64], PT[:, g % 2, 0:2, p, :], start=True, stop=False)
                    last = pe.matmul(out[:, P:T], V[:, 1, at:at + 64], PT[:, g % 2, 2, p, :],
                                     start=False, stop=True)
                last.then_inc(pv_done, 1)

            score(0)
            score(1)
            score(2)
            score(3)
            for s in range(2, 10):
                if s + 2 < 10:
                    score(s + 2)
                turn(s)
                if s % 2:
                    weigh((s - 2) // 2)
            for g in range(4):
                pe.wait_ge(out_squared, 4 * l + g + 1)
                pe.matmul(PS[:, g, 0:2 * T], heads, SQ[:, 2 * g:2 * g + 2, :], start=True, stop=True).then_inc(out_sums, 1)
            b = base + V_UNITS + QK_UNITS
            looped(pe, b, WO_UNITS, 4, lambda i, j: feature_unit(b, i, j, OS, T, (out_lo, l * KC)))
            norm_sums(1)
            b2 = b + WO_UNITS

            looped(pe, b2, FF_UNITS, 4, lambda i, j: feature_unit(b2, i, j, H1, T, (norm_done, (2 * l + 1) * KC)))
            b3 = b2 + FF_UNITS
            looped(pe, b3, DOWN_UNITS, 12, lambda i, j: down_unit(l, b3, i, j))

        pe.wait_ge(c_done, 1)
        pe.wait_ge(common_in, 16)
        spread_vector(0)
        for l in range(DEPTH):
            first_layer(l)
        for l in range(DEPTH):
            second(l)

    @block.scalar
    def _(act):
        chain = Chain(act, act_chain)

        def split_high(u, i, rounds):
            for half in range(2):
                g = 2 * u + half
                cut = slice(half * KC // 2, (half + 1) * KC // 2)
                act.wait_ge(raw_full[g % 4], 32 * rounds * i + 16 * (g // 4 + 1))
                act.activation(WH[:, u % 4, cut, :], RAW[:, g % 4, :, :], ACT.Copy).then_inc(hi_done, 1)

        def next_high(base, i, j, rounds=1):
            act.wait_ge(unit_done, 4 * rounds * i + (base + j + 1))
            if isinstance(i, int) and 4 * rounds * i + base + j + 4 >= total:
                return
            split_high(base + j + 4, i, rounds)

        def done(base, i, j, rounds=1):
            act.wait_ge(unit_done, 4 * rounds * i + (base + j + 1))

        def exponentials():
            act.preload_act_table_set("natural_log_exp_and_others")

        def sigmoids():
            act.preload_act_table(ACT.Sigmoid)

        def inverse_root(y, v, sums, scale, read, done, square=None):
            ins = act.activation(v, sums, ACT.Identity, bias=EPSC[:, 0:1], scale=scale)
            if read is None:
                chain(ins)
                chain.wait()
            else:
                ins.then_inc(read[0], 1)
                act.wait_ge(read[0], read[1])
            chain(act.activation(y, v, ACT.Ln))
            chain.wait()
            if square is None:
                act.activation(y, y, ACT.Exp, scale=-0.5).then_inc(done, 1)
            else:
                chain(act.activation(y, y, ACT.Exp, scale=-0.5))
                chain.wait()
                act.activation(square, y, ACT.Square).then_inc(done, 1)

        def norm(l, half):
            for k in range(KC):
                if half:
                    act.wait_ge(bank_read[k % 4], earlier(l * PER + V_UNITS + QK_UNITS + k) + 1)
                elif l:
                    act.wait_ge(bank_read[k % 4], earlier(l * PER - DOWN_UNITS) + k // 4 + 1)
                act.activation(SQ[:, k, :], X[:, k, :], ACT.Square).then_inc(sq_done, 1)
            act.wait_ge(sum_done, 2 * l + half + 1)
            inverse_root(RS[:, 1, :], RS[:, 0, :], PS[:, 6, 0:T], 1.0 / D, None, rstd_done)
            for k in range(KC):
                act.wait_ge(nx_done, (2 * l + half) * KC + k + 1)
                at = 24 * half + k
                act.activation(H1[:, 0, k, :], NX[:, k % 4, :], ACT.Identity,
                               bias=M1[:, l, at:at + 1]).then_inc(nhi_done, 1)

        def first_layer(l):
            base = l * PER
            norm(l, 0)

            for j in range(V_UNITS):
                done(base, 0, j)
                act.activation(V[:, j % 2, (j // 2) * 2 * P:(j // 2 + 1) * 2 * P], PS[:, j, 0:2 * P],
                               ACT.Copy).then_inc(bank_read[j], 1)
                next_high(base, 0, j)
            b = base + V_UNITS

            def features(i, j):
                done(b, i, j)
                act.activation(F[:, bass.ds(4 * i + j, 1), :], PS[:, j:j + 1, 0:T],
                               ACT.Copy).then_inc(bank_read[j], 1)
                next_high(b, i, j)

            looped(act, b, QK_UNITS, 4, features)
            for j in range(4):
                act.wait_ge(bank_read[j], earlier(b + QK_UNITS + j))
            for g in range(5):
                n = 1 if g == 4 else 2
                act.activation(TMP[:, 2 * g:2 * g + n, :], F[:, 3 + 2 * g:3 + 2 * g + n, :],
                               ACT.Square).then_inc(rsq_done, 1)
            for g in range(5):
                n = 1 if g == 4 else 2
                act.wait_ge(ms_done, 5 * l + g + 1)
                inverse_root(TMP[:, 2 * g:2 * g + n, :], VM[:, 2 * g:2 * g + n, :],
                             PS[:, 4 + g % 2, 0:n * T].rearrange("p (a b) -> p a b", a=n), 1.0 / 64,
                             (ms_read, 5 * l + g + 1), rms_roots)

            def stats(s):
                return 8 + 16 * (s % 2)

            def exps(s):
                a, w = s - 2, P * (s % 2 + 1)
                if a >= 2:
                    act.wait_ge(turned, 8 * l + a - 1)
                if s < 8:
                    act.wait_ge(masked, 6 * l + a + 1)
                    c = stats(s)
                    if s >= 4:
                        act.activation(COL[:, 40 + 4 * (s % 2):44 + 4 * (s % 2)],
                                       COL[:, 48 + 4 * (s % 2):52 + 4 * (s % 2)], ACT.Exp)
                    for h in range(4):
                        last = act.activation(PR[:, s % 2, h, 0:w], SM[:, s % 2, h, 0:w], ACT.Exp,
                                              bias=COL[:, c + 4 + h:c + 5 + h], scale=0.125,
                                              accum_out=COL[:, c + 8 + h:c + 9 + h])
                    last.then_inc(exped, 1)
                else:
                    act.wait_ge(scores_read, 10 * l + s + 1)
                    dst = PR[:, s % 2, :, 0:w]
                    chain(act.activation(dst, SM[:, s % 2, :, 0:w], ACT.Abs))
                    chain.wait()
                    chain(act.activation(dst, dst, ACT.Exp, scale=-1.0))
                    chain.wait()
                    act.activation(dst, dst, ACT.Ln, bias=EPSC[:, 1:2]).then_inc(stick_logs, 1)

            exps(2)
            for s in range(2, 10):
                a, g, n = s - 2, (s - 2) // 2, s % 2
                w = P * (n + 1)
                if s + 1 < 10:
                    exps(s + 1)
                if s >= 8:
                    act.wait_ge(stick_sums, 2 * l + s - 8 + 1)
                    act.activation(PR[:, n, :, 0:w], SM[:, n, :, 0:w], ACT.Exp).then_inc(sticks, 1)
                act.wait_ge(turned, 8 * l + a + 1)
                if g >= 2:
                    act.wait_ge(pv_done, 4 * l + g - 1)
                if n == 0:
                    act.activation(PT[:, g % 2, 0, :, :], PS[:, 4, :].rearrange("p (a b) -> p a b", a=4),
                                   ACT.Copy).then_inc(pt_ready, 1)
                else:
                    act.activation(PT[:, g % 2, 1:3, :, :],
                                   PS[:, 4:6, :].rearrange("p k (a b) -> p k a b", a=4),
                                   ACT.Copy).then_inc(pt_ready, 1)
                    o = (0, 4, 6, 2)[g]
                    act.wait_ge(pv_done, 4 * l + g + 1)
                    act.activation(O[:, o:o + 2, :], PS[:, 6, :].rearrange("p (a b) -> p a b", a=2),
                                   ACT.Copy).then_inc(o_ready, 1)
            act.wait_ge(o_ready, 4 * l + 4)
            for g in range(4):
                act.activation(SQ[:, 2 * g:2 * g + 2, :], O[:, 2 * g:2 * g + 2, :], ACT.Square).then_inc(out_squared, 1)
            for g in range(4):
                act.wait_ge(out_sums, 4 * l + g + 1)
                inverse_root(RSO[:, 2 * g:2 * g + 2, :], VO[:, 2 * g:2 * g + 2, :],
                             PS[:, g, :].rearrange("p (a b) -> p a b", a=2), 1.0 / 64, None, out_roots)
            for k in range(KC):
                act.wait_ge(out_scaled, l * KC + k + 1)
                act.activation(OS[:, 0, k, :], GATE[:, k % 4, :], ACT.Copy).then_inc(out_hi, 1)
            b = b + QK_UNITS
            looped(act, b, WO_UNITS, 4, lambda i, j: next_high(b, i, j))
            norm(l, 1)
            b2 = b + WO_UNITS

            def hidden(i, j):
                done(b2, i, j)
                if j % 2 == 0:
                    act.activation(GATE[:, 0, :], PS[:, j, 0:T], ACT.Sigmoid).then_inc(ff_sigmoid, 1)
                    next_high(b2, i, j)
                else:
                    next_high(b2, i, j)
                    act.wait_ge(bank_read[j], i + (earlier(b2 + j) + 1))
                    act.activation(HID[:, 0, bass.ds(2 * i + j // 2, 1), :], GATE[:, 2:3, :],
                                   ACT.Copy).then_inc(ff_hi, 1)

            sigmoids()
            looped(act, b2, FF_UNITS, 4, hidden)
            exponentials()
            b3 = b2 + FF_UNITS
            looped(act, b3, DOWN_UNITS, 12, lambda i, j: next_high(b3, i, j, 3))

        exponentials()
        act.wait_ge(c_in, 16)
        act.activation(CT[:, 0, :, :], CC[:, :, :], ACT.Exp, scale=-1.0).then_inc(c_exped, 1)
        act.wait_ge(c_exped, 2)
        for u in range(4):
            split_high(u, 0, 1)
        act.wait_ge(consts_in, 16 * 3)
        for l in range(DEPTH):
            first_layer(l)
        act.wait_ge(later_in, 16 * 3)
        second_act(act, done, next_high, exponentials, sigmoids, inverse_root, chain)

    @block.vector
    def _(dve):
        chain = Chain(dve, dve_chain)

        def split_low(u, i, rounds):
            dve.wait_ge(hi_done, 8 * rounds * i + (2 * u + 1))
            cut = slice(0, KC // 2)
            dve.tensor_tensor(WL[:, u % 4, cut, :], RAW[:, 2 * u % 4, :, :], WH[:, u % 4, cut, :].bitcast(f32),
                              ALU.subtract).then_inc(lo_done[0], 1)

        def next_low(base, i, j, rounds=1):
            if isinstance(i, int) and 4 * rounds * i + base + j + 4 >= total:
                return
            split_low(base + j + 4, i, rounds)

        def done(base, i, j, rounds=1):
            dve.wait_ge(unit_done, 4 * rounds * i + (base + j + 1))

        def refine(y, v, square=None):
            if square is None:
                chain(dve.tensor_tensor(v, v, y, ALU.mult))
                chain.wait()
                chain(dve.scalar_tensor_tensor(v, v, -0.5, y, ALU.mult, ALU.mult))
            else:
                chain(dve.scalar_tensor_tensor(v, v, -0.5, square, ALU.mult, ALU.mult))
            chain.wait()
            chain(dve.scalar_tensor_tensor(y, v, 1.5, y, ALU.add, ALU.mult))
            chain.wait()

        def norm(l, half):
            dve.wait_ge(rstd_done, 2 * l + half + 1)
            refine(RS[:, 1, :], RS[:, 0, :])

            def low(k):
                dve.wait_ge(nhi_done, (2 * l + half) * KC + k + 1)
                at = 24 * half + k
                dve.scalar_tensor_tensor(H1[:, 1, k, :], NX[:, k % 4, :], M1[:, l, at:at + 1],
                                         H1[:, 0, k, :].bitcast(f32), ALU.add, ALU.subtract).then_inc(norm_done, 1)

            for k in range(KC):
                if k >= 4:
                    dve.wait_ge(norm_done, (2 * l + half) * KC + k - 3)
                dve.scalar_tensor_tensor(NX[:, k % 4, :], X[:, k, :], A1[:, l, half, k:k + 1], RS[:, 1, :],
                                         ALU.mult, ALU.mult).then_inc(nx_done, 1)
                if k >= 2:
                    low(k - 2)
            low(KC - 2)
            low(KC - 1)

        def product(slot, c, sums, done, spare=None):
            for p in range(SUMS):
                w = GRING[:, slot, p, :]
                last = dve.scalar_tensor_tensor(w if spare is None else GRING[:, spare, p, :], w, 1.0,
                                                CB[:, c, p // 2, p % 2 * P:(p % 2 + 1) * P], ALU.mult, ALU.mult,
                                                accum_out=sums(p))
            last.then_inc(done, 1)

        def modulate(q, i=0, step=4):
            dve.wait_ge(mod_full[q % 4], 4 * step * i + 16 * (q // 4 + 1))
            product(q % 4, 0, lambda p: MV[:, bass.ds(step * i + q, 1), p], mod_used)

        def modulate2(x, i=0, step=4):
            w = x // 2
            dve.wait_ge(wide_full[w % 2], 4 * step * i + 16 * (w // 2 + 1))
            if x >= 2:
                dve.wait_ge(wide_used, step * i + (x - 1))
            product(w % 2, x % 2, lambda p: MV2[:, bass.ds(step // 2 * i + w, 1), x % 2, p], wide_used,
                    None if x % 2 else 2)

        def beside(u, i, j, step=4):
            if u >= PER:
                modulate2(u - PER + j, i, step)
            elif u >= PER - DOWN_UNITS:
                modulate(FIRST_MODS - PER + u + j, i, step)
            elif V_UNITS <= u < V_UNITS + QK_UNITS + WO_UNITS + FF_MODS:
                modulate(16 - V_UNITS + u + j, i, step)

        def copy_vector(v):
            dve.wait_ge(spread, v + 1)
            dve.tensor_copy(CB[:, max(v - 1, 0)], PS[:, 4:6, :].rearrange("p a (b c) -> p (a b) c", c=T)).then_inc(spread_read, 1)
            dve.wait_ge(spread_read, v + 1)

        def columns(l, at, n):
            q = l * MOD1 + at
            dve.wait_ge(mod_used, q + n)
            bias = PAR1["bmod"] + at
            chain(dve.tensor_reduce(M1[:, l, at:at + n], MV[:, q:q + n, :], AX.X, ALU.add))
            chain.wait()
            chain(dve.tensor_tensor(M1[:, l, at:at + n], M1[:, l, at:at + n], P1[:, l, bias:bias + n], ALU.add))
            chain.wait()
            for half in range(2):
                s = 24 * half + KC
                if at <= s and s + KC <= at + n:
                    g = PAR1["ln2" if half else "ln1"]
                    chain(dve.scalar_tensor_tensor(A1[:, l, half, :], M1[:, l, s:s + KC], 1.0,
                                                   P1[:, l, g:g + KC], ALU.add, ALU.mult))
                    chain.wait()

        def columns2():
            dve.wait_ge(wide_used, 2 * WIDE_MODS)
            m2 = M2[:, :, :, :].rearrange("p l m c -> p (l m) c")
            chain(dve.tensor_reduce(m2, MV2, AX.X, ALU.add))
            chain.wait()
            for c in range(2):
                ins = dve.tensor_tensor(M2[:, :, :, c], M2[:, :, :, c],
                                        P2[:, :, PAR2["bada"]:PAR2["bada"] + MOD2], ALU.add)
            ins.then_inc(mod_read, 1)
            dve.wait_ge(mod_read, 1)
            for c in range(2):
                chain(dve.scalar_tensor_tensor(A2[:, :, :, c], M2[:, :, KC:2 * KC, c], 1.0,
                                               P2[:, :, PAR2["norm"]:PAR2["norm"] + KC], ALU.add, ALU.mult))
            chain.wait()

        def first_layer(l):
            base = l * PER
            if l:
                dve.wait_ge(mod_used, FIRST_MODS)
                copy_vector(1)
            norm(l, 0)
            if l:
                copy_vector(2)
            for j in range(V_UNITS):
                beside(base, 0, j)
                next_low(base, 0, j)
            b = base + V_UNITS

            def queries(i, j):
                beside(b, i, j)
                next_low(b, i, j)

            looped(dve, b, QK_UNITS, 4, queries)
            if l == 0:
                columns(0, 16, 16)
            for j in range(4):
                dve.wait_ge(bank_read[j], earlier(b + QK_UNITS + j))
            for n in range(2):
                chain(dve.tensor_scalar(COL[:, 4 * n:4 * n + 4], V[:, n, 448:452], 1.0 / 16, None, ALU.mult))
            for c in range(9):
                if c % 2 == 0:
                    n = 1 if c == 8 else 2
                    dve.wait_ge(rms_roots, 5 * l + c // 2 + 1)
                    refine(TMP[:, c:c + n, :], VM[:, c:c + n, :])
                g = PAR1["gain"] + c
                dve.scalar_tensor_tensor(F[:, 3 + c, :], F[:, 3 + c, :], P1[:, l, g:g + 1], TMP[:, c, :],
                                         ALU.mult, ALU.mult).then_inc(rms_done, 1)
            sin = const("sin", T)[:, None, :].broadcast_to([P, 2, T])
            for g in range(6):
                dve.wait_ge(rot_done, 6 * l + g + 1)
                dve.tensor_tensor(SN[:, g % 2, :, :], PS[:, 4 + g % 2, :].rearrange("p (a b) -> p a b", a=2),
                                  sin, ALU.mult).then_inc(rot_read, 1)
                dve.wait_ge(rot_read, 6 * l + g + 1)
                dve.wait_ge(rope_cosine, 6 * l + g + 1)
                dve.tensor_tensor(F[:, 2 * g:2 * g + 2, :], RO[:, 2 * g:2 * g + 2, :], SN[:, g % 2, :, :],
                                  ALU.add).then_inc(rope_done, 1)

            def banks(s):
                return PS[:, 2 * (s % 2):2 * (s % 2) + 2, :].rearrange("p a (b t) -> p (a b) t", b=2)

            dve.wait_ge(rope_done, 6 * l + 6)
            for n in range(2):
                w = P * (n + 1)
                dve.wait_ge(scores, 10 * l + n + 1)
                for p, h in enumerate(PLACE):
                    ins = dve.tensor_scalar(SM[:, n, p, 0:w], banks(n)[:, p, 0:w], 0.0,
                                            COL[:, 4 * n + h:4 * n + h + 1], ALU.max, ALU.mult)
                ins.then_inc(scores_read, 1)
                dve.wait_ge(scores_read, 10 * l + n + 1)
                chain(dve.tensor_reduce(WK[:, n, 0:w], SM[:, n, :, 0:w].rearrange("p h t -> p t h"),
                                        AX.X, ALU.add))
            chain.wait()
            causal = const("causal", 2 * T).rearrange("p (n t) -> p n t", n=2)
            for n in range(2):
                w = P * (n + 1)
                chain(dve.tensor_tensor(WK[:, n, 0:w], WK[:, n, 0:w], causal[:, n, 0:w], ALU.add))
            for r in range(TOPK // 8):
                chain.wait()
                for n in range(2):
                    chain(dve.max(COL[:, 40 + 8 * n:48 + 8 * n], WK[:, n, 0:P * (n + 1)]))
                chain.wait()
                for n in range(2):
                    w = P * (n + 1)
                    chain(dve.match_replace(WK[:, n, 0:w], COL[:, 40 + 8 * n:48 + 8 * n], WK[:, n, 0:w], GONE))
            chain.wait()
            for n in range(2):
                w = P * (n + 1)
                chain(dve.tensor_scalar(SEL[:, n, 0:w], WK[:, n, 0:w], GONE * 0.5, -BIG, ALU.is_gt, ALU.mult))
            chain.wait()
            for n in range(2):
                w = P * (n + 1)
                chain(dve.tensor_tensor(SEL[:, n, 0:w], SEL[:, n, 0:w], causal[:, n, 0:w], ALU.add))
            chain.wait()
            band = const("band", 2 * T).rearrange("p (n t) -> p n t", n=2)
            strict = const("strict", 2 * T).rearrange("p (n t) -> p n t", n=2)

            def begin(s):
                a, n = s - 2, s % 2
                w, c = P * (n + 1), 8 + 16 * n
                sm = SM[:, n, :, 0:w]
                dve.wait_ge(scores, 10 * l + s + 1)
                if s >= 8:
                    m = strict[:, n, 0:w][:, None, :].broadcast_to([P, 4, w])
                    dve.scalar_tensor_tensor(sm, banks(s)[:, :, 0:w], 0.125, m, ALU.mult, ALU.add).then_inc(scores_read, 1)
                    return
                m = (SEL if s < 4 else band)[:, n, 0:w][:, None, :].broadcast_to([P, 4, w])
                dve.tensor_tensor(sm, banks(s)[:, :, 0:w], m, ALU.add).then_inc(scores_read, 1)
                dve.wait_ge(scores_read, 10 * l + s + 1)
                chain(dve.reduce_max(COL[:, c:c + 4], sm, AX.X))
                chain.wait()
                if s < 4:
                    dve.tensor_scalar(COL[:, c + 4:c + 8], COL[:, c:c + 4], -0.125, None, ALU.mult).then_inc(masked, 1)
                else:
                    k = PAR1["sinks"] + 4 * ((s - 4) // 2)
                    sink = P1[:, l, k:k + 4]
                    chain(dve.scalar_tensor_tensor(COL[:, c:c + 4], COL[:, c:c + 4], 0.125, sink, ALU.mult, ALU.max))
                    chain.wait()
                    dve.tensor_scalar(COL[:, c + 4:c + 8], COL[:, c:c + 4], -1.0, None, ALU.mult)
                    dve.tensor_tensor(COL[:, 48 + 4 * n:52 + 4 * n], sink, COL[:, c:c + 4],
                                      ALU.subtract).then_inc(masked, 1)

            def end(s):
                a, n = s - 2, s % 2
                w, c = P * (n + 1), 8 + 16 * n
                if s < 8:
                    dve.wait_ge(exped, 6 * l + a + 1)
                    if s >= 4:
                        chain(dve.tensor_tensor(COL[:, c + 8:c + 12], COL[:, c + 8:c + 12],
                                                COL[:, 40 + 4 * n:44 + 4 * n], ALU.add))
                        chain.wait()
                    chain(dve.reciprocal(COL[:, c + 12:c + 16], COL[:, c + 8:c + 12]))
                    chain.wait()
                    r = COL[:, c + 12:c + 16][:, :, None].broadcast_to([P, 4, w])
                    dve.tensor_tensor(PR[:, n, :, 0:w], PR[:, n, :, 0:w], r, ALU.mult).then_inc(probs, 1)
                else:
                    dve.wait_ge(scores_read, 10 * l + s + 1)
                    dve.wait_ge(stick_sums, 2 * l + s - 8)
                    chain(dve.tensor_scalar(STK[:, :, 0:w], SM[:, n, :, 0:w], 0.0, None, ALU.max))
                    dve.wait_ge(stick_logs, 2 * l + s - 8 + 1)
                    chain.wait()
                    for h in range(4):
                        chain(dve.tensor_tensor_scan(STK[:, h, 0:w][:, ::-1], PR[:, n, h, 0:w][:, ::-1],
                                                     STK[:, h, 0:w][:, ::-1], 0.0, ALU.add, ALU.add))
                    chain.wait()
                    dve.tensor_tensor(SM[:, n, :, 0:w], SM[:, n, :, 0:w], STK[:, :, 0:w],
                                      ALU.subtract).then_inc(stick_sums, 1)

            begin(2)
            for s in range(2, 10):
                if s + 1 < 10:
                    begin(s + 1)
                end(s)
            def low(k):
                dve.wait_ge(out_hi, l * KC + k + 1)
                dve.tensor_tensor(OS[:, 1, k, :], GATE[:, k % 4, :], OS[:, 0, k, :].bitcast(f32),
                                  ALU.subtract).then_inc(out_lo, 1)

            for k in range(KC):
                if k % 2 == 0:
                    dve.wait_ge(out_roots, 4 * l + k // 2 + 1)
                    refine(RSO[:, k:k + 2, :], VO[:, k:k + 2, :])
                if k >= 4:
                    dve.wait_ge(out_lo, l * KC + k - 3)
                g = PAR1["gout"] + k
                dve.scalar_tensor_tensor(GATE[:, k % 4, :], O[:, k, :], P1[:, l, g:g + 1], RSO[:, k, :],
                                         ALU.mult, ALU.mult).then_inc(out_scaled, 1)
                if k >= 2:
                    low(k - 2)
            low(KC - 2)
            low(KC - 1)
            b = b + QK_UNITS

            def project(i, j):
                beside(b, i, j)
                done(b, i, j)
                k = 4 * i + j
                dve.scalar_tensor_tensor(X[:, bass.ds(k, 1), :], PS[:, j:j + 1, 0:T],
                                         M1[:, l, bass.ds(16 + k, 1)], X[:, bass.ds(k, 1), :],
                                         ALU.mult, ALU.add).then_inc(bank_read[j], 1)
                next_low(b, i, j)

            looped(dve, b, WO_UNITS, 4, project)
            if l == 0:
                columns(0, 32, WO_UNITS)
            norm(l, 1)
            b2 = first = b + WO_UNITS

            def hidden(b2, i, j):
                beside(b2, i, j)
                if j % 2 == 0:
                    next_low(b2, i, j)
                else:
                    done(b2, i, j)
                    x = (b2 - first) // 2 + j // 2
                    m = 2 * i + (l * FC + x + 1)
                    dve.wait_ge(ff_done, m - 1 + BEGUN)
                    dve.wait_ge(ff_sigmoid, m)
                    dve.tensor_tensor(GATE[:, 1, :], GATE[:, 0, :], PS[:, j - 1, 0:T], ALU.mult).then_inc(bank_read[j - 1], 1)
                    dve.wait_ge(bank_read[j - 1], i + (earlier(b2 + j - 1) + 1))
                    dve.tensor_tensor(GATE[:, 2, :], GATE[:, 1, :], PS[:, j, 0:T], ALU.mult).then_inc(bank_read[j], 1)
                    next_low(b2, i, j)

            looped(dve, b2, FF_MODS, 4, lambda i, j: hidden(b2, i, j))
            looped(dve, b2 + FF_MODS, FF_UNITS - FF_MODS, 4, lambda i, j: hidden(b2 + FF_MODS, i, j))
            if l == 0:
                columns(0, 32 + WO_UNITS, MOD1 - 32 - WO_UNITS)
            b3 = b2 + FF_UNITS

            def down(i, j):
                beside(b3, i, j, 12)
                if j % 3 == 2:
                    done(b3, i, j, 3)
                    k, bank = 4 * i + j // 3, j // 3
                    dve.scalar_tensor_tensor(X[:, bass.ds(k, 1), :], PS[:, bank:bank + 1, 0:T],
                                             M1[:, l, bass.ds(40 + k, 1)], X[:, bass.ds(k, 1), :],
                                             ALU.mult, ALU.add).then_inc(bank_read[bank], 1)
                next_low(b3, i, j, 3)

            looped(dve, b3, DOWN_UNITS, 12, down)
            if l == 0:
                columns(1, 0, MOD1)
            else:
                dve.wait_ge(later_in, 16 * 3)
                columns2()

        for at, signal in enumerate((ff_done, o_gated, gated, acc_done)):
            dve.memset(COL[:, 56 + at:57 + at], 0.0).then_inc(signal, BEGUN)
        chain(dve.memset(EPSC[:, 0:1], EPS))
        dve.memset(EPSC[:, 1:2], 1.0).then_inc(c_exped, 1)
        dve.wait_ge(c_exped, 2)
        chain(dve.tensor_scalar(CT[:, 1, :, :], CT[:, 0, :, :], 1.0, None, ALU.add))
        chain.wait()
        chain(dve.reciprocal(CT[:, 0, :, :], CT[:, 1, :, :]))
        chain.wait()
        dve.tensor_tensor(CA[:, :, :], CC[:, :, :], CT[:, 0, :, :], ALU.mult).then_inc(c_done, 1)
        copy_vector(0)
        for u in range(4):
            modulate(u)
            split_low(u, 0, 1)
        looped(dve, 0, 12, 4, lambda i, j: modulate(4 + j, i))
        dve.wait_ge(consts_in, 16 * 3)
        columns(0, 0, 16)
        for l in range(DEPTH):
            first_layer(l)
        second_dve(dve, done, next_low, refine, chain)
    ctx.close()


def _units(w):
    k, n = w.shape
    return w.reshape(k // P, P, n // P, P).transpose(2, 1, 0, 3)


def _padded(w, n):
    out = np.zeros((w.shape[0], n), w.dtype)
    out[:, :w.shape[1]] = w
    return out


def _weights(a):
    total = DEPTH * (FIRST_UNITS + SECOND_UNITS)
    s = np.zeros((total, P, KC, P), np.float32)
    at = 0

    def put(w):
        nonlocal at
        u = _units(w)
        s[at:at + len(u)] = u
        at += len(u)

    for l in range(DEPTH):
        w = a["w_in"][l]
        cuts = np.cumsum([256, 64, 64, 256, 64, 4, 256, 256, 256, 512, 128])
        qa, ka, va, qi, ki, wi, qb, kb, vb, qc, kc, vc = np.split(w, cuts, axis=1)
        put(_padded(np.concatenate([va, vb, vc, wi], 1), 512))
        put(np.concatenate([qi, ki, ki, qa, ka, ka, qc, kc[:, :64], kc[:, :64], kc[:, 64:], kc[:, 64:], qb, kb], 1))
        put(a["w_o"][l])
        both = np.stack([a["w_gate"][l].reshape(D, FC, P), a["w_up"][l].reshape(D, FC, P)], 2)
        put(both.reshape(D, 2 * D_FF))
        down = _units(a["w_down"][l])
        for n in range(KC):
            for part in range(3):
                piece = down[n][:, part * KC:(part + 1) * KC]
                s[at, :, :piece.shape[1]] = piece
                at += 1
    for l in range(DEPTH):
        w = a["w_in_2"][l]
        cuts = np.cumsum([512, 512, 1024, 16, 1024, 1024, 1024, 1024, 1024, 1024, 1024, 1024])
        aq, ak, av, ag, ao, az, bq, bk, bv, bz, cu, cz, mg = np.split(w, cuts, axis=1)
        put(np.stack([aq.reshape(D, 4, P), ak.reshape(D, 4, P)], 2).reshape(D, D))
        put(av)
        g = np.zeros((D, 2 * P), np.float32)
        for i in range(4):
            g[:, 32 * i:32 * i + 4] = ag[:, 4 * i:4 * i + 4]
        put(g)
        put(ao)
        put(az)

        def pairs(i, out):
            m = mg[:, i * D:(i + 1) * D].reshape(D, KC, P)
            put(np.stack([m, out.reshape(D, KC, P)], 2).reshape(D, 2 * D))

        pairs(0, a["w_a_out_2"][l])
        put(bq)
        put(bk)
        put(bv)
        put(bz)
        pairs(1, a["w_b_out_2"][l])
        put(cu)
        put(cz)
        pairs(2, a["w_c_out_2"][l])
        put(a["w_out_2"][l])
    assert at == total
    return s


def _modulations(a):
    units = np.concatenate([_units(a["w_mod"][l]) for l in range(DEPTH)]
                           + [_units(a["w_ada_2"][l]) for l in range(DEPTH)])
    return units.transpose(0, 3, 2, 1)


def _column(v):
    return v.reshape(-1, P).T


def _parameters(a):
    p1 = np.zeros((P, DEPTH, PAR1_W), np.float32)
    p2 = np.zeros((P, DEPTH, PAR2_W), np.float32)

    def put(dst, places, l, name, v):
        dst[:, l, places[name]:places[name] + v.shape[1]] = v

    twice = lambda v: np.tile(v, 2)[:, None]
    for l in range(DEPTH):
        put(p1, PAR1, l, "ln1", _column(a["ln1"][l]))
        put(p1, PAR1, l, "ln2", _column(a["ln2"][l]))
        put(p1, PAR1, l, "bmod", _column(a["b_mod"][l]))
        qa, ka, qc, kc = (twice(a[n][l]) for n in ("qn_a", "kn_a", "qn_c", "kn_c"))
        put(p1, PAR1, l, "gain", np.concatenate([qa, qa, ka, qc, qc, qc, qc, kc, kc], 1))
        put(p1, PAR1, l, "gout", _column(a["g_out"][l].reshape(-1)))
        put(p1, PAR1, l, "sinks", np.tile(a["sinks"][l].reshape(2, 4)[:, PLACE].reshape(1, 8), (P, 1)))
        put(p2, PAR2, l, "norm", _column(a["norm_w_2"][l]))
        put(p2, PAR2, l, "bada", _column(a["b_ada_2"][l]))
        b = np.zeros((P, 1), np.float32)
        for i in range(4):
            b[32 * i:32 * i + 4, 0] = a["b_if_2"][l][4 * i:4 * i + 4]
        put(p2, PAR2, l, "bif", b)
        put(p2, PAR2, l, "anorm", _column(a["a_norm_w_2"][l]))
        put(p2, PAR2, l, "qn", twice(a["q_norm_w_2"][l]))
        put(p2, PAR2, l, "kn", twice(a["k_norm_w_2"][l]))
        put(p2, PAR2, l, "subln", a["subln_w_2"][l][:, None])
    lam = np.stack([a[n] for n in ("lambda_q1_2", "lambda_k1_2", "lambda_q2_2", "lambda_k2_2")], 1)
    return p1, p2, np.tile(lam[None], (P, 1, 1, 1))


def _laid_out(a):
    p1, p2, lam = _parameters(a)
    first, second = constants()
    cols = np.stack([_column(a["c"][0]), _column(a["c_2"][0]), _column(a["c_ctx_2"])], 1)
    chunked = lambda x: x.T.reshape(KC, P, T).transpose(1, 0, 2)
    return {"stream": _weights(a), "mods": _modulations(a), "consts": first, "consts2": second, "par1": p1, "par2": p2, "lam": lam,
            "ccols": cols, "xT": chunked(a["x"][0]), "ctxT": chunked(a["ctx_2"][0])}


def kernel(**inputs):
    import concourse.bacc as bacc
    from concourse.bass_utils import run_bass_kernel_spmd

    a = {k: np.asarray(v) for k, v in inputs.items()}
    nc = bacc.Bacc("TRN2", target_bir_lowering=False, num_devices=1, dynamic_dma_scratch_size=2048)
    arrays = {k: np.ascontiguousarray(v) for k, v in _laid_out(a).items()}
    args = [nc.dram_tensor(k, v.shape, mybir.dt.from_np(v.dtype), kind="ExternalInput").ap()
            for k, v in arrays.items()]
    out = nc.dram_tensor("outT", (P, KC, T), mybir.dt.float32, kind="ExternalOutput").ap()
    build(nc, *args, out)
    r = run_bass_kernel_spmd(nc, [arrays], core_ids=[0])
    return r.results[0]["outT"].transpose(1, 0, 2).reshape(D, T).T[None]
```
